# Optimizing a Trainium2 kernel written in Bass

```python
import jax, jax.numpy as jnp
from jax import lax
import numpy as np

D_MODEL = 1024
BATCH = 1
SEQ = 1024
DEPTH = 1

GRID_W = 64
D_MIX = D_MODEL
D_CONV = D_MIX // 2
D_ATTN = D_MIX - D_CONV
HEAD_DIM = 64
N_HEADS = D_ATTN // HEAD_DIM
CONV_WIDTH = 31
NA_ROWS = 8
NA_COLS = 16
D_FF = -(-8 * D_MODEL // (3 * 256)) * 256
D_IN = 2 * D_CONV + 3 * D_ATTN
EPS = 1e-6


def rms_norm(x, g):
    xf = x.astype(jnp.float32)
    y = xf * lax.rsqrt(jnp.mean(xf * xf, axis=-1, keepdims=True) + EPS)
    return (y * g.astype(jnp.float32)).astype(x.dtype)

def layer_norm(x, g, b):
    xf = x.astype(jnp.float32)
    mu = jnp.mean(xf, axis=-1, keepdims=True)
    xc = xf - mu
    y = xc * lax.rsqrt(jnp.mean(xc * xc, axis=-1, keepdims=True) + EPS)
    return (y * g.astype(jnp.float32) + b.astype(jnp.float32)).astype(x.dtype)

def conformer_conv(a, gate, dw_kernel, dw_bias, ln_g, ln_b):
    u = a * jax.nn.sigmoid(gate)
    pad = CONV_WIDTH // 2
    y = lax.conv_general_dilated(
        u, dw_kernel[:, None, :], window_strides=(1,), padding=[(pad, pad)],
        dimension_numbers=("NWC", "WIO", "NWC"), feature_group_count=u.shape[-1])
    y = y + dw_bias
    y = layer_norm(y, ln_g, ln_b)
    return jax.nn.silu(y)

def neighbourhood_attention(q, k, v, rpb):
    B, S, H, Dh = q.shape
    rows = S // GRID_W
    kh = min(NA_ROWS, rows)
    kw = NA_COLS
    qg = q.reshape(B, rows, GRID_W, H, Dh)
    kg = k.reshape(B, rows, GRID_W, H, Dh)
    vg = v.reshape(B, rows, GRID_W, H, Dh)
    cols = jnp.arange(GRID_W)
    col_start = jnp.clip(cols - kw // 2, 0, GRID_W - kw)
    col_idx = col_start[:, None] + jnp.arange(kw)[None, :]
    col_bias_idx = col_idx - cols[:, None] + (NA_COLS - 1)
    scale = Dh ** -0.5

    def row_block(r):
        row_start = jnp.clip(r - kh // 2, 0, rows - kh)
        q_r = lax.dynamic_index_in_dim(qg, r, axis=1, keepdims=False)
        k_rows = lax.dynamic_slice_in_dim(kg, row_start, kh, axis=1)
        v_rows = lax.dynamic_slice_in_dim(vg, row_start, kh, axis=1)
        k_win = k_rows[:, :, col_idx]
        v_win = v_rows[:, :, col_idx]
        s = jnp.einsum("bqhd,brqchd->bhqrc", q_r, k_win,
                       preferred_element_type=jnp.float32) * scale
        row_bias_idx = row_start + jnp.arange(kh) - r + (NA_ROWS - 1)
        bias = rpb[:, row_bias_idx][:, :, col_bias_idx]
        s = s + jnp.transpose(bias, (0, 2, 1, 3))[None].astype(jnp.float32)
        p = jax.nn.softmax(s, axis=(-2, -1))
        return jnp.einsum("bhqrc,brqchd->bqhd", p.astype(v_win.dtype), v_win)

    out = lax.map(row_block, jnp.arange(rows))
    return jnp.moveaxis(out, 0, 1).reshape(B, S, H * Dh)

def first_inputs(seed: int = 0) -> dict:
    key = jax.random.key(seed)
    ks = jax.random.split(key, 16)
    f32 = jnp.float32
    n = lambda k, shape, s: (jax.random.normal(k, shape, f32) * s).astype(f32)
    return {
        "x": n(ks[0], (BATCH, SEQ, D_MODEL), 1.0),
        "norm1_g": 1.0 + n(ks[1], (DEPTH, D_MODEL), 0.02),
        "w_in": n(ks[2], (DEPTH, D_MODEL, D_IN), D_MODEL ** -0.5),
        "q_norm_g": 1.0 + n(ks[3], (DEPTH, HEAD_DIM), 0.02),
        "k_norm_g": 1.0 + n(ks[4], (DEPTH, HEAD_DIM), 0.02),
        "rpb": n(ks[5], (DEPTH, N_HEADS, 2 * NA_ROWS - 1, 2 * NA_COLS - 1), 0.1),
        "dw_kernel": n(ks[6], (DEPTH, CONV_WIDTH, D_CONV), CONV_WIDTH ** -0.5),
        "dw_bias": n(ks[7], (DEPTH, D_CONV), 0.02),
        "conv_ln_g": 1.0 + n(ks[8], (DEPTH, D_CONV), 0.02),
        "conv_ln_b": n(ks[9], (DEPTH, D_CONV), 0.02),
        "w_out": n(ks[10], (DEPTH, D_MIX, D_MODEL), D_MIX ** -0.5),
        "norm2_g": 1.0 + n(ks[11], (DEPTH, D_MODEL), 0.02),
        "w_gate": n(ks[12], (DEPTH, D_MODEL, D_FF), D_MODEL ** -0.5),
        "w_up": n(ks[13], (DEPTH, D_MODEL, D_FF), D_MODEL ** -0.5),
        "w_down": n(ks[14], (DEPTH, D_FF, D_MODEL), D_FF ** -0.5),
    }

def first_block(x, norm1_g, w_in, q_norm_g, k_norm_g, rpb, dw_kernel, dw_bias,
              conv_ln_g, conv_ln_b, w_out, norm2_g, w_gate, w_up, w_down):
    B, S, _ = x.shape
    splits = [D_CONV, 2 * D_CONV, 2 * D_CONV + D_ATTN, 2 * D_CONV + 2 * D_ATTN]
    for l in range(DEPTH):
        h = rms_norm(x, norm1_g[l])
        z = h @ w_in[l]
        a, gate, q, k, v = jnp.split(z, splits, axis=-1)
        conv_out = conformer_conv(a, gate, dw_kernel[l], dw_bias[l],
                                  conv_ln_g[l], conv_ln_b[l])
        q = rms_norm(q.reshape(B, S, N_HEADS, HEAD_DIM), q_norm_g[l])
        k = rms_norm(k.reshape(B, S, N_HEADS, HEAD_DIM), k_norm_g[l])
        v = v.reshape(B, S, N_HEADS, HEAD_DIM)
        attn_out = neighbourhood_attention(q, k, v, rpb[l])
        mix = jnp.concatenate([conv_out, attn_out], axis=-1)
        x = x + mix @ w_out[l]
        h = rms_norm(x, norm2_g[l])
        x = x + (jax.nn.silu(h @ w_gate[l]) * (h @ w_up[l])) @ w_down[l]
    return x


CHUNK = 64
POOL_WIDTH = D_MODEL // 2
POOL_WINDOWS = (2, 4, 8, 16)
N_POOL_GROUPS = len(POOL_WINDOWS)
POOL_GROUP = POOL_WIDTH // N_POOL_GROUPS
SB_WIDTH = D_MODEL - POOL_WIDTH
SB_HEAD_DIM = 64
SB_HEADS = SB_WIDTH // SB_HEAD_DIM
Q_BLOCK = 128
D_FF_2 = 4 * D_MODEL
PLE_DIM = 256
IN_WIDTH = POOL_WIDTH + 3 * SB_WIDTH


def rms_norm_2(x, g):
    xf = x.astype(jnp.float32)
    y = xf * lax.rsqrt(jnp.mean(xf * xf, axis=-1, keepdims=True) + EPS)
    return (y * g.astype(jnp.float32)).astype(x.dtype)

def pool_mixer(u, w_pool, scale):
    b, s, _ = u.shape
    uf = u.astype(jnp.float32).reshape(b, s, N_POOL_GROUPS, POOL_GROUP)
    t = jnp.arange(s)
    outs = []
    for gi, w in enumerate(POOL_WINDOWS):
        ug = uf[:, :, gi]
        c = jnp.cumsum(ug, axis=1)
        c_prev = jnp.pad(c, ((0, 0), (w, 0), (0, 0)))[:, :s]
        cnt = jnp.minimum(t + 1, w).astype(jnp.float32)[None, :, None]
        outs.append((c - c_prev) / cnt - ug)
    d = jnp.stack(outs, axis=2).astype(u.dtype)
    y = jnp.einsum('bsgc,gcd->bsgd', d, w_pool).reshape(b, s, POOL_WIDTH)
    return y * scale

def stick_breaking_attention(q, k, v):
    b, s_len, h, dh = q.shape
    scale = dh ** -0.5
    outs = []
    for start in range(0, s_len, Q_BLOCK):
        end = start + Q_BLOCK
        qb = q[:, start:end]
        kb = k[:, :end]
        vb = v[:, :end]
        z = jnp.einsum('bqhd,bkhd->bhqk', qb, kb,
                       preferred_element_type=jnp.float32) * scale
        t_idx = start + jnp.arange(Q_BLOCK)
        s_idx = jnp.arange(end)
        mask = s_idx[None, :] < t_idx[:, None]
        log_fail = jnp.where(mask, jax.nn.log_sigmoid(-z), 0.0)
        after = lax.cumsum(log_fail, axis=3, reverse=True) - log_fail
        log_a = jax.nn.log_sigmoid(z) + after
        a = jnp.where(mask, jnp.exp(log_a), 0.0)
        outs.append(jnp.einsum('bhqk,bkhd->bqhd', a.astype(v.dtype), vb))
    return jnp.concatenate(outs, axis=1)

def second_inputs(seed: int = 0) -> dict:
    key = jax.random.key(seed)
    ks = jax.random.split(key, 20)
    f32 = jnp.float32

    def nrm(k, shape, fan_in):
        return jax.random.normal(k, shape, f32) * (fan_in ** -0.5)

    def gain(k, shape):
        return 1.0 + 0.05 * jax.random.normal(k, shape, f32)

    return {
        "x": jax.random.normal(ks[0], (BATCH, SEQ, D_MODEL), f32),
        "p": jax.random.normal(ks[1], (DEPTH, BATCH, SEQ, PLE_DIM), f32),
        "g_mix_pre": gain(ks[2], (DEPTH, D_MODEL)),
        "w_in": nrm(ks[3], (DEPTH, D_MODEL, IN_WIDTH), D_MODEL),
        "w_pool": nrm(ks[4], (DEPTH, N_POOL_GROUPS, POOL_GROUP, POOL_GROUP), POOL_GROUP),
        "pool_scale": gain(ks[5], (DEPTH, POOL_WIDTH)),
        "g_sb": gain(ks[6], (DEPTH, SB_WIDTH)),
        "w_out": nrm(ks[7], (DEPTH, D_MODEL, D_MODEL), D_MODEL),
        "g_mix_post": gain(ks[8], (DEPTH, D_MODEL)),
        "g_mlp_pre": gain(ks[9], (DEPTH, D_MODEL)),
        "w_up": nrm(ks[10], (DEPTH, D_MODEL, D_FF_2), D_MODEL),
        "w_down": nrm(ks[11], (DEPTH, D_FF_2, D_MODEL), D_FF_2),
        "g_mlp_post": gain(ks[12], (DEPTH, D_MODEL)),
        "w_ple_gate": nrm(ks[13], (DEPTH, D_MODEL, D_MODEL), D_MODEL),
        "w_ple_proj": nrm(ks[14], (DEPTH, PLE_DIM, D_MODEL), PLE_DIM),
        "g_ple": gain(ks[15], (DEPTH, D_MODEL)),
    }

def second_block(x, p, g_mix_pre, w_in, w_pool, pool_scale, g_sb, w_out, g_mix_post,
              g_mlp_pre, w_up, w_down, g_mlp_post, w_ple_gate, w_ple_proj, g_ple):
    b, s, _ = x.shape
    assert s % CHUNK == 0
    h = x
    for i in range(DEPTH):
        hn = rms_norm_2(h, g_mix_pre[i])
        proj = hn @ w_in[i]
        u = proj[..., :POOL_WIDTH]
        q, k, v = jnp.split(proj[..., POOL_WIDTH:], 3, axis=-1)
        q = q.reshape(b, s, SB_HEADS, SB_HEAD_DIM)
        k = k.reshape(b, s, SB_HEADS, SB_HEAD_DIM)
        v = v.reshape(b, s, SB_HEADS, SB_HEAD_DIM)

        y_pool = pool_mixer(u, w_pool[i], pool_scale[i])
        o_sb = stick_breaking_attention(q, k, v)
        y_sb = rms_norm_2(o_sb, jnp.ones((SB_HEAD_DIM,), jnp.float32)).reshape(b, s, SB_WIDTH) * g_sb[i]

        mix = jnp.concatenate([y_pool, y_sb], axis=-1) @ w_out[i]
        h = h + rms_norm_2(mix, g_mix_post[i])

        m = rms_norm_2(h, g_mlp_pre[i]) @ w_up[i]
        m = jnp.square(jax.nn.relu(m)) @ w_down[i]
        h = h + rms_norm_2(m, g_mlp_post[i])

        gate = jax.nn.sigmoid(h @ w_ple_gate[i])
        e = rms_norm_2(p[i] @ w_ple_proj[i], g_ple[i])
        h = h + gate * e
    return h


def setup_inputs(seed=0):
    out = dict(first_inputs(seed))
    for name, value in second_inputs(seed + 1).items():
        if name != "x":
            out[name + "_2"] = value
    return out


def reference(
    x, norm1_g, w_in, q_norm_g, k_norm_g, rpb, dw_kernel, dw_bias, conv_ln_g, conv_ln_b, w_out,
    norm2_g, w_gate, w_up, w_down, p_2, g_mix_pre_2, w_in_2, w_pool_2, pool_scale_2, g_sb_2,
    w_out_2, g_mix_post_2, g_mlp_pre_2, w_up_2, w_down_2, g_mlp_post_2, w_ple_gate_2,
    w_ple_proj_2, g_ple_2,
):
    x = first_block(
        x, norm1_g, w_in, q_norm_g, k_norm_g, rpb, dw_kernel, dw_bias, conv_ln_g, conv_ln_b,
        w_out, norm2_g, w_gate, w_up, w_down,
    )
    return second_block(
        x, p_2, g_mix_pre_2, w_in_2, w_pool_2, pool_scale_2, g_sb_2, w_out_2, g_mix_post_2,
        g_mlp_pre_2, w_up_2, w_down_2, g_mlp_post_2, w_ple_gate_2, w_ple_proj_2, g_ple_2,
    )


_drawn_inputs = setup_inputs


def setup_inputs(seed=0):
    import zlib

    import numpy as np

    out = dict(_drawn_inputs(seed))
    spreads = {}
    factors = {'norm1_g': 4.86,
     'q_norm_g': 8.0,
     'k_norm_g': 8.0,
     'rpb': 5.461,
     'dw_bias': 10.656,
     'conv_ln_g': 18.336,
     'conv_ln_b': 17.838,
     'norm2_g': 3.87,
     'pool_scale_2': 21.576,
     'g_ple_2': 19.654,
     'g_mix_pre_2': 8.0,
     'g_sb_2': 8.0,
     'g_mix_post_2': 8.0,
     'g_mlp_pre_2': 8.0,
     'g_mlp_post_2': 8.0}
    for name, (base, spread) in spreads.items():
        noise = np.random.default_rng([zlib.crc32(name.encode()), seed]).standard_normal(out[name].shape)
        drawn = base * np.exp(spread * noise) if base else spread * noise
        out[name] = __import__('jax').numpy.asarray(drawn.astype(out[name].dtype))
    for name, factor in factors.items():
        out[name] = (out[name] * factor).astype(out[name].dtype)
    return out
```

```python
import concourse.bass as bass
from concourse import mybir
from contextlib import ExitStack

T = 1024
D = 1024
P = 128
KD = D // P
H2 = T // 2
EPS = 1e-6
GRID_W, ROWS, NA_ROWS, NA_COLS = 64, 16, 8, 16
HEADS, DH = 8, 64
TAPS = 31
PADT = TAPS // 2
FF1, FF2 = 2816, 4096
G = 4
NG1, TAIL = FF1 // P // G, FF1 // P % G
NG2 = FF2 // P // G
MASKED = -1.0e30
WINDOWS = (2, 4, 8, 16)

U_GLU = 0
U_QKV = U_GLU + 8
U_OUT = U_QKV + 12
U_FF = U_OUT + 8
U_TAIL = U_FF + NG1 * 3 * G
U_POOL = U_TAIL + 2 * TAIL + 4
U_QKV2 = U_POOL + 4
U_OUT2 = U_QKV2 + 12
U_MLP = U_OUT2 + 8
U_PLEP = U_MLP + NG2 * 2 * G
U_PLEG = U_PLEP + 4
U_END = U_PLEG + 8


class Chain:

    def __init__(self, eng, sem):
        self.eng, self.sem, self.base, self.local, self.i, self.per = eng, sem, 0, 0, None, 0

    def __call__(self, ins):
        ins.then_inc(self.sem, 1)
        self.local += 1
        return self.local

    def wait(self, mark=None):
        mark = self.local if mark is None else mark
        value = self.base + mark
        self.eng.wait_ge(self.sem, value if self.i is None else self.i * self.per + value)

    def enter(self, i, per):
        self.base, self.local, self.i, self.per = self.base + self.local, 0, i, per

    def leave(self, turns):
        assert self.local == self.per, (self.local, self.per)
        self.base, self.local, self.i = self.base + turns * self.per, 0, None


def key_rows(rp):
    first = [min(max(r - NA_ROWS // 2, 0), ROWS - NA_ROWS) for r in (2 * rp, 2 * rp + 1)]
    return first[0], first[1] + NA_ROWS - first[0]


def sb_tiles():
    out = []
    for h in range(2):
        for half in range(2):
            for b in range(4 * half + 3, -1, -1):
                lo = max(0, b * P - half * H2)
                out.append((h, half, b, lo, H2 - lo))
    return out


GAINS = (("norm1", 8), ("norm2", 8), ("g_mix_pre", 8), ("g_mix_post", 8), ("g_mlp_pre", 8),
         ("g_mlp_post", 8), ("g_ple", 8), ("q_g", 1), ("k_g", 1), ("dw_bias", 4), ("ln_g", 4),
         ("ln_b", 4), ("pool_scale", 4), ("g_sb", 4))


def up32(n):
    return -(-n // 32) * 32


def gains_at():
    at, out = 0, {}
    for name, n in GAINS:
        out[name] = at
        at += n
    return out


def program(nc, x, w_glu, w_qkv, w_out, w_ff, w_ffd, w_tail, w_taild, gains, taps, rpb,
            p_t, w_in2, w_pool, w_out2, w_mlp, w_mlpd, w_plep, w_pleg, out):
    f32, f32r = mybir.dt.float32, mybir.dt.float32r
    ALU, ACT = mybir.AluOpType, mybir.ActivationFunctionType

    ctx = ExitStack()
    with ctx:
        base = 16512

        def at(name, shape, offset, dt=f32):
            return nc.alloc_sbuf_tensor_at(name, shape, dt, offset=base + offset)

        def sem(name):
            return ctx.enter_context(nc.semaphore(name))

        KB32 = 4 * KD * T
        X = at("residual", [P, KD, T], 0)
        INH = at("input_hi", [P, KD, T], KB32, f32r)
        INL = at("input_lo", [P, KD, T], 2 * KB32, f32r)
        QK0 = 3 * KB32
        R2 = 4 * KB32
        W0 = 5 * KB32
        RAW = at("weight_raw", [P, 2, 1024], W0)
        WH = at("weight_hi", [P, 2, 1024], W0 + 8192, f32r)
        WL = at("weight_lo", [P, 2, 1024], W0 + 16384, f32r)
        S0 = W0 + 24576
        RS = at("token_scale", [P, T], S0)
        SQ = at("squares", [P, T], S0 + 4096)
        TA = at("work_a", [P, T], S0 + 8192)
        TB = at("work_b", [P, T], S0 + 12288)
        TC = at("work_c", [P, T], S0 + 16384)
        C0 = S0 + 20480
        IDENT = at("identity", [P, P], C0)
        MEAN = at("mean_all", [P, P], C0 + 512)
        MEANH = at("mean_head", [P, P], C0 + 1024)
        NGAIN = gains.shape[1]
        GN = at("gains_sb", [P, NGAIN], C0 + 1536)
        TP = at("taps_sb", [P, 4, TAPS], C0 + 1536 + up32(4 * NGAIN))
        C1 = C0 + 1536 + up32(4 * NGAIN) + up32(16 * TAPS)
        EPSC = at("eps_col", [P, 2], C1)
        ZERO = at("zero_col", [P, 1], C1 + 64)
        GS = at("qk_gain", [P, 2], C1 + 32)
        UP = at("glu_padded", [P, 4, T + 2 * PADT], 0)
        UW = 4 * (T + 2 * PADT)
        U4 = up32(4 * UW)
        BT = [at(f"bias_table{i}", [P, 16, GRID_W], U4 + 4096 * i) for i in range(2)]
        BI = at("bias_inner", [P, 9, GRID_W], U4 + 8192)
        SB = [at(f"scores{i}", [P, 9 * GRID_W], U4 + 8192 + 2304 * (i + 1)) for i in range(2)]
        ST = at("softmax_stats", [P, 3, 16], U4 + 8192 + 3 * 2304)
        OC = [at(f"attn_out{c}", [P, T], up32(c * UW)) for c in range(4)]
        QH, QL, KH, KL = (at(n, [P, T], QK0 + 4096 * i, f32r)
                          for i, n in enumerate(("q_hi", "q_lo", "k_hi", "k_lo")))
        V = at("v_tokens", [P, 8, P], QK0 + 16384)
        PT = [at(f"probs_t{i}", [P, 5, P], QK0 + 20480 + 2560 * i) for i in range(2)]
        Y = at("conv_out", [P, 4, T], R2)
        NEG = at("masked_tile", [P, T], R2 + 16384)
        HH = at("hidden_hi", [P, G, T], R2, f32r)
        HL = at("hidden_lo", [P, G, T], R2 + 16384, f32r)
        UB = at("pool_u", [P, 4, T], R2)
        OB = [at(f"sb_out{c}", [P, T], QK0 + 16384 + 4096 * c) for c in range(4)]
        V2 = at("v2_tokens", [P, 8, P], R2 + 16384)
        NTRI = at("minus_tri", [P, P], R2 + 20480)
        NONE = at("minus_ones", [P, P], R2 + 20992)
        NMASK = at("diag_masked", [P, P], R2 + 21504)
        KEEP = at("diag_keep", [P, P], R2 + 22016)
        WP = at("w_pool_sb", [P, 4, P], R2 + 22528)
        EX = [at(f"sb_e{i}", [P, H2], R2 + 24576 + 2048 * i) for i in range(2)]
        SP_ = [at(f"sb_softplus{i}", [P, H2], R2 + 28672 + 2048 * i) for i in range(2)]
        RUN = at("sb_running", [P, H2], S0 + 4096)
        AW = at("sb_weights", [P, H2], S0 + 6144)
        MM = at("branch_out", [P, KD, T], QK0)
        PPH = at("ple_in_hi", [P, 2, T], R2, f32r)
        PPL = at("ple_in_lo", [P, 2, T], R2 + 8192, f32r)
        GL = at("gate_lo", [P, KD, T], QK0, f32r)
        EMB = at("embedding", [P, KD, T], KB32)
        PPF = at("ple_in", [P, 2, T], R2 + 16384)

        PS = ctx.enter_context(nc.psum_tensor("ps", [P, 8, H2], f32))

        def bank(b, n=2):
            return PS[:, b:b + n, :].rearrange("p b t -> p (b t)")

        names = """w_loaded0 w_loaded1 w_hi w_split unit_done bank_free consts_ready gains_in x_in0 x_in1 x_in2 x_in3
            split_hi split_lo sq_ready sq_added mean_done ln_exp scale_ready
            glu_sig qk_sq norm_sum qk_y0 qk_scaled qk_hi qk_lo v_tr v_ready
            neg_ready neg_out table_out bt_in0 bt_in1 bi_ready scores_done scores_max probs_done probs_scaled
            pt_done pt_sb pv_done head_done conv_out_done attn_out_done
            ln_in ln_mean ln_cent ln_sq ln_ssq ln_var ln_y0 ln_norm ln_silu mix_hi mix_lo
            aux_free ff_silu ff_h ff_hi ff_lo ff_acc
            act_chain dve_chain pool_chain
            sb_const sb_z sb_abs sb_lse sb_sp sb_cum sb_exp sb_pv sb_o sb_osq sb_osum
            sb_o0 sb_on pool_d pool_y pool_done q2_hi q2_lo v2_tr v2_ready pool_w_in
            post_sq post_y0 post_rs post_x
            ple_p_in ple_hi ple_lo ple_sig ple_out stored""".split()
        s = {n: sem(n) for n in names}
        block = ctx.enter_context(nc.Block())
        pool_, act_, dve_ = nc.gpsimd, nc.scalar, nc.vector
        g_of = gains_at()

        def g(name, k=0):
            return GN[:, g_of[name] + k:g_of[name] + k + 1]

        BD = nc.dram_tensor("bias_tables", [HEADS, P, 16 * GRID_W], f32).ap()
        N_TABLE_DMAS = 2 * (HEADS + NA_COLS - 1)

        @block.sync
        def _(sp):
            def load_unit(u, slot, src, width=1024):
                if not isinstance(u, int) or u >= 2:
                    sp.wait_ge(s["w_split"], u - 1)
                sp.dma_start(RAW[:, slot, 0:width], src).then_inc(s[f"w_loaded{slot}"], 16)

            def load_units(u0, w, n, width=1024):
                with sp.Fori(0, n // 2) as i:
                    for slot in range(2):
                        load_unit(i * 2 + u0 + slot, slot, w[bass.ds(i * 2 + slot, 1), :, :]
                                  .rearrange("u p n -> (u p) n"), width)

            sp.dma_start(GN[:], gains).then_inc(s["gains_in"], 16)
            sp.dma_start(TP[:], taps).then_inc(s["gains_in"], 16)
            load_unit(0, 0, w_glu[0])
            for k in range(4):
                sp.dma_start(X[:, 2 * k:2 * k + 2, :], x[:, 2 * k:2 * k + 2, :]).then_inc(s[f"x_in{k}"], 16)
            load_unit(1, 1, w_glu[1])
            for u in range(2, 8):
                load_unit(u, u % 2, w_glu[u])
            for c in range(4):
                for j in range(3):
                    u = U_QKV + 3 * c + j
                    load_unit(u, u % 2, w_qkv[3 * c + j])
                for h in (2 * c, 2 * c + 1):
                    if h >= 2:
                        sp.wait_ge(s["scores_max"], 8 * (h - 1))
                    sp.wait_ge(s["scale_ready"], 1)
                    sp.wait_ge(s["table_out"], 16 * N_TABLE_DMAS)
                    sp.dma_start(BT[h % 2][:], BD[h]).then_inc(s[f"bt_in{h % 2}"], 16)
            for j in range(2):
                load_unit(U_OUT + j, j % 2, w_out[j])
            sp.wait_ge(s["mix_lo"], 8)
            for k in range(4):
                sp.dma_start(X[:, 2 * k:2 * k + 2, :], x[:, 2 * k:2 * k + 2, :]).then_inc(s[f"x_in{k}"], 16)
            for j in range(2, 8):
                load_unit(U_OUT + j, j % 2, w_out[j])
            with sp.Fori(0, NG1) as i:
                for j in range(2 * G):
                    load_unit(i * (3 * G) + (U_FF + j), j % 2,
                              w_ff[bass.ds(i * (2 * G) + j, 1), :, :].rearrange("u p n -> (u p) n"))
                for j in range(G):
                    load_unit(i * (3 * G) + (U_FF + 2 * G + j), j % 2,
                              w_ffd[bass.ds(i * G + j, 1), :, :].rearrange("u p n -> (u p) n"))
            for j in range(2 * TAIL):
                load_unit(U_TAIL + j, j % 2, w_tail[j])
            for j in range(4):
                load_unit(U_TAIL + 2 * TAIL + j, j % 2, w_taild[j], TAIL * 256)
            for j in range(16):
                load_unit(U_POOL + j, j % 2, w_in2[j])
                if j == 1:
                    sp.wait_ge(s["unit_done"], U_POOL)
                    sp.dma_start(WP[:], w_pool).then_inc(s["pool_w_in"], 16)
            load_units(U_OUT2, w_out2, 8)
            with sp.Fori(0, NG2) as i:
                for j in range(G):
                    load_unit(i * (2 * G) + (U_MLP + j), j % 2,
                              w_mlp[bass.ds(i * G + j, 1), :, :].rearrange("u p n -> (u p) n"))
                for j in range(G):
                    load_unit(i * (2 * G) + (U_MLP + G + j), j % 2,
                              w_mlpd[bass.ds(i * G + j, 1), :, :].rearrange("u p n -> (u p) n"))
            for j in range(4):
                load_unit(U_PLEP + j, j % 2, w_plep[j], 512)
                if j == 1:
                    sp.wait_ge(s["unit_done"], U_PLEP)
                    sp.dma_start(PPF[:], p_t).then_inc(s["ple_p_in"], 16)
            for j in range(8):
                load_unit(U_PLEG + j, j % 2, w_pleg[j])
            for k in range(KD):
                sp.wait_ge(s["ple_out"], k + 1)
                sp.dma_start(out[:, k, :], X[:, k, :]).then_inc(s["stored"], 16)
            sp.wait_ge(s["stored"], 16 * KD)

        @block.gpsimd
        def _(pool):
            pool_.memset(NEG[:], MASKED).then_inc(s["neg_ready"], 1)
            chain = Chain(pool, s["pool_chain"])
            chain(pool_.memset(EPSC[:, 0:1], EPS))
            chain(pool_.memset(ZERO[:], 0.0))
            chain(pool_.memset(IDENT[:], 0.0))
            chain(pool_.memset(MEAN[:], 1.0 / D))
            chain(pool_.memset(MEANH[:], 1.0 / DH))
            chain.wait()
            chain(pool_.affine_select(out=IDENT[:], in_=IDENT[:], compare_op=ALU.not_equal, fill=1.0,
                                      base=0, pattern=[[-1, P]], channel_multiplier=1))
            chain.wait()
            chain(pool_.memset(MEANH[0:DH, DH:P], 0.0))
            chain.wait()
            chain(pool_.memset(MEANH[DH:P, 0:DH], 0.0))
            chain.wait()
            pool_.memset(EPSC[:, 1:2], EPS).then_inc(s["consts_ready"], 1)

            def split(u, slot, turn, width=1024):
                pool.wait_ge(s[f"w_loaded{slot}"], turn)
                if not isinstance(u, int) or u >= 2:
                    pool.wait_ge(s["unit_done"], u - 1)
                raw = RAW[:, slot, 0:width]
                pool_.tensor_tensor(WH[:, slot, 0:width], raw, ZERO[:].to_broadcast([P, width]), ALU.add).then_inc(s["w_hi"], 1)
                pool.wait_ge(s["w_hi"], u + 1)
                pool_.tensor_tensor(WL[:, slot, 0:width], raw, WH[:, slot, 0:width].bitcast(f32),
                                    ALU.subtract).then_inc(s["w_split"], 1)

            def splits(u0, n, width=1024):
                with pool.Fori(0, n // 2) as i:
                    for slot in range(2):
                        split(i * 2 + (u0 + slot), slot, i * 16 + 8 * u0 + 16, width)

            for u in range(2):
                split(u, u, 16)
            splits(2, U_TAIL + 2 * TAIL - 2)
            splits(U_TAIL + 2 * TAIL, 4, TAIL * 256)
            pool.wait_ge(s["unit_done"], U_POOL)
            chain(pool_.memset(NTRI[:], -1.0))
            chain(pool_.memset(NMASK[:], 0.0))
            chain(pool_.memset(KEEP[:], 1.0))
            chain(pool_.memset(NONE[:], -1.0))
            chain.wait()
            chain(pool_.affine_select(out=NTRI[:], in_=NTRI[:], compare_op=ALU.is_ge, fill=0.0,
                                      base=0, pattern=[[-1, P]], channel_multiplier=1))
            chain(pool_.affine_select(out=NMASK[:], in_=NMASK[:], compare_op=ALU.is_ge, fill=MASKED,
                                      base=-1, pattern=[[1, P]], channel_multiplier=-1))
            chain(pool_.affine_select(out=KEEP[:], in_=KEEP[:], compare_op=ALU.is_ge, fill=0.0,
                                      base=-1, pattern=[[1, P]], channel_multiplier=-1))
            chain.wait()
            pool_.memset(EPSC[:, 1:2], EPS).then_inc(s["sb_const"], 1)
            splits(U_POOL, U_PLEP - U_POOL)
            splits(U_PLEP, 4, 512)
            splits(U_PLEG, 8)

        @block.tensor
        def _(pe):
            mm = nc.tensor.matmul

            def unit(u, slot, b, kc=8, nc_=1, inh=INH, inl=INL, k_ready=None):
                pe.wait_ge(s["w_split"], u + 1)
                n = P * nc_
                for k in range(kc):
                    if k_ready:
                        k_ready(k)
                    for step, (w, a) in enumerate(((WH, inh), (WH, inl), (WL, inh))):
                        for c in range(nc_):
                            for h in range(2):
                                last = mm(PS[:, b + 2 * c + h, :],
                                          w[:, slot, k * n + P * c:k * n + P * (c + 1)],
                                          a[:, k, h * H2:(h + 1) * H2],
                                          start=(k == 0 and step == 0),
                                          stop=(k == kc - 1 and step == 2))
                last.then_inc(s["unit_done"], 1)

            def mean(mat, src, b, signal):
                for h in range(2):
                    last = mm(PS[:, b + h, :], mat[:], src[:, h * H2:(h + 1) * H2], start=True, stop=True)
                last.then_inc(s[signal], 1)

            def inputs(hi0, lo0):
                def ready(k):
                    pe.wait_ge(s["split_hi"], hi0 + k + 1)
                    pe.wait_ge(s["split_lo"], lo0 + k + 1)
                return ready

            pe.wait_ge(s["consts_ready"], 1)
            for u in range(8):
                if u == 1:
                    pe.wait_ge(s["sq_added"], KD)
                    mean(MEAN, SQ, 6, "mean_done")
                if u == 3:
                    pe.wait_ge(s["scale_ready"], 1)
                if u >= 4:
                    pe.wait_ge(s["bank_free"], u - 3)
                unit(u, u % 2, 2 * (u % 4), k_ready=inputs(0, 0) if u == 0 else None)

            for c in range(4):
                u = U_QKV + 3 * c
                pe.wait_ge(s["bank_free"], u)
                if c:
                    pe.wait_ge(s["scores_max"], 16 * c)
                unit(u, u % 2, 2 * (u % 2))
                unit(u + 1, (u + 1) % 2, 2 * ((u + 1) % 2))
                pe.wait_ge(s["qk_sq"], 2 * c + 1)
                if c:
                    pe.wait_ge(s["pt_sb"], 16 * c)
                else:
                    pe.wait_ge(s["bank_free"], 8)
                mean(MEANH, SQ, 4, "norm_sum")
                pe.wait_ge(s["bank_free"], u + 1)
                unit(u + 2, u % 2, 2 * (u % 2))
                pe.wait_ge(s["qk_sq"], 2 * c + 2)
                pe.wait_ge(s["qk_scaled"], 2 * c + 1)
                mean(MEANH, SQ, 4, "norm_sum")
                pe.wait_ge(s["bank_free"], u + 3)
                pe.wait_ge(s["qk_scaled"], 2 * c + 2)
                for b in range(8):
                    last = nc.tensor.transpose(PS[:, 4 + b // 4, (b % 4) * P:(b % 4 + 1) * P],
                                               TC[:, b * P:(b + 1) * P], IDENT[:])
                last.then_inc(s["v_tr"], 1)
                pe.wait_ge(s["bank_free"], u + 3)

                def scores(n):
                    h, rp = n // 8, n % 8
                    ks, nk = key_rows(rp)
                    lo = DH * h
                    if n == 0:
                        pe.wait_ge(s["qk_hi"], 2 * c + 2)
                        pe.wait_ge(s["qk_lo"], 2 * c + 2)
                    else:
                        pe.wait_ge(s["scores_max"], 16 * c + n)
                    for q, k_, step in ((QH, KH, 0), (QH, KL, 1), (QL, KH, 2)):
                        for b, w in ((0, 512), (1, nk * GRID_W - 512)):
                            if w:
                                last = mm(PS[:, 2 + b, 0:w], q[lo:lo + DH, rp * P:(rp + 1) * P],
                                          k_[lo:lo + DH, ks * GRID_W + b * 512:ks * GRID_W + b * 512 + w],
                                          start=(step == 0), stop=(step == 2))
                    last.then_inc(s["scores_done"], 1)

                def turn(n):
                    _, nk = key_rows(n % 8)
                    pe.wait_ge(s["probs_scaled"], 16 * c + n + 1)
                    if n:
                        pe.wait_ge(s["pt_sb"], 16 * c + n)
                    else:
                        pe.wait_ge(s["v_ready"], c + 1)
                    for b in range(5 if nk == 9 else 4):
                        w = P if b < 4 else GRID_W
                        last = nc.tensor.transpose(PS[0:w, 4 + b // 4, (b % 4) * P:(b % 4 + 1) * P],
                                                   SB[n % 2][:, b * P:b * P + w], IDENT[:])
                    last.then_inc(s["pt_done"], 1)

                def values(n):
                    h, rp = n // 8, n % 8
                    ks, nk = key_rows(rp)
                    pe.wait_ge(s["pt_sb"], 16 * c + n + 1)
                    if n == 0 and c:
                        pe.wait_ge(s["attn_out_done"], c)
                    nb = 5 if nk == 9 else 4
                    for b in range(nb):
                        w = P if b < 4 else GRID_W
                        last = mm(PS[DH * h:DH * (h + 1), 6 + rp // 4, (rp % 4) * P:(rp % 4 + 1) * P],
                                  V[0:w, ks // 2 + b, DH * h:DH * (h + 1)], PT[n % 2][0:w, b, :],
                                  start=(b == 0), stop=(b == nb - 1), skip_group_check=True)
                    last.then_inc(s["pv_done"], 1)

                scores(0)
                for n in range(16):
                    if n < 15:
                        scores(n + 1)
                    turn(n)
                    if n:
                        values(n - 1)
                values(15)

            pe.wait_ge(s["ln_in"], 1)
            mean(MEAN, TA, 0, "ln_mean")
            pe.wait_ge(s["ln_ssq"], 4)
            mean(MEAN, TA, 2, "ln_var")
            pe.wait_ge(s["aux_free"], 1)
            for j in range(8):
                u = U_OUT + j
                if j >= 4:
                    pe.wait_ge(s["bank_free"], u - 3)
                elif j == 3:
                    pe.wait_ge(s["attn_out_done"], 4)

                def mix_ready(k):
                    pe.wait_ge(s["mix_hi"], k + 1)
                    pe.wait_ge(s["mix_lo"], k + 1)
                unit(u, j % 2, 2 * (j % 4), k_ready=mix_ready if j == 0 else None)

            def scale_sum(squares):
                pe.wait_ge(s["sq_added"], squares)
                mean(MEAN, SQ, 6, "mean_done")

            def scale_left(n):
                pe.wait_ge(s["scale_ready"], n)

            pe.wait_ge(s["bank_free"], U_FF)
            scale_sum(2 * KD)

            def ff_group(i, u0, n_h, up, split0, first=False, ready=None, scale=0):
                for j in range(up * n_h):
                    u = i * (up * G + G) + (u0 + j)
                    if j < 4:
                        if not first:
                            pe.wait_ge(s["bank_free"], u - j + (-1 if j < 2 else 0))
                    else:
                        pe.wait_ge(s["bank_free"], u - 3)
                    if first and j == 3:
                        scale_left(scale)
                    unit(u, j % 2, 2 * (j % 4), k_ready=ready if (first and j == 0) else None)
                for m in range(4):
                    u = i * (up * G + G) + (u0 + up * n_h + m)
                    if up * n_h >= 4 and m < 2:
                        pe.wait_ge(s["bank_free"], u - m - (2 if m == 0 else 0))
                    else:
                        pe.wait_ge(s["bank_free"], u - 1)

                    def hidden(k):
                        pe.wait_ge(s["ff_hi"], i * n_h + (split0 + k + 1))
                        pe.wait_ge(s["ff_lo"], i * n_h + (split0 + k + 1))
                    unit(u, m % 2, 4 * (m % 2), kc=n_h, nc_=2, inh=HH, inl=HL,
                         k_ready=hidden if m == 0 else None)

            ff_group(0, U_FF, G, 2, 0, first=True, ready=inputs(KD, KD), scale=2)
            with pe.Fori(1, NG1) as i:
                ff_group(i, U_FF, G, 2, 0)
            ff_group(0, U_TAIL, TAIL, 2, NG1 * G)

            pe.wait_ge(s["bank_free"], U_POOL)
            scale_sum(3 * KD)
            for j in range(4):
                if j == 3:
                    scale_left(3)
                unit(U_POOL + j, j % 2, 2 * (j % 4), k_ready=inputs(2 * KD, 2 * KD) if j == 0 else None)
            pe.wait_ge(s["pool_w_in"], 16)
            for j in range(4):
                pe.wait_ge(s["pool_d"], j + 1)
                pe.wait_ge(s["bank_free"], U_POOL + 4)
                if j >= 1:
                    pe.wait_ge(s["pool_done"], j)
                for h in range(2):
                    last = mm(PS[:, 6 + h, :], WP[:, j, :], UB[:, j, h * H2:(h + 1) * H2], start=True, stop=True)
                last.then_inc(s["pool_y"], 1)
            pe.wait_ge(s["pool_done"], 4)

            pe.wait_ge(s["sb_const"], 1)
            tile = 0
            for c in range(4):
                u = U_QKV2 + 3 * c
                pe.wait_ge(s["bank_free"], u - 1)
                if c:
                    pe.wait_ge(s["sb_exp"], tile)
                for j in range(3):
                    pe.wait_ge(s["bank_free"], u + j - 1)
                    unit(u + j, (u + j) % 2, 2 * ((u + j) % 2))
                pe.wait_ge(s["bank_free"], u + 3)
                if c:
                    pe.wait_ge(s["sb_on"], c)
                for b in range(8):
                    last = nc.tensor.transpose(PS[:, 4 + b // 4, (b % 4) * P:(b % 4 + 1) * P],
                                               TC[:, b * P:(b + 1) * P], IDENT[:])
                last.then_inc(s["v2_tr"], 1)
                pe.wait_ge(s["q2_hi"], 2 * c + 2)
                pe.wait_ge(s["q2_lo"], 2 * c + 2)
                pe.wait_ge(s["bank_free"], u + 3)
                tiles = sb_tiles()

                def z_tile(n):
                    h, half, b, lo, w = tiles[n]
                    r = DH * h
                    if n >= 4:
                        pe.wait_ge(s["sb_exp"], c * len(tiles) + n - 3)
                    for q, k_, step in ((QH, KH, 0), (QL, KH, 1), (QH, KL, 2)):
                        last = mm(PS[:, n % 4, lo:], k_[r:r + DH, b * P:(b + 1) * P],
                                  q[r:r + DH, half * H2 + lo:(half + 1) * H2],
                                  start=(step == 0), stop=(step == 2), skip_group_check=True)
                    last.then_inc(s["sb_z"], 1)

                def cum_tile(n):
                    h, half, b, lo, w = tiles[n]
                    diag = b * P >= half * H2
                    pe.wait_ge(s["sb_sp"], c * len(tiles) + n + 1)
                    if diag:
                        mm(PS[:, n % 4, lo:lo + P], IDENT[:], NMASK[:], start=False, stop=False,
                           skip_group_check=True)
                    if b < 4 * half + 3:
                        mm(PS[:, n % 4, lo:], NONE[:], RUN[:, lo:], start=False, stop=False,
                           skip_group_check=True)
                    mm(PS[:, n % 4, lo:], NTRI[:], SP_[n % 2][:, lo:], start=False, stop=True,
                       skip_group_check=True).then_inc(s["sb_cum"], 1)

                def pv_tile(n):
                    h, half, b, lo, w = tiles[n]
                    pe.wait_ge(s["sb_exp"], c * len(tiles) + n + 1)
                    if n == 0:
                        pe.wait_ge(s["v2_ready"], c + 1)
                        if c:
                            pe.wait_ge(s["sb_on"], c)
                    mm(PS[DH * h:DH * (h + 1), 6 + half, lo:], V2[:, b, DH * h:DH * (h + 1)],
                       AW[:, lo:], start=(b == 4 * half + 3), stop=(b == 0),
                       skip_group_check=True).then_inc(s["sb_pv"], 1)

                z_tile(0)
                z_tile(1)
                for n in range(len(tiles)):
                    if n + 2 < len(tiles):
                        z_tile(n + 2)
                    cum_tile(n)
                    if n:
                        pv_tile(n - 1)
                pv_tile(len(tiles) - 1)
                tile += len(tiles)
                pe.wait_ge(s["sb_osq"], c + 1)
                mean(MEANH, TA, 4, "sb_osum")

            for j in range(8):
                u = U_OUT2 + j
                if j >= 4:
                    pe.wait_ge(s["bank_free"], u - 3)
                elif j == 0:
                    pe.wait_ge(s["sb_exp"], tile)
                elif j == 2:
                    pe.wait_ge(s["sb_on"], 4)

                def mix_ready(k):
                    pe.wait_ge(s["mix_hi"], 8 + k + 1)
                    pe.wait_ge(s["mix_lo"], 8 + k + 1)
                unit(u, j % 2, 2 * (j % 4), k_ready=mix_ready if j == 0 else None)
            pe.wait_ge(s["bank_free"], U_MLP)
            scale_sum(4 * KD)
            scale_left(4)
            scale_sum(5 * KD)
            ff_group(0, U_MLP, G, 1, NG1 * G + TAIL, first=True, ready=inputs(3 * KD, 3 * KD), scale=5)
            with pe.Fori(1, NG2) as i:
                ff_group(i, U_MLP, G, 1, NG1 * G + TAIL)
            for m in range(4):
                u = U_PLEP + m
                pe.wait_ge(s["bank_free"], u - 1)

                def p_ready(k):
                    pe.wait_ge(s["ple_hi"], k + 1)
                    pe.wait_ge(s["ple_lo"], k + 1)
                unit(u, m % 2, 4 * (m % 2), kc=2, nc_=2, inh=PPH, inl=PPL,
                     k_ready=p_ready if m == 0 else None)
            pe.wait_ge(s["bank_free"], U_PLEG)
            scale_sum(6 * KD)
            scale_left(6)
            for j in range(8):
                u = U_PLEG + j
                if j >= 4:
                    pe.wait_ge(s["bank_free"], u - 3)
                if j == 3:
                    scale_sum(7 * KD)
                    scale_left(7)
                unit(u, j % 2, 2 * (j % 4), inh=INL, inl=GL, k_ready=inputs(4 * KD, 4 * KD) if j == 0 else None)

        @block.scalar
        def _(act):
            chain = Chain(act, s["act_chain"])
            copy = lambda out, in_, scale=1.0: act_.activation(out, in_, ACT.Copy, scale=scale)
            lnexp = "natural_log_exp_and_others"

            sq_count = [0]

            def square(src, dst):
                n = sq_count[0]
                if n >= 2:
                    act.wait_ge(s["sq_added"], n - 1)
                act_.activation(dst, src, ACT.Square).then_inc(s["sq_ready"], 1)
                sq_count[0] += 1

            def first_guess(ps, dst, wait, value, signal, scale=1.0):
                act.wait_ge(s[wait], value)
                act_.preload_act_table_set(lnexp)
                chain(act_.activation(dst, ps, ACT.Ln, bias=EPSC[:, 0:1], scale=scale))
                chain.wait()
                act_.activation(dst, dst, ACT.Exp, scale=-0.5).then_inc(s[signal], 1)

            def hi(k, src, gain):
                act_.activation(INH[:, k, :], src, ACT.Identity, scale=gain).then_inc(s["split_hi"], 1)

            act.wait_ge(s["gains_in"], 32)
            act.wait_ge(s["consts_ready"], 1)
            for k in range(KD):
                act.wait_ge(s[f"x_in{k // 2}"], 16)
                hi(k, X[:, k, :], g("norm1", k))
                square(X[:, k, :], (TA, TB)[k % 2][:])
            first_guess(bank(6), RS[:], "mean_done", 1, "ln_exp")
            act.wait_ge(s["neg_ready"], 1)
            for h in range(HEADS):
                act.dma_start(BD[h], NEG[:]).then_inc(s["neg_out"], 16)

            def bias_windows():
                act.wait_ge(s["neg_out"], 16 * HEADS)
                rows, cols = 2 * NA_ROWS - 1, 2 * NA_COLS - 1
                half = NA_COLS // 2
                inner = GRID_W - NA_COLS + 1
                with nc.allow_non_contiguous_dma(reason="64-byte windows of the bias"):
                    for r in range(2):
                        for h in range(HEADS):
                            dst = bass.AP(tensor=BD.tensor, offset=((h * P + r * GRID_W + half) * 16 + r) * GRID_W,
                                          ap=[[16 * GRID_W + 1, inner], [GRID_W, rows], [1, NA_COLS]])
                            src = bass.AP(tensor=rpb.tensor, offset=h * rows * cols + half - 1,
                                          ap=[[0, inner], [cols, rows], [1, NA_COLS]])
                            act.dma_start(dst, src).then_inc(s["table_out"], 16)
                        for q in [*range(half), *range(half + inner, GRID_W)]:
                            start = 0 if q < half else GRID_W - NA_COLS
                            dst = bass.AP(tensor=BD.tensor, offset=((r * GRID_W + q) * 16 + r) * GRID_W + start,
                                          ap=[[P * 16 * GRID_W, HEADS], [GRID_W, rows], [1, NA_COLS]])
                            src = bass.AP(tensor=rpb.tensor, offset=start - q + NA_COLS - 1,
                                          ap=[[rows * cols, HEADS], [cols, rows], [1, NA_COLS]])
                            act.dma_start(dst, src).then_inc(s["table_out"], 16)

            for c in range(4):
                act.wait_ge(s["bank_free"], 2 * c + 1)
                act_.activation(TB[:], TA[:], ACT.Sigmoid).then_inc(s["glu_sig"], 1)
                if c == 1:
                    bias_windows()

            for c in range(4):
                for j, t in ((0, TA), (1, TB)):
                    act.wait_ge(s["bank_free"], U_QKV + 3 * c + j + 1)
                    if c or j:
                        act.wait_ge(s["qk_scaled"], 2 * c + j)
                    act_.activation(SQ[:], t[:], ACT.Square).then_inc(s["qk_sq"], 1)
                    first_guess(bank(4), SQ[:], "norm_sum", 2 * c + j + 1, "qk_y0")
                    act.wait_ge(s["qk_scaled"], 2 * c + j + 1)
                    if j == 0 and c:
                        act.wait_ge(s["scores_done"], 16 * c)
                    copy((QH, KH)[j][:], t[:]).then_inc(s["qk_hi"], 1)
                act.wait_ge(s["v_tr"], c + 1)
                if c:
                    act.wait_ge(s["pv_done"], 16 * c)
                copy(V[:, :, :].rearrange("p b d -> p (b d)"), bank(4)).then_inc(s["v_ready"], 1)
                for n in range(16):
                    _, nk = key_rows(n % 8)
                    w = nk * GRID_W

                    def exps(m):
                        wm = key_rows(m % 8)[1] * GRID_W
                        act.wait_ge(s["scores_max"], 16 * c + m + 1)
                        act_.activation(SB[m % 2][:, 0:wm], SB[m % 2][:, 0:wm], ACT.Exp, scale=-1.0,
                                        bias=ST[:, 0, m:m + 1], accum_out=ST[:, 1, m:m + 1])\
                            .then_inc(s["probs_done"], 1)
                    if n == 0:
                        exps(0)
                    if n < 15:
                        exps(n + 1)
                    act.wait_ge(s["pt_done"], 16 * c + n + 1)
                    if n >= 2:
                        act.wait_ge(s["pv_done"], 16 * c + n - 1)
                    if nk == 9:
                        copy(PT[n % 2][0:GRID_W, 4, :], PS[0:GRID_W, 5, 0:P])
                    copy(PT[n % 2][:, 0:4, :].rearrange("p b q -> p (b q)"), PS[:, 4, :])\
                        .then_inc(s["pt_sb"], 1)
                act.wait_ge(s["pv_done"], 16 * (c + 1))
                act.wait_ge(s["conv_out_done"], c + 1)
                copy(OC[c][:], bank(6)).then_inc(s["attn_out_done"], 1)

            for c in range(4):
                act.wait_ge(s["ln_cent"], c + 1)
                if c >= 2:
                    act.wait_ge(s["ln_ssq"], c - 1)
                act_.activation((TB, TC)[c % 2][:], Y[:, c, :], ACT.Square).then_inc(s["ln_sq"], 1)
            first_guess(bank(2), RS[:], "ln_var", 1, "ln_y0", scale=2.0)

            def mix_hi(k, src):
                copy(INH[:, k, :], src).then_inc(s["mix_hi"], 1)
            for c in range(4):
                act.wait_ge(s["ln_norm"], c + 1)
                chain(act_.activation(Y[:, c, :], Y[:, c, :], ACT.Silu, bias=g("ln_b", c), scale=g("ln_g", c)))
                chain.wait()
                if c == 0:
                    act.wait_ge(s["unit_done"], U_OUT)
                mix_hi(c, Y[:, c, :])
            for c in range(4):
                act.wait_ge(s["attn_out_done"], 4)
                mix_hi(4 + c, OC[c][:])

            def squares_of(u0, signal="bank_free"):
                for k in range(KD):
                    act.wait_ge(s[signal], u0 + k + 1)
                    square(X[:, k, :], (TA, TB)[k % 2][:])

            def next_input(name, u_done, wait=None):
                act.wait_ge(s["unit_done"], u_done)
                for k in range(KD):
                    if wait:
                        wait(k)
                    hi(k, X[:, k, :], g(name, k))

            squares_of(U_OUT)
            next_input("norm2", U_FF)
            first_guess(bank(6), RS[:], "mean_done", 2, "ln_exp")

            def ff_hi(i, u0, n_h, up, h0):
                for n in range(n_h):
                    act.wait_ge(s["bank_free"], i * (up * G + G) + (u0 + up * n + 1))
                    if up == 2:
                        act_.activation(TB[:], TA[:], ACT.Silu).then_inc(s["ff_silu"], 1)
                    else:
                        act_.activation(TB[:], TA[:], ACT.Square).then_inc(s["ff_silu"], 1)
                    if up == 2:
                        act.wait_ge(s["ff_h"], i * n_h + (h0 + n + 1))
                        src = TC
                    else:
                        act.wait_ge(s["ff_silu"], i * n_h + (h0 + n + 1))
                        src = TB
                    act.wait_ge(s["unit_done"], i * (up * G + G) + u0)
                    copy(HH[:, n, :], src[:]).then_inc(s["ff_hi"], 1)

            with act.Fori(0, NG1) as i:
                ff_hi(i, U_FF, G, 2, 0)
            ff_hi(0, U_TAIL, TAIL, 2, NG1 * G)

            def two_chunks(u0, name):
                for m in range(4):
                    act.wait_ge(s["bank_free"], u0 + m + 1)
                    for k in (2 * m, 2 * m + 1):
                        square(X[:, k, :], (TA, TB)[k % 2][:])
                        hi(k, X[:, k, :], g(name, k))
            two_chunks(U_TAIL + 2 * TAIL, "g_mix_pre")
            first_guess(bank(6), RS[:], "mean_done", 3, "ln_exp")

            act_.preload_act_table_set(lnexp)
            tiles = sb_tiles()
            for c in range(4):
                for j in range(2):
                    act.wait_ge(s["bank_free"], U_QKV2 + 3 * c + j + 1)
                    if c:
                        act.wait_ge(s["sb_z"], c * len(tiles))
                    copy((QH, KH)[j][:], (TA, TB)[j][:]).then_inc(s["q2_hi"], 1)
                act.wait_ge(s["v2_tr"], c + 1)
                if c:
                    act.wait_ge(s["sb_pv"], c * len(tiles))
                copy(V2[:, :, :].rearrange("p b d -> p (b d)"), bank(4)).then_inc(s["v2_ready"], 1)

                def lse(n):
                    h, half, b, lo, w = tiles[n]
                    act.wait_ge(s["sb_z"], c * len(tiles) + n + 1)
                    if n >= 2:
                        act.wait_ge(s["sb_sp"], c * len(tiles) + n - 1)
                    e = EX[n % 2][:, lo:]
                    chain(act_.activation(e, PS[:, n % 4, lo:], ACT.Abs))
                    chain.wait()
                    chain(act_.activation(e, e, ACT.Exp, scale=-1.0))
                    chain.wait()
                    act_.activation(e, e, ACT.Ln, bias=1.0).then_inc(s["sb_lse"], 1)

                lse(0)
                for n in range(len(tiles)):
                    h, half, b, lo, w = tiles[n]
                    if n + 1 < len(tiles):
                        lse(n + 1)
                    act.wait_ge(s["sb_cum"], c * len(tiles) + n + 1)
                    if n:
                        act.wait_ge(s["sb_pv"], c * len(tiles) + n)
                    act_.activation(AW[:, lo:], PS[:, n % 4, lo:], ACT.Exp).then_inc(s["sb_exp"], 1)
                act.wait_ge(s["sb_pv"], (c + 1) * len(tiles))
                chain(copy(OB[c][:], bank(6)))
                chain.wait()
                act_.activation(TA[:], OB[c][:], ACT.Square).then_inc(s["sb_osq"], 1)
                first_guess(bank(4), TB[:], "sb_osum", c + 1, "sb_o0")

            for c in range(4):
                if c == 0:
                    act.wait_ge(s["unit_done"], U_OUT2)
                    act.wait_ge(s["pool_done"], 4)
                mix_hi(c, UB[:, c, :])
            for c in range(4):
                act.wait_ge(s["sb_on"], c + 1)
                mix_hi(4 + c, OB[c][:])

            for k in range(KD):
                act.wait_ge(s["bank_free"], U_OUT2 + k + 1)
                square(MM[:, k, :], (TA, TB)[k % 2][:])
            first_guess(bank(6), RS[:], "mean_done", 4, "ln_exp")

            def after_residual(x0, name):
                for k in range(KD):
                    act.wait_ge(s["post_x"], x0 + k + 1)
                    square(X[:, k, :], (TA, TB)[k % 2][:])
                    hi(k, X[:, k, :], g(name, k))
            after_residual(0, "g_mlp_pre")
            first_guess(bank(6), RS[:], "mean_done", 5, "ln_exp")
            with act.Fori(0, NG2) as i:
                ff_hi(i, U_MLP, G, 1, NG1 * G + TAIL)
            act.wait_ge(s["ple_p_in"], 16)
            for k in range(2):
                copy(PPH[:, k, :], PPF[:, k, :]).then_inc(s["ple_hi"], 1)
            act.wait_ge(s["bank_free"], U_PLEP)
            for k in range(KD):
                square(MM[:, k, :], (TA, TB)[k % 2][:])
            first_guess(bank(6), RS[:], "mean_done", 6, "ln_exp")
            for k in range(KD):
                act.wait_ge(s["post_x"], KD + k + 1)
                copy(INL[:, k, :], X[:, k, :]).then_inc(s["split_hi"], 1)
            for k in range(KD):
                square(EMB[:, k, :], (TA, TB)[k % 2][:])
            first_guess(bank(6), RS[:], "mean_done", 7, "ln_exp")
            for k in range(KD):
                act.wait_ge(s["bank_free"], U_PLEG + k + 1)
                act_.activation((TA, TB)[k % 2][:], (TA, TB)[k % 2][:], ACT.Sigmoid).then_inc(s["ple_sig"], 1)

        @block.vector
        def _(dve):
            chain = Chain(dve, s["dve_chain"])
            stt, tt, ts = dve_.scalar_tensor_tensor, dve_.tensor_tensor, dve_.tensor_scalar

            added = [0]

            def add_square():
                n = added[0]
                dve.wait_ge(s["sq_ready"], n + 1)
                if n % KD:
                    dve.wait_ge(s["sq_added"], n)
                t = (TA, TB)[n % 2]
                if n % KD == 0:
                    dve_.tensor_copy(SQ[:], t[:]).then_inc(s["sq_added"], 1)
                else:
                    tt(SQ[:], SQ[:], t[:], ALU.add).then_inc(s["sq_added"], 1)
                added[0] += 1

            def refine(ps, y0, scale=1.0):
                chain(stt(ps, ps, EPS / scale, y0, ALU.add, ALU.mult))
                chain.wait()
                chain(stt(ps, ps, -0.5 * scale, y0, ALU.mult, ALU.mult))
                chain.wait()
                return stt(y0, ps, 1.5, y0, ALU.add, ALU.mult)

            def lo(k, src, gain=1.0):
                stt(INL[:, k, :], src, gain, INH[:, k, :].bitcast(f32), ALU.mult, ALU.subtract)\
                    .then_inc(s["split_lo"], 1)

            def scale_from(n):
                dve.wait_ge(s["ln_exp"], n)
                refine(bank(6), RS[:]).then_inc(s["scale_ready"], 1)
                dve.wait_ge(s["scale_ready"], n)

            for k in range(KD):
                dve.wait_ge(s["split_hi"], k + 1)
                lo(k, X[:, k, :], g("norm1", k))
                add_square()
            scale_from(1)
            for m in (slice(0, PADT), slice(T + PADT, T + 2 * PADT)):
                chain(dve_.memset(UP[:, :, m], 0.0))
            for c in range(4):
                dve.wait_ge(s["unit_done"], 2 * c + 1)
                if c:
                    dve.wait_ge(s["glu_sig"], c)
                tt(TA[:], bank(4 * (c % 2)), RS[:], ALU.mult).then_inc(s["bank_free"], 1)
                dve.wait_ge(s["bank_free"], 2 * c + 1)
                dve.wait_ge(s["unit_done"], 2 * c + 2)
                tt(TC[:], bank(4 * (c % 2) + 2), RS[:], ALU.mult).then_inc(s["bank_free"], 1)
                dve.wait_ge(s["bank_free"], 2 * c + 2)
                dve.wait_ge(s["glu_sig"], c + 1)
                chain(tt(UP[:, c, PADT:PADT + T], TC[:], TB[:], ALU.mult))
            chain(ts(GS[:, 0:1], g("q_g"), DH ** -0.5, None, ALU.mult))
            chain(dve_.tensor_copy(GS[:, 1:2], g("k_g")))
            chain.wait()

            def conv(c, first, last):
                for t in range(first, last):
                    src = UP[:, c, t:t + T]
                    if t == 0:
                        ins = ts(Y[:, c, :], src, TP[:, c, 0:1], g("dw_bias", c), ALU.mult, ALU.add)
                    else:
                        ins = stt(Y[:, c, :], src, TP[:, c, t:t + 1], Y[:, c, :], ALU.mult, ALU.add)
                    if t == TAPS - 1:
                        ins.then_inc(s["conv_out_done"], 1)
                        dve.wait_ge(s["conv_out_done"], c + 1)
                    else:
                        chain(ins)
                        chain.wait()

            for c in range(4):
                u = U_QKV + 3 * c

                def evac(j, t):
                    dve.wait_ge(s["unit_done"], u + j + 1)
                    tt(t[:], bank(2 * ((u + j) % 2)), RS[:], ALU.mult).then_inc(s["bank_free"], 1)
                    dve.wait_ge(s["bank_free"], u + j + 1)

                def normed(j, t):
                    dve.wait_ge(s["qk_y0"], 2 * c + j + 1)
                    chain(refine(bank(4), SQ[:]))
                    chain.wait()
                    stt(t[:], t[:], GS[:, j:j + 1], SQ[:], ALU.mult, ALU.mult).then_inc(s["qk_scaled"], 1)
                    dve.wait_ge(s["qk_scaled"], 2 * c + j + 1)
                    dve.wait_ge(s["qk_hi"], 2 * c + j + 1)
                    hi_ = (QH, KH)[j][:].bitcast(f32)
                    tt((QL, KL)[j][:], t[:], hi_, ALU.subtract).then_inc(s["qk_lo"], 1)

                def probs(m):
                    w = key_rows(m % 8)[1] * GRID_W
                    dve.wait_ge(s["probs_done"], 16 * c + m + 1)
                    chain(dve_.reciprocal(ST[:, 2, m:m + 1], ST[:, 1, m:m + 1]))
                    chain.wait()
                    ts(SB[m % 2][:, 0:w], SB[m % 2][:, 0:w], ST[:, 2, m:m + 1], None, ALU.mult)\
                        .then_inc(s["probs_scaled"], 1)

                evac(0, TA)
                conv(c, 0, 7)
                evac(1, TB)
                normed(0, TA)
                conv(c, 7, 11)
                if c:
                    dve.wait_ge(s["v_tr"], c)
                evac(2, TC)
                normed(1, TB)
                for n in range(16):
                    h, rp = 2 * c + n // 8, n % 8
                    ks, nk = key_rows(rp)
                    w = nk * GRID_W
                    if rp == 0:
                        dve.wait_ge(s[f"bt_in{h % 2}"], 16 * (h // 2 + 1))
                        chain(dve_.tensor_copy(BI[:], BT[h % 2][:, 3:12, :]))
                        chain.wait()
                        chain(dve_.memset(BI[0:GRID_W, 8, :], MASKED))
                        chain(dve_.memset(BI[GRID_W:P, 0, :], MASKED))
                        chain.wait()
                    first = ks - 2 * rp + NA_ROWS - 1
                    bias = BI[:] if nk == 9 else BT[h % 2][:, first:first + nk, :]
                    dve.wait_ge(s["scores_done"], 16 * c + n + 1)
                    if n >= 2:
                        dve.wait_ge(s["pt_done"], 16 * c + n - 1)
                    dve_.tensor_tensor_reduce(
                        out=SB[n % 2][:, 0:w], in0=bank(2)[:, 0:w], in1=bias.rearrange("p r c -> p (r c)"),
                        scale=-1.0, scalar=3.0e38, op0=ALU.add, op1=ALU.min,
                        accum_out=ST[:, 0, n:n + 1]).then_inc(s["scores_max"], 1)
                    if n:
                        probs(n - 1)
                    conv(c, 11 + n, 12 + n)
                probs(15)
                conv(c, 27, TAPS)

            chain(tt(TA[:], Y[:, 0, :], Y[:, 1, :], ALU.add))
            chain.wait()
            chain(tt(TA[:], TA[:], Y[:, 2, :], ALU.add))
            chain.wait()
            tt(TA[:], TA[:], Y[:, 3, :], ALU.add).then_inc(s["ln_in"], 1)
            dve.wait_ge(s["ln_mean"], 1)
            for c in range(4):
                stt(Y[:, c, :], bank(0), -2.0, Y[:, c, :], ALU.mult, ALU.add).then_inc(s["ln_cent"], 1)
            for c in range(4):
                dve.wait_ge(s["ln_sq"], c + 1)
                t = (TB, TC)[c % 2]
                if c == 0:
                    dve_.tensor_copy(TA[:], t[:]).then_inc(s["ln_ssq"], 1)
                else:
                    dve.wait_ge(s["ln_ssq"], c)
                    tt(TA[:], TA[:], t[:], ALU.add).then_inc(s["ln_ssq"], 1)
            dve.wait_ge(s["ln_y0"], 1)
            refine(bank(2), RS[:], scale=2.0).then_inc(s["aux_free"], 1)
            dve.wait_ge(s["aux_free"], 1)
            for c in range(4):
                tt(Y[:, c, :], Y[:, c, :], RS[:], ALU.mult).then_inc(s["ln_norm"], 1)

            def mix_lo(k, src, n0):
                dve.wait_ge(s["mix_hi"], n0 + k + 1)
                tt(INL[:, k, :], src, INH[:, k, :].bitcast(f32), ALU.subtract).then_inc(s["mix_lo"], 1)
            for k in range(KD):
                mix_lo(k, Y[:, k, :] if k < 4 else OC[k - 4][:], 0)
            for k in range(KD):
                dve.wait_ge(s["unit_done"], U_OUT + k + 1)
                dve.wait_ge(s[f"x_in{k // 2}"], 32)
                tt(X[:, k, :], bank(2 * (k % 4)), X[:, k, :], ALU.add).then_inc(s["bank_free"], 1)
                if k:
                    add_square()
            add_square()
            for k in range(KD):
                dve.wait_ge(s["split_hi"], KD + k + 1)
                lo(k, X[:, k, :], g("norm2", k))
            scale_from(2)

            def ff_lo(i, u0, n_h, up, h0, target, ff_first=False, after=None):
                per = up * G + G
                for n in range(n_h):
                    b = 4 * (n % 2) if up == 2 else 2 * (n % 4)
                    dve.wait_ge(s["unit_done"], i * per + (u0 + up * n + 1))
                    if not (ff_first and n == 0):
                        dve.wait_ge(s["ff_silu"], i * n_h + (h0 + n))
                        dve.wait_ge(s["ff_lo"], i * n_h + (h0 + n))
                    if up == 2:
                        tt(TA[:], bank(b), RS[:], ALU.mult).then_inc(s["bank_free"], 1)
                        dve.wait_ge(s["bank_free"], i * per + (u0 + up * n + 1))
                        dve.wait_ge(s["unit_done"], i * per + (u0 + up * n + 2))
                        tt(TC[:], bank(b + 2), RS[:], ALU.mult).then_inc(s["bank_free"], 1)
                        dve.wait_ge(s["bank_free"], i * per + (u0 + up * n + 2))
                        dve.wait_ge(s["ff_silu"], i * n_h + (h0 + n + 1))
                        tt(TC[:], TC[:], TB[:], ALU.mult).then_inc(s["ff_h"], 1)
                        dve.wait_ge(s["ff_h"], i * n_h + (h0 + n + 1))
                        src = TC
                    else:
                        stt(TA[:], bank(b), 0.0, RS[:], ALU.max, ALU.mult).then_inc(s["bank_free"], 1)
                        dve.wait_ge(s["bank_free"], i * per + (u0 + up * n + 1))
                        dve.wait_ge(s["ff_silu"], i * n_h + (h0 + n + 1))
                        src = TB
                    dve.wait_ge(s["ff_hi"], i * n_h + (h0 + n + 1))
                    tt(HL[:, n, :], src[:], HH[:, n, :].bitcast(f32), ALU.subtract).then_inc(s["ff_lo"], 1)
                for m in range(4):
                    dve.wait_ge(s["unit_done"], i * per + (u0 + up * n_h + m + 1))
                    for c in range(2):
                        dst = target[:, 2 * m + c, :]
                        src = bank(4 * (m % 2) + 2 * c)
                        if after == "fill":
                            ins = dve_.tensor_copy(dst, src)
                        else:
                            ins = tt(dst, src, dst, ALU.add)
                        if c == 0:
                            ins.then_inc(s["ff_acc"], 1)
                        else:
                            ins.then_inc(s["bank_free"], 1)

            def tail_lo():
                for m in range(4):
                    for k in (2 * m, 2 * m + 1):
                        add_square()
                        dve.wait_ge(s["split_hi"], 2 * KD + k + 1)
                        lo(k, X[:, k, :], g("g_mix_pre", k))

            ff_lo(0, U_FF, G, 2, 0, X, ff_first=True)
            with dve.Fori(1, NG1) as i:
                dve.wait_ge(s["bank_free"], i * (3 * G) + U_FF)
                dve.wait_ge(s["ff_acc"], i * 4)
                ff_lo(i, U_FF, G, 2, 0, X)
            dve.wait_ge(s["bank_free"], U_TAIL)
            dve.wait_ge(s["ff_acc"], NG1 * 4)
            ff_lo(0, U_TAIL, TAIL, 2, NG1 * G, X)
            tail_lo()
            scale_from(3)

            for j in range(4):
                dve.wait_ge(s["unit_done"], U_POOL + j + 1)
                tt(UB[:, j, :], bank(2 * (j % 4)), RS[:], ALU.mult).then_inc(s["bank_free"], 1)
                dve.wait_ge(s["bank_free"], U_POOL + j + 1)
            for j, w in enumerate(WINDOWS):
                src, bufs, step = UB[:, j, :], [TA[:], TB[:]], 1
                while step < w:
                    dst = bufs[0]
                    chain(dve_.tensor_copy(dst[:, 0:step], src[:, 0:step]))
                    chain(tt(dst[:, step:], src[:, step:], src[:, 0:T - step], ALU.add))
                    chain.wait()
                    src, bufs, step = dst, bufs[::-1], 2 * step
                for t in range(w - 1):
                    chain(ts(src[:, t:t + 1], src[:, t:t + 1], float(w) / (t + 1), None, ALU.mult))
                chain.wait()
                stt(UB[:, j, :], src, 1.0 / w, UB[:, j, :], ALU.mult, ALU.subtract).then_inc(s["pool_d"], 1)
                dve.wait_ge(s["pool_d"], j + 1)
            for j in range(4):
                dve.wait_ge(s["pool_y"], j + 1)
                ts(UB[:, j, :], bank(6), g("pool_scale", j), None, ALU.mult).then_inc(s["pool_done"], 1)

            tiles = sb_tiles()
            for c in range(4):
                u = U_QKV2 + 3 * c

                def evac2(j, t):
                    dve.wait_ge(s["unit_done"], u + j + 1)
                    stt(t[:], bank(2 * ((u + j) % 2)), DH ** -0.5 if j == 0 else 1.0, RS[:],
                        ALU.mult, ALU.mult).then_inc(s["bank_free"], 1)
                    dve.wait_ge(s["bank_free"], u + j + 1)
                for j in range(2):
                    evac2(j, (TA, TB)[j])
                    dve.wait_ge(s["q2_hi"], 2 * c + j + 1)
                    tt((QL, KL)[j][:], (TA, TB)[j][:], (QH, KH)[j][:].bitcast(f32), ALU.subtract)\
                        .then_inc(s["q2_lo"], 1)
                evac2(2, TC)
                dve.wait_ge(s["q2_lo"], 2 * c + 2)
                for n in range(len(tiles)):
                    h, half, b, l0, w = tiles[n]
                    N = c * len(tiles) + n
                    sp_ = SP_[n % 2]
                    dve.wait_ge(s["sb_lse"], N + 1)
                    if n >= 2:
                        dve.wait_ge(s["sb_cum"], N - 1)
                    if b < 4 * half + 3:
                        dve.wait_ge(s["sb_cum"], N)
                        top, pl = tiles[n - 1][2] == 4 * half + 3, tiles[n - 1][3]
                        before = SP_[(n - 1) % 2][:, pl:]
                        if top:
                            chain(dve_.memset(RUN[:, 0:pl], 0.0))
                            chain(dve_.tensor_copy(RUN[:, pl:], before))
                        else:
                            chain(tt(RUN[:, pl:], RUN[:, pl:], before, ALU.add))
                        chain.wait()
                    softplus = stt(sp_[:, l0:], PS[:, n % 4, l0:], 0.0, EX[n % 2][:, l0:], ALU.max, ALU.add)
                    if b * P >= half * H2:
                        chain(softplus)
                        chain.wait()
                        softplus = tt(sp_[:, l0:l0 + P], sp_[:, l0:l0 + P], KEEP[:], ALU.mult)
                    softplus.then_inc(s["sb_sp"], 1)
                    dve.wait_ge(s["sb_sp"], N + 1)
                dve.wait_ge(s["sb_o0"], c + 1)
                chain(refine(bank(4), TB[:]))
                chain.wait()
                stt(OB[c][:], OB[c][:], g("g_sb", c), TB[:], ALU.mult, ALU.mult).then_inc(s["sb_on"], 1)
                dve.wait_ge(s["sb_on"], c + 1)

            for k in range(KD):
                mix_lo(k, UB[:, k, :] if k < 4 else OB[k - 4][:], 8)
            dve.wait_ge(s["mix_lo"], 16)
            for k in range(KD):
                dve.wait_ge(s["unit_done"], U_OUT2 + k + 1)
                dve_.tensor_copy(MM[:, k, :], bank(2 * (k % 4))).then_inc(s["bank_free"], 1)
                if k:
                    add_square()
            add_square()

            def residual(name):
                for k in range(KD):
                    chain(stt(MM[:, k, :], MM[:, k, :], g(name, k), RS[:], ALU.mult, ALU.mult))
                    chain.wait()
                    tt(X[:, k, :], X[:, k, :], MM[:, k, :], ALU.add).then_inc(s["post_x"], 1)
            scale_from(4)
            residual("g_mix_post")
            for k in range(KD):
                add_square()
                dve.wait_ge(s["split_hi"], 3 * KD + k + 1)
                lo(k, X[:, k, :], g("g_mlp_pre", k))
            scale_from(5)
            h0 = NG1 * G + TAIL
            ff_lo(0, U_MLP, G, 1, h0, MM, after="fill")
            with dve.Fori(1, NG2) as i:
                dve.wait_ge(s["bank_free"], i * (2 * G) + U_MLP)
                dve.wait_ge(s["ff_acc"], i * 4 + 4 * (NG1 + 1))
                ff_lo(i, U_MLP, G, 1, h0, MM)
            for k in range(2):
                dve.wait_ge(s["ple_hi"], k + 1)
                tt(PPL[:, k, :], PPF[:, k, :], PPH[:, k, :].bitcast(f32), ALU.subtract).then_inc(s["ple_lo"], 1)
            for m in range(4):
                dve.wait_ge(s["unit_done"], U_PLEP + m + 1)
                chain(dve_.tensor_copy(EMB[:, 2 * m, :], bank(4 * (m % 2))))
                dve_.tensor_copy(EMB[:, 2 * m + 1, :], bank(4 * (m % 2) + 2)).then_inc(s["bank_free"], 1)
                for k in range(2):
                    add_square()
            scale_from(6)
            residual("g_mlp_post")
            for k in range(KD):
                dve.wait_ge(s["split_hi"], 4 * KD + k + 1)
                tt(GL[:, k, :], X[:, k, :], INL[:, k, :].bitcast(f32), ALU.subtract).then_inc(s["split_lo"], 1)
            for k in range(KD):
                add_square()
            scale_from(7)
            for k in range(KD):
                dve.wait_ge(s["unit_done"], U_PLEG + k + 1)
                t = (TA, TB)[k % 2]
                if k >= 2:
                    dve.wait_ge(s["ple_out"], k - 1)
                if k == 0:
                    dve.wait_ge(s["sq_added"], 7 * KD)
                dve_.tensor_copy(t[:], bank(2 * (k % 4))).then_inc(s["bank_free"], 1)
                dve.wait_ge(s["bank_free"], U_PLEG + k + 1)
                chain(stt(EMB[:, k, :], EMB[:, k, :], g("g_ple", k), RS[:], ALU.mult, ALU.mult))
                chain.wait()
                dve.wait_ge(s["ple_sig"], k + 1)
                chain(tt(t[:], t[:], EMB[:, k, :], ALU.mult))
                chain.wait()
                tt(X[:, k, :], X[:, k, :], t[:], ALU.add).then_inc(s["ple_out"], 1)


def units(w, k_chunks, cols):
    k, n = w.shape
    w = w.reshape(k // (P * k_chunks), k_chunks, P, n // cols, cols)
    return w.transpose(0, 3, 2, 1, 4).reshape(-1, P, k_chunks * cols)


def columns(*vectors):
    import numpy as np
    return np.concatenate([v.reshape(-1, P).T for v in vectors], axis=1)


def kernel(x, norm1_g, w_in, q_norm_g, k_norm_g, rpb, dw_kernel, dw_bias, conv_ln_g, conv_ln_b, w_out,
           norm2_g, w_gate, w_up, w_down, p_2, g_mix_pre_2, w_in_2, w_pool_2, pool_scale_2, g_sb_2,
           w_out_2, g_mix_post_2, g_mlp_pre_2, w_up_2, w_down_2, g_mlp_post_2, w_ple_gate_2,
           w_ple_proj_2, g_ple_2):
    import numpy as np
    import concourse.bacc as bacc
    from concourse.bass_utils import run_bass_kernel_spmd

    def interleave(*ws):
        return np.stack(ws, axis=1).reshape(-1, *ws[0].shape[1:])

    def chunks(a):
        return a.T.reshape(-1, P, T).transpose(1, 0, 2)

    w = units(w_in[0], KD, P)
    main = NG1 * G
    ffu = interleave(units(w_gate[0], KD, P), units(w_up[0], KD, P))
    w2 = units(w_in_2[0], KD, P)
    arrays = {
        "x": chunks(x[0]),
        "w_glu": interleave(w[4:8], w[0:4]),
        "w_qkv": interleave(w[8:12], w[12:16], w[16:20]),
        "w_out": units(w_out[0], KD, P),
        "w_ff": ffu[:2 * main],
        "w_ffd": units(w_down[0][:main * P], G, 2 * P),
        "w_tail": ffu[2 * main:],
        "w_taild": units(w_down[0][main * P:], TAIL, 2 * P),
        "gains": columns(norm1_g[0], norm2_g[0], g_mix_pre_2[0], g_mix_post_2[0], g_mlp_pre_2[0],
                         g_mlp_post_2[0], g_ple_2[0], np.concatenate([q_norm_g[0], q_norm_g[0]]),
                         np.concatenate([k_norm_g[0], k_norm_g[0]]), dw_bias[0], conv_ln_g[0],
                         conv_ln_b[0], pool_scale_2[0], g_sb_2[0]),
        "taps": dw_kernel[0].T.reshape(4, P, TAPS).transpose(1, 0, 2),
        "rpb": rpb[0],
        "p_t": p_2[0, 0].T.reshape(2, P, T).transpose(1, 0, 2),
        "w_in2": np.concatenate([w2[0:4], interleave(w2[4:8], w2[8:12], w2[12:16])]),
        "w_pool": w_pool_2[0].transpose(1, 0, 2),
        "w_out2": units(w_out_2[0], KD, P),
        "w_mlp": units(w_up_2[0], KD, P),
        "w_mlpd": units(w_down_2[0], G, 2 * P),
        "w_plep": units(w_ple_proj_2[0], 2, 2 * P),
        "w_pleg": units(w_ple_gate_2[0], KD, P),
    }
    nc = bacc.Bacc("TRN2", target_bir_lowering=False, num_devices=1)
    aps = {}
    for name, a in arrays.items():
        arrays[name] = a = np.ascontiguousarray(a)
        aps[name] = nc.dram_tensor(name, a.shape, mybir.dt.from_np(a.dtype), kind="ExternalInput").ap()
    aps["out"] = nc.dram_tensor("out", (P, KD, T), mybir.dt.float32, kind="ExternalOutput").ap()
    program(nc, **aps)
    r = run_bass_kernel_spmd(nc, [arrays], core_ids=[0])
    got = r.results[0]["out"]
    return np.ascontiguousarray(got.transpose(2, 1, 0).reshape(1, T, D))
```

```python
import concourse.bass as bass
from concourse import mybir
from contextlib import ExitStack

T = 1024
D = 1024
P = 128
KD = D // P
H2 = T // 2
EPS = 1e-6
GRID_W, ROWS, NA_ROWS, NA_COLS = 64, 16, 8, 16
HEADS, DH = 8, 64
TAPS = 31
PADT = TAPS // 2
FF1, FF2 = 2816, 4096
G = 4
NG1, TAIL = FF1 // P // G, FF1 // P % G
NG2 = FF2 // P // G
MASKED = -1.0e30
WINDOWS = (2, 4, 8, 16)

U_GLU = 0
U_QKV = U_GLU + 8
U_OUT = U_QKV + 12
U_FF = U_OUT + 8
U_TAIL = U_FF + NG1 * 3 * G
U_POOL = U_TAIL + 2 * TAIL + 4
U_QKV2 = U_POOL + 4
U_OUT2 = U_QKV2 + 12
U_MLP = U_OUT2 + 8
U_PLEP = U_MLP + NG2 * 2 * G
U_PLEG = U_PLEP + 4
U_END = U_PLEG + 8


class Chain:

    def __init__(self, eng, sem):
        self.eng, self.sem, self.base, self.local, self.i, self.per = eng, sem, 0, 0, None, 0

    def __call__(self, ins):
        ins.then_inc(self.sem, 1)
        self.local += 1
        return self.local

    def wait(self, mark=None):
        mark = self.local if mark is None else mark
        value = self.base + mark
        self.eng.wait_ge(self.sem, value if self.i is None else self.i * self.per + value)

    def enter(self, i, per):
        self.base, self.local, self.i, self.per = self.base + self.local, 0, i, per

    def leave(self, turns):
        assert self.local == self.per, (self.local, self.per)
        self.base, self.local, self.i = self.base + turns * self.per, 0, None


def key_rows(rp):
    first = [min(max(r - NA_ROWS // 2, 0), ROWS - NA_ROWS) for r in (2 * rp, 2 * rp + 1)]
    return first[0], first[1] + NA_ROWS - first[0]


def sb_tiles():
    out = []
    for h in range(2):
        for half in range(2):
            for b in range(4 * half + 3, -1, -1):
                lo = max(0, b * P - half * H2)
                out.append((h, half, b, lo, H2 - lo))
    return out


GAINS = (("norm1", 8), ("norm2", 8), ("g_mix_pre", 8), ("g_mix_post", 8), ("g_mlp_pre", 8),
         ("g_mlp_post", 8), ("g_ple", 8), ("q_g", 1), ("k_g", 1), ("dw_bias", 4), ("ln_g", 4),
         ("ln_b", 4), ("pool_scale", 4), ("g_sb", 4))


def up32(n):
    return -(-n // 32) * 32


def gains_at():
    at, out = 0, {}
    for name, n in GAINS:
        out[name] = at
        at += n
    return out


def program(nc, x, w_glu, w_qkv, w_out, w_ff, w_ffd, w_tail, w_taild, gains, taps, rpb,
            p_t, w_in2, w_pool, w_out2, w_mlp, w_mlpd, w_plep, w_pleg, out):
    f32, f32r = mybir.dt.float32, mybir.dt.float32r
    ALU, ACT = mybir.AluOpType, mybir.ActivationFunctionType

    ctx = ExitStack()
    with ctx:
        base = 16512

        def at(name, shape, offset, dt=f32):
            return nc.alloc_sbuf_tensor_at(name, shape, dt, offset=base + offset)

        def sem(name):
            return ctx.enter_context(nc.semaphore(name))

        KB32 = 4 * KD * T
        X = at("residual", [P, KD, T], 0)
        INH = at("input_hi", [P, KD, T], KB32, f32r)
        INL = at("input_lo", [P, KD, T], 2 * KB32, f32r)
        QK0 = 3 * KB32
        R2 = 4 * KB32
        W0 = 5 * KB32
        RAW = at("weight_raw", [P, 2, 1024], W0)
        WH = at("weight_hi", [P, 2, 1024], W0 + 8192, f32r)
        WL = at("weight_lo", [P, 2, 1024], W0 + 16384, f32r)
        S0 = W0 + 24576
        RS = at("token_scale", [P, T], S0)
        SQ = at("squares", [P, T], S0 + 4096)
        TA = at("work_a", [P, T], S0 + 8192)
        TB = at("work_b", [P, T], S0 + 12288)
        TC = at("work_c", [P, T], S0 + 16384)
        C0 = S0 + 20480
        IDENT = at("identity", [P, P], C0)
        MEAN = at("mean_all", [P, P], C0 + 512)
        MEANH = at("mean_head", [P, P], C0 + 1024)
        NGAIN = gains.shape[1]
        GN = at("gains_sb", [P, NGAIN], C0 + 1536)
        TP = at("taps_sb", [P, 4, TAPS], C0 + 1536 + up32(4 * NGAIN))
        C1 = C0 + 1536 + up32(4 * NGAIN) + up32(16 * TAPS)
        EPSC = at("eps_col", [P, 2], C1)
        ZERO = at("zero_col", [P, 1], C1 + 64)
        GS = at("qk_gain", [P, 2], C1 + 32)
        UP = at("glu_padded", [P, 4, T + 2 * PADT], 0)
        UW = 4 * (T + 2 * PADT)
        U4 = up32(4 * UW)
        BT = [at(f"bias_table{i}", [P, 16, GRID_W], U4 + 4096 * i) for i in range(2)]
        BI = at("bias_inner", [P, 9, GRID_W], U4 + 8192)
        SB = [at(f"scores{i}", [P, 9 * GRID_W], U4 + 8192 + 2304 * (i + 1)) for i in range(2)]
        ST = at("softmax_stats", [P, 3, 16], U4 + 8192 + 3 * 2304)
        OC = [at(f"attn_out{c}", [P, T], up32(c * UW)) for c in range(4)]
        QH, QL, KH, KL = (at(n, [P, T], QK0 + 4096 * i, f32r)
                          for i, n in enumerate(("q_hi", "q_lo", "k_hi", "k_lo")))
        V = at("v_tokens", [P, 8, P], QK0 + 16384)
        PT = [at(f"probs_t{i}", [P, 5, P], QK0 + 20480 + 2560 * i) for i in range(2)]
        Y = at("conv_out", [P, 4, T], R2)
        NEG = at("masked_tile", [P, T], R2 + 16384)
        LT = [at(f"ln_work{c}", [P, T], R2 + 16384 + 4096 * c) for c in range(4)]
        HH = at("hidden_hi", [P, G, T], R2, f32r)
        HL = at("hidden_lo", [P, G, T], R2 + 16384, f32r)
        UB = at("pool_u", [P, 4, T], R2)
        OB = [at(f"sb_out{c}", [P, T], QK0 + 16384 + 4096 * c) for c in range(4)]
        V2 = at("v2_tokens", [P, 8, P], R2 + 16384)
        NTRI = at("minus_tri", [P, P], R2 + 20480)
        NONE = at("minus_ones", [P, P], R2 + 20992)
        NMASK = at("diag_masked", [P, P], R2 + 21504)
        KEEP = at("diag_keep", [P, P], R2 + 22016)
        WP = at("w_pool_sb", [P, 4, P], R2 + 22528)
        EX = [at(f"sb_e{i}", [P, H2], R2 + 24576 + 2048 * i) for i in range(2)]
        SP_ = [at(f"sb_softplus{i}", [P, H2], R2 + 28672 + 2048 * i) for i in range(2)]
        RUN = [at(f"sb_running{i}", [P, H2], o) for i, o in enumerate((S0 + 4096, R2 + 22528))]
        AW = [at("sb_weights0", [P, H2], S0 + 6144), TA[:, 0:H2]]
        MM = at("branch_out", [P, KD, T], QK0)
        PPH = at("ple_in_hi", [P, 2, T], 2 * KB32, f32r)
        PPL = at("ple_in_lo", [P, 2, T], 2 * KB32 + 8192, f32r)
        GL = at("gate_lo", [P, KD, T], QK0, f32r)
        EMB = at("embedding", [P, KD, T], KB32)
        PPF = at("ple_in", [P, 2, T], 2 * KB32 + 16384)

        PS = ctx.enter_context(nc.psum_tensor("ps", [P, 8, H2], f32))

        def bank(b, n=2):
            return PS[:, b:b + n, :].rearrange("p b t -> p (b t)")

        names = """w_loaded0 w_loaded1 w_hi w_split unit_done bank_free consts_ready gains_in x_in0 x_in1 x_in2 x_in3
            split_hi split_lo sq_ready sq_added mean_done ln_exp scale_ready
            glu_sig qk_sq norm_sum qk_y0 qk_scaled qk_hi qk_lo v_tr v_ready
            neg_ready neg_out table_out bt_in0 bt_in1 bi_ready scores_done scores_max probs_done probs_scaled
            pt_done pt_sb pv_done head_done conv_out_done attn_out_done
            ln_in ln_mean ln_cent ln_sq ln_ssq ln_var ln_y0 ln_norm ln_silu mix_hi mix_lo
            aux_free ff_silu ff_h ff_hi ff_lo ff_acc
            act_chain dve_chain pool_chain
            sb_const sb_z sb_abs sb_lse sb_sp sb_cum sb_exp sb_pv sb_o sb_osq sb_osum
            sb_o0 sb_on pool_d pool_y pool_done q2_hi q2_lo v2_tr v2_ready pool_w_in
            post_sq post_y0 post_rs post_x
            ple_p_in ple_hi ple_lo ple_sig ple_out stored post_scaled x_first""".split()
        s = {n: sem(n) for n in names}
        block = ctx.enter_context(nc.Block())
        pool_, act_, dve_ = nc.gpsimd, nc.scalar, nc.vector
        g_of = gains_at()

        def g(name, k=0):
            return GN[:, g_of[name] + k:g_of[name] + k + 1]

        BD = nc.dram_tensor("bias_tables", [HEADS, P, 16 * GRID_W], f32).ap()
        N_TABLE_DMAS = 2 * (HEADS + NA_COLS - 1)

        @block.sync
        def _(sp):
            def load_unit(u, slot, src, width=1024):
                if not isinstance(u, int) or u >= 2:
                    sp.wait_ge(s["w_split"], u - 1)
                sp.dma_start(RAW[:, slot, 0:width], src).then_inc(s[f"w_loaded{slot}"], 16)

            def load_units(u0, w, n, width=1024):
                with sp.Fori(0, n // 2) as i:
                    for slot in range(2):
                        load_unit(i * 2 + u0 + slot, slot, w[bass.ds(i * 2 + slot, 1), :, :]
                                  .rearrange("u p n -> (u p) n"), width)

            sp.dma_start(GN[:], gains).then_inc(s["gains_in"], 16)
            sp.dma_start(TP[:], taps).then_inc(s["gains_in"], 16)
            load_unit(0, 0, w_glu[0])
            sp.dma_start(X[:, 0, :], x[:, 0, :]).then_inc(s["x_first"], 16)
            sp.dma_start(X[:, 1, :], x[:, 1, :]).then_inc(s["x_in0"], 16)
            for k in range(1, 4):
                sp.dma_start(X[:, 2 * k:2 * k + 2, :], x[:, 2 * k:2 * k + 2, :]).then_inc(s[f"x_in{k}"], 16)
            load_unit(1, 1, w_glu[1])
            for u in range(2, 8):
                load_unit(u, u % 2, w_glu[u])
            for c in range(4):
                for j in range(3):
                    u = U_QKV + 3 * c + j
                    load_unit(u, u % 2, w_qkv[3 * c + j])
                for h in (2 * c, 2 * c + 1):
                    if h >= 2:
                        sp.wait_ge(s["scores_max"], 8 * (h - 1))
                    sp.wait_ge(s["scale_ready"], 1)
                    sp.wait_ge(s["table_out"], 16 * N_TABLE_DMAS)
                    sp.dma_start(BT[h % 2][:], BD[h]).then_inc(s[f"bt_in{h % 2}"], 16)
            for j in range(2):
                load_unit(U_OUT + j, j % 2, w_out[j])
            sp.wait_ge(s["mix_lo"], 8)
            for k in range(4):
                sp.dma_start(X[:, 2 * k:2 * k + 2, :], x[:, 2 * k:2 * k + 2, :]).then_inc(s[f"x_in{k}"], 16)
            for j in range(2, 8):
                load_unit(U_OUT + j, j % 2, w_out[j])
            with sp.Fori(0, NG1) as i:
                for j in range(2 * G):
                    load_unit(i * (3 * G) + (U_FF + j), j % 2,
                              w_ff[bass.ds(i * (2 * G) + j, 1), :, :].rearrange("u p n -> (u p) n"))
                for j in range(G):
                    load_unit(i * (3 * G) + (U_FF + 2 * G + j), j % 2,
                              w_ffd[bass.ds(i * G + j, 1), :, :].rearrange("u p n -> (u p) n"))
            for j in range(2 * TAIL):
                load_unit(U_TAIL + j, j % 2, w_tail[j])
            for j in range(4):
                load_unit(U_TAIL + 2 * TAIL + j, j % 2, w_taild[j], TAIL * 256)
            for j in range(16):
                load_unit(U_POOL + j, j % 2, w_in2[j])
                if j == 1:
                    sp.wait_ge(s["unit_done"], U_POOL)
                    sp.dma_start(WP[:], w_pool).then_inc(s["pool_w_in"], 16)
            load_units(U_OUT2, w_out2, 8)
            with sp.Fori(0, NG2) as i:
                for j in range(G):
                    load_unit(i * (2 * G) + (U_MLP + j), j % 2,
                              w_mlp[bass.ds(i * G + j, 1), :, :].rearrange("u p n -> (u p) n"))
                for j in range(G):
                    load_unit(i * (2 * G) + (U_MLP + G + j), j % 2,
                              w_mlpd[bass.ds(i * G + j, 1), :, :].rearrange("u p n -> (u p) n"))
            sp.wait_ge(s["unit_done"], U_PLEP - 4)
            sp.dma_start(PPF[:], p_t).then_inc(s["ple_p_in"], 16)
            for j in range(4):
                load_unit(U_PLEP + j, j % 2, w_plep[j], 512)
            for j in range(8):
                load_unit(U_PLEG + j, j % 2, w_pleg[j])
            for k in range(KD):
                sp.wait_ge(s["ple_out"], k + 1)
                sp.dma_start(out[:, k, :], X[:, k, :]).then_inc(s["stored"], 16)
            sp.wait_ge(s["stored"], 16 * KD)

        @block.gpsimd
        def _(pool):
            pool_.memset(NEG[:], MASKED).then_inc(s["neg_ready"], 1)
            chain = Chain(pool, s["pool_chain"])
            chain(pool_.memset(EPSC[:, 0:1], EPS))
            chain(pool_.memset(ZERO[:], 0.0))
            chain(pool_.memset(IDENT[:], 0.0))
            chain(pool_.memset(MEAN[:], 1.0 / D))
            chain(pool_.memset(MEANH[:], 1.0 / DH))
            chain.wait()
            chain(pool_.affine_select(out=IDENT[:], in_=IDENT[:], compare_op=ALU.not_equal, fill=1.0,
                                      base=0, pattern=[[-1, P]], channel_multiplier=1))
            chain.wait()
            chain(pool_.memset(MEANH[0:DH, DH:P], 0.0))
            chain.wait()
            chain(pool_.memset(MEANH[DH:P, 0:DH], 0.0))
            chain.wait()
            pool_.memset(EPSC[:, 1:2], EPS).then_inc(s["consts_ready"], 1)

            def split(u, slot, turn, width=1024):
                pool.wait_ge(s[f"w_loaded{slot}"], turn)
                if not isinstance(u, int) or u >= 2:
                    pool.wait_ge(s["unit_done"], u - 1)
                raw = RAW[:, slot, 0:width]
                pool_.tensor_tensor(WH[:, slot, 0:width], raw, ZERO[:].to_broadcast([P, width]), ALU.add).then_inc(s["w_hi"], 1)
                pool.wait_ge(s["w_hi"], u + 1)
                pool_.tensor_tensor(WL[:, slot, 0:width], raw, WH[:, slot, 0:width].bitcast(f32),
                                    ALU.subtract).then_inc(s["w_split"], 1)

            def splits(u0, n, width=1024):
                with pool.Fori(0, n // 2) as i:
                    for slot in range(2):
                        split(i * 2 + (u0 + slot), slot, i * 16 + 8 * u0 + 16, width)

            for u in range(2):
                split(u, u, 16)
            splits(2, U_TAIL + 2 * TAIL - 2)
            splits(U_TAIL + 2 * TAIL, 4, TAIL * 256)
            pool.wait_ge(s["unit_done"], U_POOL)
            chain(pool_.memset(NTRI[:], -1.0))
            chain(pool_.memset(NMASK[:], 0.0))
            chain(pool_.memset(KEEP[:], 1.0))
            chain(pool_.memset(NONE[:], -1.0))
            chain.wait()
            chain(pool_.affine_select(out=NTRI[:], in_=NTRI[:], compare_op=ALU.is_ge, fill=0.0,
                                      base=0, pattern=[[-1, P]], channel_multiplier=1))
            chain(pool_.affine_select(out=NMASK[:], in_=NMASK[:], compare_op=ALU.is_ge, fill=MASKED,
                                      base=-1, pattern=[[1, P]], channel_multiplier=-1))
            chain(pool_.affine_select(out=KEEP[:], in_=KEEP[:], compare_op=ALU.is_ge, fill=0.0,
                                      base=-1, pattern=[[1, P]], channel_multiplier=-1))
            chain.wait()
            pool_.memset(EPSC[:, 1:2], EPS).then_inc(s["sb_const"], 1)
            splits(U_POOL, U_MLP + 2 - U_POOL)
            pool.wait_ge(s["scale_ready"], 4)
            for k in range(1, KD):
                pool_.tensor_tensor(MM[:, k, :], MM[:, k, :], RS[:], ALU.mult).then_inc(s["post_scaled"], 1)
            splits(U_MLP + 2, U_PLEP - U_MLP - 2)
            splits(U_PLEP, 4, 512)
            splits(U_PLEG, 8)

        @block.tensor
        def _(pe):
            mm = nc.tensor.matmul

            def unit(u, slot, b, kc=8, nc_=1, inh=INH, inl=INL, k_ready=None):
                pe.wait_ge(s["w_split"], u + 1)
                for k in range(kc):
                    if k_ready:
                        k_ready(k)
                    last = chunk(slot, b, k, kc, nc_, inh, inl)
                last.then_inc(s["unit_done"], 1)

            def chunk(slot, b, k, kc=8, nc_=1, inh=INH, inl=INL):
                n = P * nc_
                for step, (w, a) in enumerate(((WH, inh), (WH, inl), (WL, inh))):
                    for c in range(nc_):
                        for h in range(2):
                            last = mm(PS[:, b + 2 * c + h, :],
                                      w[:, slot, k * n + P * c:k * n + P * (c + 1)],
                                      a[:, k, h * H2:(h + 1) * H2],
                                      start=(k == 0 and step == 0),
                                      stop=(k == kc - 1 and step == 2))
                return last

            def first_two(u, k_ready, inh=INH, inl=INL):
                order = [(j, k) for k in range(6) for j in range(2)] + [(0, 6), (0, 7), (1, 6), (1, 7)]
                for j, k in order:
                    if k == 0:
                        pe.wait_ge(s["w_split"], u + j + 1)
                    if j == 0:
                        k_ready(k)
                    last = chunk(j, 2 * j, k, inh=inh, inl=inl)
                    if k == KD - 1:
                        last.then_inc(s["unit_done"], 1)

            def mean(mat, src, b, signal):
                for h in range(2):
                    last = mm(PS[:, b + h, :], mat[:], src[:, h * H2:(h + 1) * H2], start=True, stop=True)
                last.then_inc(s[signal], 1)

            def inputs(hi0, lo0):
                def ready(k):
                    pe.wait_ge(s["split_hi"], hi0 + k + 1)
                    pe.wait_ge(s["split_lo"], lo0 + k + 1)
                return ready

            pe.wait_ge(s["consts_ready"], 1)
            first_two(0, inputs(0, 0))
            for u in range(2, 8):
                if u == 2:
                    pe.wait_ge(s["sq_added"], KD)
                    mean(MEAN, SQ, 6, "mean_done")
                if u == 3:
                    pe.wait_ge(s["scale_ready"], 1)
                if u >= 4:
                    pe.wait_ge(s["bank_free"], u - 3)
                unit(u, u % 2, 2 * (u % 4))

            for c in range(4):
                u = U_QKV + 3 * c
                pe.wait_ge(s["bank_free"], u)
                if c:
                    pe.wait_ge(s["scores_max"], 16 * c)
                unit(u, u % 2, 2 * (u % 2))
                if c == 3:
                    pe.wait_ge(s["attn_out_done"], 3)
                    pe.wait_ge(s["ln_in"], 1)
                    mean(MEAN, LT[0], 6, "ln_mean")

                def head_sum(j):
                    def at_chunk(k):
                        if k == 3 - 2 * j:
                            pe.wait_ge(s["qk_sq"], 2 * c + j + 1)
                            if c == 3 and j:
                                pe.wait_ge(s["ln_cent"], 4)
                            if c and j:
                                pe.wait_ge(s["attn_out_done"], c)
                            elif c:
                                pe.wait_ge(s["pt_sb"], 16 * c)
                            mean(MEANH, (SQ, TC)[j], 4 + 2 * j, "norm_sum")
                    return at_chunk
                if c == 0:
                    pe.wait_ge(s["bank_free"], 8)
                unit(u + 1, (u + 1) % 2, 2 * ((u + 1) % 2), k_ready=head_sum(0))
                pe.wait_ge(s["bank_free"], u + 1)
                unit(u + 2, u % 2, 2 * (u % 2), k_ready=head_sum(1))

                def scores(n):
                    h, rp = n // 8, n % 8
                    ks, nk = key_rows(rp)
                    lo = DH * h
                    if n == 0:
                        pe.wait_ge(s["qk_hi"], 2 * c + 2)
                        pe.wait_ge(s["qk_lo"], 2 * c + 2)
                    else:
                        pe.wait_ge(s["scores_max"], 16 * c + n)
                    for q, k_, step in ((QH, KH, 0), (QH, KL, 1), (QL, KH, 2)):
                        for b, w in ((0, 512), (1, nk * GRID_W - 512)):
                            if w:
                                last = mm(PS[:, 2 + b, 0:w], q[lo:lo + DH, rp * P:(rp + 1) * P],
                                          k_[lo:lo + DH, ks * GRID_W + b * 512:ks * GRID_W + b * 512 + w],
                                          start=(step == 0), stop=(step == 2))
                    last.then_inc(s["scores_done"], 1)

                def turn(n):
                    _, nk = key_rows(n % 8)
                    pe.wait_ge(s["probs_scaled"], 16 * c + n + 1)
                    if n:
                        pe.wait_ge(s["pt_sb"], 16 * c + n)
                    else:
                        pe.wait_ge(s["v_ready"], c + 1)
                    for b in range(5 if nk == 9 else 4):
                        w = P if b < 4 else GRID_W
                        last = nc.tensor.transpose(PS[0:w, 4 + b // 4, (b % 4) * P:(b % 4 + 1) * P],
                                                   SB[n % 2][:, b * P:b * P + w], IDENT[:])
                    last.then_inc(s["pt_done"], 1)

                def values(n):
                    h, rp = n // 8, n % 8
                    ks, nk = key_rows(rp)
                    pe.wait_ge(s["pt_sb"], 16 * c + n + 1)
                    nb = 5 if nk == 9 else 4
                    for b in range(nb):
                        w = P if b < 4 else GRID_W
                        last = mm(PS[DH * h:DH * (h + 1), 6 + rp // 4, (rp % 4) * P:(rp % 4 + 1) * P],
                                  V[0:w, ks // 2 + b, DH * h:DH * (h + 1)], PT[n % 2][0:w, b, :],
                                  start=(b == 0), stop=(b == nb - 1), skip_group_check=True)
                    last.then_inc(s["pv_done"], 1)

                pe.wait_ge(s["bank_free"], u + 3)
                scores(0)
                if c:
                    pe.wait_ge(s["attn_out_done"], c)
                for b in range(8):
                    last = nc.tensor.transpose(PS[:, 6 + b // 4, (b % 4) * P:(b % 4 + 1) * P],
                                               TC[:, b * P:(b + 1) * P], IDENT[:])
                last.then_inc(s["v_tr"], 1)
                if c == 3:
                    pe.wait_ge(s["ln_ssq"], 3)
                    mean(MEAN, LT[0], 0, "ln_var")
                for n in range(16):
                    if n < 15:
                        scores(n + 1)
                    if n:
                        values(n - 1)
                    turn(n)
                values(15)

            for j in range(8):
                u = U_OUT + j
                if j >= 4:
                    pe.wait_ge(s["bank_free"], u - 3)
                elif j == 3:
                    pe.wait_ge(s["attn_out_done"], 4)
                elif j == 2:
                    pe.wait_ge(s["pt_sb"], 64)
                elif j == 1:
                    pe.wait_ge(s["scores_max"], 64)
                else:
                    pe.wait_ge(s["aux_free"], 1)

                def mix_ready(k):
                    pe.wait_ge(s["mix_hi"], k + 1)
                    pe.wait_ge(s["mix_lo"], k + 1)
                unit(u, j % 2, 2 * (j % 4), k_ready=mix_ready if j == 0 else None)

            def scale_sum(squares):
                pe.wait_ge(s["sq_added"], squares)
                mean(MEAN, SQ, 6, "mean_done")

            def scale_left(n):
                pe.wait_ge(s["scale_ready"], n)

            def ff_group(i, u0, n_h, up, split0, first=False, ready=None, scale=0):
                for j in range(2 if first else 0, up * n_h):
                    u = i * (up * G + G) + (u0 + j)
                    if first and j == 2:
                        pe.wait_ge(s["bank_free"], u0 - 2)
                        first_two(u0, ready)
                        pe.wait_ge(s["bank_free"], u0)
                        scale_sum(scale * KD)
                    if j < 4:
                        if not first:
                            pe.wait_ge(s["bank_free"], u - j + (-1 if j < 2 else 0))
                    else:
                        pe.wait_ge(s["bank_free"], u - 3)
                    if first and j == 3:
                        scale_left(scale)
                    unit(u, j % 2, 2 * (j % 4))
                for m in range(4):
                    u = i * (up * G + G) + (u0 + up * n_h + m)
                    if up * n_h >= 4 and m < 2:
                        pe.wait_ge(s["bank_free"], u - m - (2 if m == 0 else 0))
                    else:
                        pe.wait_ge(s["bank_free"], u - 1)

                    def hidden(k):
                        pe.wait_ge(s["ff_hi"], i * n_h + (split0 + k + 1))
                        pe.wait_ge(s["ff_lo"], i * n_h + (split0 + k + 1))
                    unit(u, m % 2, 4 * (m % 2), kc=n_h, nc_=2, inh=HH, inl=HL,
                         k_ready=hidden if m == 0 else None)

            ff_group(0, U_FF, G, 2, 0, first=True, ready=inputs(KD, KD), scale=2)
            with pe.Fori(1, NG1) as i:
                ff_group(i, U_FF, G, 2, 0)
            ff_group(0, U_TAIL, TAIL, 2, NG1 * G)

            pe.wait_ge(s["bank_free"], U_POOL - 1)
            first_two(U_POOL, inputs(2 * KD, 2 * KD))
            pe.wait_ge(s["bank_free"], U_POOL)
            scale_sum(3 * KD)
            for j in range(2, 4):
                if j == 3:
                    scale_left(3)
                unit(U_POOL + j, j % 2, 2 * (j % 4))
            pe.wait_ge(s["pool_w_in"], 16)
            for j in range(4):
                pe.wait_ge(s["pool_d"], j + 1)
                pe.wait_ge(s["bank_free"], U_POOL + 4)
                if j >= 1:
                    pe.wait_ge(s["pool_done"], j)
                for h in range(2):
                    last = mm(PS[:, 6 + h, :], WP[:, j, :], UB[:, j, h * H2:(h + 1) * H2], start=True, stop=True)
                last.then_inc(s["pool_y"], 1)
            pe.wait_ge(s["pool_done"], 4)

            pe.wait_ge(s["sb_const"], 1)
            tile = 0
            for c in range(4):
                u = U_QKV2 + 3 * c
                pe.wait_ge(s["bank_free"], u - 1)
                if c:
                    pe.wait_ge(s["sb_exp"], tile)
                for j in range(3):
                    pe.wait_ge(s["bank_free"], u + j - 1)
                    unit(u + j, (u + j) % 2, 2 * ((u + j) % 2))
                pe.wait_ge(s["bank_free"], u + 3)
                if c:
                    pe.wait_ge(s["sb_on"], c)
                for b in range(8):
                    last = nc.tensor.transpose(PS[:, 4 + b // 4, (b % 4) * P:(b % 4 + 1) * P],
                                               TC[:, b * P:(b + 1) * P], IDENT[:])
                last.then_inc(s["v2_tr"], 1)
                pe.wait_ge(s["q2_hi"], 2 * c + 2)
                pe.wait_ge(s["q2_lo"], 2 * c + 2)
                pe.wait_ge(s["bank_free"], u + 3)
                tiles = sb_tiles()

                def z_tile(n):
                    h, half, b, lo, w = tiles[n]
                    r = DH * h
                    if n >= 4:
                        pe.wait_ge(s["sb_exp"], c * len(tiles) + n - 3)
                    for q, k_, step in ((QH, KH, 0), (QL, KH, 1), (QH, KL, 2)):
                        last = mm(PS[:, n % 4, lo:], k_[r:r + DH, b * P:(b + 1) * P],
                                  q[r:r + DH, half * H2 + lo:(half + 1) * H2],
                                  start=(step == 0), stop=(step == 2), skip_group_check=True)
                    last.then_inc(s["sb_z"], 1)

                def cum_tile(n):
                    h, half, b, lo, w = tiles[n]
                    diag = b * P >= half * H2
                    pe.wait_ge(s["sb_sp"], c * len(tiles) + n + 1)
                    if diag:
                        mm(PS[:, n % 4, lo:lo + P], IDENT[:], NMASK[:], start=False, stop=False,
                           skip_group_check=True)
                    if b < 4 * half + 3:
                        mm(PS[:, n % 4, lo:], NONE[:], RUN[n % 2][:, lo:], start=False, stop=False,
                           skip_group_check=True)
                    mm(PS[:, n % 4, lo:], NTRI[:], SP_[n % 2][:, lo:], start=False, stop=True,
                       skip_group_check=True).then_inc(s["sb_cum"], 1)

                def pv_tile(n):
                    h, half, b, lo, w = tiles[n]
                    pe.wait_ge(s["sb_exp"], c * len(tiles) + n + 1)
                    if n == 0:
                        pe.wait_ge(s["v2_ready"], c + 1)
                        if c:
                            pe.wait_ge(s["sb_on"], c)
                    mm(PS[DH * h:DH * (h + 1), 6 + half, lo:], V2[:, b, DH * h:DH * (h + 1)],
                       AW[n % 2][:, lo:], start=(b == 4 * half + 3), stop=(b == 0),
                       skip_group_check=True).then_inc(s["sb_pv"], 1)

                z_tile(0)
                z_tile(1)
                for n in range(len(tiles)):
                    if n + 2 < len(tiles):
                        z_tile(n + 2)
                    cum_tile(n)
                    if n:
                        pv_tile(n - 1)
                pv_tile(len(tiles) - 1)
                tile += len(tiles)
                pe.wait_ge(s["sb_osq"], c + 1)
                mean(MEANH, TA, 4, "sb_osum")

            for j in range(8):
                u = U_OUT2 + j
                if j >= 4:
                    pe.wait_ge(s["bank_free"], u - 3)
                elif j == 0:
                    pe.wait_ge(s["sb_exp"], tile)
                elif j == 2:
                    pe.wait_ge(s["sb_on"], 4)

                def mix_ready(k):
                    pe.wait_ge(s["mix_hi"], 8 + k + 1)
                    pe.wait_ge(s["mix_lo"], 8 + k + 1)
                unit(u, j % 2, 2 * (j % 4), k_ready=mix_ready if j == 0 else None)
            pe.wait_ge(s["bank_free"], U_MLP)
            scale_sum(4 * KD)
            ff_group(0, U_MLP, G, 1, NG1 * G + TAIL, first=True, ready=inputs(3 * KD, 3 * KD), scale=5)
            with pe.Fori(1, NG2) as i:
                ff_group(i, U_MLP, G, 1, NG1 * G + TAIL)
            for m in range(4):
                u = U_PLEP + m
                b = (0, 0, 4, 0)[m]
                if m == 1:
                    pe.wait_ge(s["bank_free"], U_PLEP)
                    scale_sum(6 * KD)
                if m == 2:
                    scale_left(6)
                pe.wait_ge(s["bank_free"], u - 1 if m != 1 else u)

                def p_ready(k):
                    pe.wait_ge(s["ple_hi"], k + 1)
                    pe.wait_ge(s["ple_lo"], k + 1)
                unit(u, m % 2, b, kc=2, nc_=2, inh=PPH, inl=PPL,
                     k_ready=p_ready if m == 0 else None)
            pe.wait_ge(s["bank_free"], U_PLEG)
            first_two(U_PLEG, inputs(4 * KD, 4 * KD), INL, GL)
            for j in range(2, 8):
                u = U_PLEG + j
                if j >= 3:
                    pe.wait_ge(s["bank_free"], u - 2)
                if j == 4:
                    scale_sum(7 * KD)
                unit(u, j % 2, 2 * (j % 3), inh=INL, inl=GL)

        @block.scalar
        def _(act):
            chain = Chain(act, s["act_chain"])
            copy = lambda out, in_, scale=1.0: act_.activation(out, in_, ACT.Copy, scale=scale)
            lnexp = "natural_log_exp_and_others"

            sq_count = [0]

            def square(src, dst):
                n = sq_count[0]
                if n >= 2:
                    act.wait_ge(s["sq_added"], n - 1)
                act_.activation(dst, src, ACT.Square).then_inc(s["sq_ready"], 1)
                sq_count[0] += 1

            def first_guess(ps, dst, wait, value, signal, scale=1.0):
                act.wait_ge(s[wait], value)
                act_.preload_act_table_set(lnexp)
                chain(act_.activation(dst, ps, ACT.Ln, bias=EPSC[:, 0:1], scale=scale))
                chain.wait()
                act_.activation(dst, dst, ACT.Exp, scale=-0.5).then_inc(s[signal], 1)

            def hi(k, src, gain):
                act_.activation(INH[:, k, :], src, ACT.Identity, scale=gain).then_inc(s["split_hi"], 1)

            act.wait_ge(s["gains_in"], 32)
            act.wait_ge(s["consts_ready"], 1)
            for k in range(KD):
                act.wait_ge(s[f"x_in{k // 2}" if k else "x_first"], 16)
                hi(k, X[:, k, :], g("norm1", k))
                square(X[:, k, :], (TA, TB)[k % 2][:])
            first_guess(bank(6), RS[:], "mean_done", 1, "ln_exp")
            act.wait_ge(s["neg_ready"], 1)
            for h in range(HEADS):
                act.dma_start(BD[h], NEG[:]).then_inc(s["neg_out"], 16)

            def bias_windows():
                act.wait_ge(s["neg_out"], 16 * HEADS)
                rows, cols = 2 * NA_ROWS - 1, 2 * NA_COLS - 1
                half = NA_COLS // 2
                inner = GRID_W - NA_COLS + 1
                with nc.allow_non_contiguous_dma(reason="64-byte windows of the bias"):
                    for r in range(2):
                        for h in range(HEADS):
                            dst = bass.AP(tensor=BD.tensor, offset=((h * P + r * GRID_W + half) * 16 + r) * GRID_W,
                                          ap=[[16 * GRID_W + 1, inner], [GRID_W, rows], [1, NA_COLS]])
                            src = bass.AP(tensor=rpb.tensor, offset=h * rows * cols + half - 1,
                                          ap=[[0, inner], [cols, rows], [1, NA_COLS]])
                            act.dma_start(dst, src).then_inc(s["table_out"], 16)
                        for q in [*range(half), *range(half + inner, GRID_W)]:
                            start = 0 if q < half else GRID_W - NA_COLS
                            dst = bass.AP(tensor=BD.tensor, offset=((r * GRID_W + q) * 16 + r) * GRID_W + start,
                                          ap=[[P * 16 * GRID_W, HEADS], [GRID_W, rows], [1, NA_COLS]])
                            src = bass.AP(tensor=rpb.tensor, offset=start - q + NA_COLS - 1,
                                          ap=[[rows * cols, HEADS], [cols, rows], [1, NA_COLS]])
                            act.dma_start(dst, src).then_inc(s["table_out"], 16)

            for c in range(4):
                act.wait_ge(s["bank_free"], 2 * c + 1)
                act_.activation(TB[:], TA[:], ACT.Sigmoid).then_inc(s["glu_sig"], 1)
                if c == 1:
                    bias_windows()

            MIX = [Y[:, c, :] for c in range(4)] + [OC[c][:] for c in range(4)]

            def mix_hi(k, src):
                copy(INH[:, k, :], src).then_inc(s["mix_hi"], 1)

            for c in range(4):
                def head_square(j):
                    act.wait_ge(s["bank_free"], U_QKV + 3 * c + j + 1)
                    if j and c:
                        act.wait_ge(s["v_tr"], c)
                    act_.activation((SQ, TC)[j][:], (TA, TB)[j][:], ACT.Square).then_inc(s["qk_sq"], 1)

                def head_hi(j):
                    act.wait_ge(s["qk_scaled"], 2 * c + j + 1)
                    if j == 0 and c:
                        act.wait_ge(s["scores_done"], 16 * c)
                    copy((QH, KH)[j][:], (TA, TB)[j][:]).then_inc(s["qk_hi"], 1)

                head_square(0)
                if c == 3:
                    for m in range(4):
                        act.wait_ge(s["ln_cent"], m + 1)
                        act_.activation(LT[m][:], Y[:, m, :], ACT.Square).then_inc(s["ln_sq"], 1)
                first_guess(bank(4), SQ[:], "norm_sum", 2 * c + 1, "qk_y0")
                head_square(1)
                head_hi(0)
                first_guess(bank(6), TC[:], "norm_sum", 2 * c + 2, "qk_y0")
                head_hi(1)
                act.wait_ge(s["v_tr"], c + 1)
                if c:
                    act.wait_ge(s["pv_done"], 16 * c)
                copy(V[:, :, :].rearrange("p b d -> p (b d)"), bank(6)).then_inc(s["v_ready"], 1)
                for n in range(16):
                    _, nk = key_rows(n % 8)
                    w = nk * GRID_W

                    def exps(m):
                        wm = key_rows(m % 8)[1] * GRID_W
                        act.wait_ge(s["scores_max"], 16 * c + m + 1)
                        act_.activation(SB[m % 2][:, 0:wm], SB[m % 2][:, 0:wm], ACT.Exp, scale=-1.0,
                                        bias=ST[:, 0, m:m + 1], accum_out=ST[:, 1, m:m + 1])\
                            .then_inc(s["probs_done"], 1)
                    if n == 0:
                        exps(0)
                    if n < 15:
                        exps(n + 1)
                    if c == 3 and n == 1:
                        first_guess(bank(0), LT[1][:], "ln_var", 1, "ln_y0", scale=2.0)
                    if c == 3 and n == 7:
                        for m in range(4):
                            act.wait_ge(s["ln_norm"], m + 1)
                            act_.activation(Y[:, m, :], Y[:, m, :], ACT.Silu, bias=g("ln_b", m),
                                            scale=g("ln_g", m)).then_inc(s["ln_silu"], 1)
                    if c == 3 and 8 <= n < 15:
                        if n == 8:
                            act.wait_ge(s["unit_done"], U_OUT)
                            act.wait_ge(s["ln_silu"], 4)
                        mix_hi(n - 8, MIX[n - 8])
                    act.wait_ge(s["pt_done"], 16 * c + n + 1)
                    if n >= 2:
                        act.wait_ge(s["pv_done"], 16 * c + n - 1)
                    if nk == 9:
                        copy(PT[n % 2][0:GRID_W, 4, :], PS[0:GRID_W, 5, 0:P])
                    copy(PT[n % 2][:, 0:4, :].rearrange("p b q -> p (b q)"), PS[:, 4, :])\
                        .then_inc(s["pt_sb"], 1)
                act.wait_ge(s["pv_done"], 16 * (c + 1))
                act.wait_ge(s["conv_out_done"], c + 1)
                copy(OC[c][:], bank(6)).then_inc(s["attn_out_done"], 1)
            act.wait_ge(s["attn_out_done"], 4)
            mix_hi(7, OC[3][:])

            for k in range(KD):
                if k < KD - 1:
                    act.wait_ge(s["bank_free"], U_OUT + k + 1)
                    square(X[:, k, :], (TA, TB)[k % 2][:])
            act.wait_ge(s["unit_done"], U_FF)
            for k in range(KD):
                if k == 2:
                    act.wait_ge(s["bank_free"], U_FF)
                    square(X[:, KD - 1, :], (TA, TB)[(KD - 1) % 2][:])
                hi(k, X[:, k, :], g("norm2", k))
            first_guess(bank(6), RS[:], "mean_done", 2, "ln_exp")

            def ff_hi(i, u0, n_h, up, h0):
                for n in range(n_h):
                    act.wait_ge(s["bank_free"], i * (up * G + G) + (u0 + up * n + 1))
                    if up == 2:
                        act_.activation(TB[:], TA[:], ACT.Silu).then_inc(s["ff_silu"], 1)
                    else:
                        act_.activation(TB[:], TA[:], ACT.Square).then_inc(s["ff_silu"], 1)
                    if up == 2:
                        act.wait_ge(s["ff_h"], i * n_h + (h0 + n + 1))
                        src = TC
                    else:
                        act.wait_ge(s["ff_silu"], i * n_h + (h0 + n + 1))
                        src = TB
                    act.wait_ge(s["unit_done"], i * (up * G + G) + u0)
                    copy(HH[:, n, :], src[:]).then_inc(s["ff_hi"], 1)

            with act.Fori(0, NG1) as i:
                ff_hi(i, U_FF, G, 2, 0)
            ff_hi(0, U_TAIL, TAIL, 2, NG1 * G)

            def two_chunks(u0, name):
                for m in range(4):
                    act.wait_ge(s["bank_free"], u0 + m + 1)
                    for k in (2 * m, 2 * m + 1):
                        hi(k, X[:, k, :], g(name, k))
                    for k in (2 * m, 2 * m + 1):
                        square(X[:, k, :], (TA, TB)[k % 2][:])
            two_chunks(U_TAIL + 2 * TAIL, "g_mix_pre")
            first_guess(bank(6), RS[:], "mean_done", 3, "ln_exp")

            act_.preload_act_table_set(lnexp)
            tiles = sb_tiles()
            for c in range(4):
                for j in range(2):
                    act.wait_ge(s["bank_free"], U_QKV2 + 3 * c + j + 1)
                    if c:
                        act.wait_ge(s["sb_z"], c * len(tiles))
                    copy((QH, KH)[j][:], (TA, TB)[j][:]).then_inc(s["q2_hi"], 1)
                act.wait_ge(s["v2_tr"], c + 1)
                if c:
                    act.wait_ge(s["sb_pv"], c * len(tiles))
                copy(V2[:, :, :].rearrange("p b d -> p (b d)"), bank(4)).then_inc(s["v2_ready"], 1)

                def lse(n):
                    h, half, b, lo, w = tiles[n]
                    act.wait_ge(s["sb_z"], c * len(tiles) + n + 1)
                    if n >= 2:
                        act.wait_ge(s["sb_sp"], c * len(tiles) + n - 1)
                    e = EX[n % 2][:, lo:]
                    chain(act_.activation(e, PS[:, n % 4, lo:], ACT.Abs))
                    chain.wait()
                    chain(act_.activation(e, e, ACT.Exp, scale=-1.0))
                    chain.wait()
                    act_.activation(e, e, ACT.Ln, bias=1.0).then_inc(s["sb_lse"], 1)

                lse(0)
                for n in range(len(tiles)):
                    h, half, b, lo, w = tiles[n]
                    if n + 1 < len(tiles):
                        lse(n + 1)
                    act.wait_ge(s["sb_cum"], c * len(tiles) + n + 1)
                    if n >= 2:
                        act.wait_ge(s["sb_pv"], c * len(tiles) + n - 1)
                    act_.activation(AW[n % 2][:, lo:], PS[:, n % 4, lo:], ACT.Exp).then_inc(s["sb_exp"], 1)
                act.wait_ge(s["sb_pv"], (c + 1) * len(tiles))
                chain(copy(OB[c][:], bank(6)))
                chain.wait()
                act_.activation(TA[:], OB[c][:], ACT.Square).then_inc(s["sb_osq"], 1)
                first_guess(bank(4), TB[:], "sb_osum", c + 1, "sb_o0")

            for c in range(4):
                if c == 0:
                    act.wait_ge(s["unit_done"], U_OUT2)
                    act.wait_ge(s["pool_done"], 4)
                mix_hi(c, UB[:, c, :])
            for c in range(4):
                act.wait_ge(s["sb_on"], c + 1)
                mix_hi(4 + c, OB[c][:])

            for k in range(KD):
                act.wait_ge(s["bank_free"], U_OUT2 + k + 1)
                square(MM[:, k, :], (TA, TB)[k % 2][:])
            first_guess(bank(6), RS[:], "mean_done", 4, "ln_exp")

            for k in range(KD):
                act.wait_ge(s["post_x"], k + 1)
                hi(k, X[:, k, :], g("g_mlp_pre", k))
                square(X[:, k, :], (TA, TB)[k % 2][:])
            first_guess(bank(6), RS[:], "mean_done", 5, "ln_exp")
            with act.Fori(0, NG2) as i:
                ff_hi(i, U_MLP, G, 1, NG1 * G + TAIL)
            act.wait_ge(s["ple_p_in"], 16)
            for k in range(2):
                copy(PPH[:, k, :], PPF[:, k, :]).then_inc(s["ple_hi"], 1)
            for m in range(4):
                act.wait_ge(s["bank_free"], U_PLEP - 4 + m + 1)
                for k in (2 * m, 2 * m + 1):
                    square(MM[:, k, :], (TA, TB)[k % 2][:])

            def embedding(m):
                act.wait_ge(s["unit_done"], U_PLEP + m + 1)
                chain(copy(EMB[:, 2 * m, :], bank((0, 0, 4, 0)[m])))
                copy(EMB[:, 2 * m + 1, :], bank((2, 2, 6, 2)[m])).then_inc(s["bank_free"], 1)
            embedding(0)
            first_guess(bank(6), RS[:], "mean_done", 6, "ln_exp")
            embedding(1)
            embedding(2)
            embedding(3)
            for k in range(KD):
                act.wait_ge(s["post_x"], KD + k + 1)
                copy(INL[:, k, :], X[:, k, :]).then_inc(s["split_hi"], 1)
            act.wait_ge(s["bank_free"], U_PLEG)
            chain.wait()
            for k in range(KD):
                square(EMB[:, k, :], (TA, TB)[k % 2][:])

            def gate(k):
                act.wait_ge(s["unit_done"], U_PLEG + k + 1)
                if k < 2:
                    act.wait_ge(s["sq_added"], 7 * KD)
                else:
                    act.wait_ge(s["ple_out"], k - 1)
                act_.activation((TA, TB)[k % 2][:], bank(2 * (k % 3)), ACT.Sigmoid).then_inc(s["bank_free"], 1)
            gate(0)
            gate(1)
            first_guess(bank(6), RS[:], "mean_done", 7, "ln_exp")
            for k in range(2, KD):
                gate(k)

        @block.vector
        def _(dve):
            chain = Chain(dve, s["dve_chain"])
            stt, tt, ts = dve_.scalar_tensor_tensor, dve_.tensor_tensor, dve_.tensor_scalar

            added = [0]

            def add_square():
                n = added[0]
                dve.wait_ge(s["sq_ready"], n + 1)
                if n % KD:
                    dve.wait_ge(s["sq_added"], n)
                t = (TA, TB)[n % 2]
                if n % KD == 0:
                    dve_.tensor_copy(SQ[:], t[:]).then_inc(s["sq_added"], 1)
                else:
                    tt(SQ[:], SQ[:], t[:], ALU.add).then_inc(s["sq_added"], 1)
                added[0] += 1

            def refine(ps, y0, scale=1.0):
                chain(stt(ps, ps, EPS / scale, y0, ALU.add, ALU.mult))
                chain.wait()
                chain(stt(ps, ps, -0.5 * scale, y0, ALU.mult, ALU.mult))
                chain.wait()
                return stt(y0, ps, 1.5, y0, ALU.add, ALU.mult)

            def lo(k, src, gain=1.0):
                stt(INL[:, k, :], src, gain, INH[:, k, :].bitcast(f32), ALU.mult, ALU.subtract)\
                    .then_inc(s["split_lo"], 1)

            def scale_from(n):
                dve.wait_ge(s["ln_exp"], n)
                refine(bank(6), RS[:]).then_inc(s["scale_ready"], 1)
                dve.wait_ge(s["scale_ready"], n)

            for k in range(KD):
                dve.wait_ge(s["split_hi"], k + 1)
                lo(k, X[:, k, :], g("norm1", k))
                add_square()
            scale_from(1)
            for m in (slice(0, PADT), slice(T + PADT, T + 2 * PADT)):
                chain(dve_.memset(UP[:, :, m], 0.0))
            chain(ts(GS[:, 0:1], g("q_g"), DH ** -0.5, None, ALU.mult))
            chain(dve_.tensor_copy(GS[:, 1:2], g("k_g")))
            chain.wait()

            tap = [0]

            def conv(n):
                for _ in range(n):
                    c, t = divmod(tap[0], TAPS)
                    src = UP[:, c, t:t + T]
                    if t == 0:
                        ins = ts(Y[:, c, :], src, TP[:, c, 0:1], g("dw_bias", c), ALU.mult, ALU.add)
                    else:
                        ins = stt(Y[:, c, :], src, TP[:, c, t:t + 1], Y[:, c, :], ALU.mult, ALU.add)
                    if t == TAPS - 1:
                        ins.then_inc(s["conv_out_done"], 1)
                        dve.wait_ge(s["conv_out_done"], c + 1)
                    else:
                        chain(ins)
                        chain.wait()
                    tap[0] += 1

            for c in range(4):
                dve.wait_ge(s["unit_done"], 2 * c + 1)
                if c:
                    dve.wait_ge(s["glu_sig"], c)
                tt(TA[:], bank(4 * (c % 2)), RS[:], ALU.mult).then_inc(s["bank_free"], 1)
                dve.wait_ge(s["bank_free"], 2 * c + 1)
                if c:
                    conv(6)
                dve.wait_ge(s["unit_done"], 2 * c + 2)
                tt(TC[:], bank(4 * (c % 2) + 2), RS[:], ALU.mult).then_inc(s["bank_free"], 1)
                dve.wait_ge(s["bank_free"], 2 * c + 2)
                dve.wait_ge(s["glu_sig"], c + 1)
                chain(tt(UP[:, c, PADT:PADT + T], TC[:], TB[:], ALU.mult))
                if c:
                    conv(6)
            MIX = [Y[:, c, :] for c in range(4)] + [OC[c][:] for c in range(4)]

            def mix_lo(k, src, n0):
                dve.wait_ge(s["mix_hi"], n0 + k + 1)
                tt(INL[:, k, :], src, INH[:, k, :].bitcast(f32), ALU.subtract).then_inc(s["mix_lo"], 1)

            for c in range(4):
                u = U_QKV + 3 * c
                if c == 3:
                    assert tap[0] == 4 * TAPS

                def evac(j, t):
                    dve.wait_ge(s["unit_done"], u + j + 1)
                    tt(t[:], bank(2 * ((u + j) % 2)), RS[:], ALU.mult).then_inc(s["bank_free"], 1)
                    dve.wait_ge(s["bank_free"], u + j + 1)

                def head_refine(j):
                    dve.wait_ge(s["qk_y0"], 2 * c + j + 1)
                    chain(refine(bank(4 + 2 * j), (SQ, TC)[j][:]))

                def head_scale(j):
                    t = (TA, TB)[j]
                    chain.wait()
                    stt(t[:], t[:], GS[:, j:j + 1], (SQ, TC)[j][:], ALU.mult, ALU.mult).then_inc(s["qk_scaled"], 1)

                def head_lo(j):
                    dve.wait_ge(s["qk_hi"], 2 * c + j + 1)
                    tt((QL, KL)[j][:], (TA, TB)[j][:], (QH, KH)[j][:].bitcast(f32), ALU.subtract)\
                        .then_inc(s["qk_lo"], 1)

                def probs(m):
                    w = key_rows(m % 8)[1] * GRID_W
                    dve.wait_ge(s["probs_done"], 16 * c + m + 1)
                    chain(dve_.reciprocal(ST[:, 2, m:m + 1], ST[:, 1, m:m + 1]))
                    chain.wait()
                    ts(SB[m % 2][:, 0:w], SB[m % 2][:, 0:w], ST[:, 2, m:m + 1], None, ALU.mult)\
                        .then_inc(s["probs_scaled"], 1)

                if c == 3:
                    chain(tt(LT[0][:], Y[:, 0, :], Y[:, 1, :], ALU.add))
                    chain.wait()
                    chain(tt(LT[0][:], LT[0][:], Y[:, 2, :], ALU.add))
                    chain.wait()
                    tt(LT[0][:], LT[0][:], Y[:, 3, :], ALU.add).then_inc(s["ln_in"], 1)
                else:
                    conv(2 if c == 0 else 8)
                evac(0, TA)
                if c < 3:
                    conv(6)
                else:
                    dve.wait_ge(s["ln_mean"], 1)
                    for m in range(4):
                        stt(Y[:, m, :], bank(6), -2.0, Y[:, m, :], ALU.mult, ALU.add).then_inc(s["ln_cent"], 1)
                head_refine(0)
                evac(1, TB)
                head_scale(0)
                if c == 3:
                    for m in range(1, 4):
                        dve.wait_ge(s["ln_sq"], m + 1)
                        if m > 1:
                            dve.wait_ge(s["ln_ssq"], m - 1)
                        tt(LT[0][:], LT[0][:], LT[m][:], ALU.add).then_inc(s["ln_ssq"], 1)
                head_lo(0)
                if c < 3:
                    conv(2 if c == 2 else 1)
                head_refine(1)
                head_scale(1)
                dve.wait_ge(s["qk_scaled"], 2 * c + 2)
                head_lo(1)
                evac(2, TC)
                for n in range(16):
                    h, rp = 2 * c + n // 8, n % 8
                    ks, nk = key_rows(rp)
                    w = nk * GRID_W
                    if rp == 0:
                        dve.wait_ge(s[f"bt_in{h % 2}"], 16 * (h // 2 + 1))
                        chain(dve_.tensor_copy(BI[:], BT[h % 2][:, 3:12, :]))
                        chain.wait()
                        chain(dve_.memset(BI[0:GRID_W, 8, :], MASKED))
                        chain(dve_.memset(BI[GRID_W:P, 0, :], MASKED))
                        chain.wait()
                    first = ks - 2 * rp + NA_ROWS - 1
                    bias = BI[:] if nk == 9 else BT[h % 2][:, first:first + nk, :]
                    dve.wait_ge(s["scores_done"], 16 * c + n + 1)
                    if n >= 2:
                        dve.wait_ge(s["pt_done"], 16 * c + n - 1)
                    dve_.tensor_tensor_reduce(
                        out=SB[n % 2][:, 0:w], in0=bank(2)[:, 0:w], in1=bias.rearrange("p r c -> p (r c)"),
                        scale=-1.0, scalar=3.0e38, op0=ALU.add, op1=ALU.min,
                        accum_out=ST[:, 0, n:n + 1]).then_inc(s["scores_max"], 1)
                    if c < 3:
                        conv(1)
                    elif n == 2:
                        dve.wait_ge(s["ln_y0"], 1)
                        refine(bank(0), LT[1][:], scale=2.0).then_inc(s["aux_free"], 1)
                        dve.wait_ge(s["aux_free"], 1)
                    elif 3 <= n < 7:
                        tt(Y[:, n - 3, :], Y[:, n - 3, :], LT[1][:], ALU.mult).then_inc(s["ln_norm"], 1)
                    elif n >= 9:
                        mix_lo(n - 9, MIX[n - 9], 0)
                    probs(n)
            mix_lo(7, OC[3][:], 0)

            for k in range(KD):
                dve.wait_ge(s["unit_done"], U_OUT + k + 1)
                dve.wait_ge(s[f"x_in{k // 2}"], 32)
                tt(X[:, k, :], bank(2 * (k % 4)), X[:, k, :], ALU.add).then_inc(s["bank_free"], 1)
                if 0 < k < KD - 1:
                    add_square()
            for k in range(KD):
                dve.wait_ge(s["split_hi"], KD + k + 1)
                lo(k, X[:, k, :], g("norm2", k))
                if k < 2:
                    add_square()
            scale_from(2)

            def ff_lo(i, u0, n_h, up, h0, target, ff_first=False, after=None, beside=None):
                per = up * G + G
                for n in range(n_h):
                    b = 4 * (n % 2) if up == 2 else 2 * (n % 4)
                    dve.wait_ge(s["unit_done"], i * per + (u0 + up * n + 1))
                    if not (ff_first and n == 0):
                        dve.wait_ge(s["ff_silu"], i * n_h + (h0 + n))
                        dve.wait_ge(s["ff_lo"], i * n_h + (h0 + n))
                    if up == 2:
                        tt(TA[:], bank(b), RS[:], ALU.mult).then_inc(s["bank_free"], 1)
                        dve.wait_ge(s["bank_free"], i * per + (u0 + up * n + 1))
                        dve.wait_ge(s["unit_done"], i * per + (u0 + up * n + 2))
                        tt(TC[:], bank(b + 2), RS[:], ALU.mult).then_inc(s["bank_free"], 1)
                        dve.wait_ge(s["bank_free"], i * per + (u0 + up * n + 2))
                        dve.wait_ge(s["ff_silu"], i * n_h + (h0 + n + 1))
                        tt(TC[:], TC[:], TB[:], ALU.mult).then_inc(s["ff_h"], 1)
                        dve.wait_ge(s["ff_h"], i * n_h + (h0 + n + 1))
                        src = TC
                    else:
                        stt(TA[:], bank(b), 0.0, RS[:], ALU.max, ALU.mult).then_inc(s["bank_free"], 1)
                        dve.wait_ge(s["bank_free"], i * per + (u0 + up * n + 1))
                        dve.wait_ge(s["ff_silu"], i * n_h + (h0 + n + 1))
                        src = TB
                    dve.wait_ge(s["ff_hi"], i * n_h + (h0 + n + 1))
                    tt(HL[:, n, :], src[:], HH[:, n, :].bitcast(f32), ALU.subtract).then_inc(s["ff_lo"], 1)
                for m in range(4):
                    dve.wait_ge(s["unit_done"], i * per + (u0 + up * n_h + m + 1))
                    for c in range(2):
                        dst = target[:, 2 * m + c, :]
                        src = bank(4 * (m % 2) + 2 * c)
                        if after == "fill":
                            ins = dve_.tensor_copy(dst, src)
                        else:
                            ins = tt(dst, src, dst, ALU.add)
                        if c == 0:
                            ins.then_inc(s["ff_acc"], 1)
                        else:
                            ins.then_inc(s["bank_free"], 1)
                    if beside:
                        beside(m)

            def tail_lo(m):
                if m:
                    add_square()
                for k in (2 * m, 2 * m + 1):
                    dve.wait_ge(s["split_hi"], 2 * KD + k + 1)
                    lo(k, X[:, k, :], g("g_mix_pre", k))
                add_square()

            ff_lo(0, U_FF, G, 2, 0, X, ff_first=True)
            with dve.Fori(1, NG1) as i:
                dve.wait_ge(s["bank_free"], i * (3 * G) + U_FF)
                dve.wait_ge(s["ff_acc"], i * 4)
                ff_lo(i, U_FF, G, 2, 0, X)
            dve.wait_ge(s["bank_free"], U_TAIL)
            dve.wait_ge(s["ff_acc"], NG1 * 4)
            ff_lo(0, U_TAIL, TAIL, 2, NG1 * G, X, beside=tail_lo)
            add_square()
            scale_from(3)

            for j in range(4):
                dve.wait_ge(s["unit_done"], U_POOL + j + 1)
                tt(UB[:, j, :], bank(2 * (j % 4)), RS[:], ALU.mult).then_inc(s["bank_free"], 1)
                dve.wait_ge(s["bank_free"], U_POOL + j + 1)
            for j, w in enumerate(WINDOWS):
                src, bufs, step = UB[:, j, :], [TA[:], TB[:]], 1
                while step < w:
                    dst = bufs[0]
                    chain(dve_.tensor_copy(dst[:, 0:step], src[:, 0:step]))
                    chain(tt(dst[:, step:], src[:, step:], src[:, 0:T - step], ALU.add))
                    chain.wait()
                    src, bufs, step = dst, bufs[::-1], 2 * step
                for t in range(w - 1):
                    chain(ts(src[:, t:t + 1], src[:, t:t + 1], float(w) / (t + 1), None, ALU.mult))
                chain.wait()
                stt(UB[:, j, :], src, 1.0 / w, UB[:, j, :], ALU.mult, ALU.subtract).then_inc(s["pool_d"], 1)
                dve.wait_ge(s["pool_d"], j + 1)
            for j in range(4):
                dve.wait_ge(s["pool_y"], j + 1)
                ts(UB[:, j, :], bank(6), g("pool_scale", j), None, ALU.mult).then_inc(s["pool_done"], 1)

            tiles = sb_tiles()
            for c in range(4):
                u = U_QKV2 + 3 * c

                def evac2(j, t):
                    dve.wait_ge(s["unit_done"], u + j + 1)
                    stt(t[:], bank(2 * ((u + j) % 2)), DH ** -0.5 if j == 0 else 1.0, RS[:],
                        ALU.mult, ALU.mult).then_inc(s["bank_free"], 1)
                    dve.wait_ge(s["bank_free"], u + j + 1)
                for j in range(2):
                    evac2(j, (TA, TB)[j])
                    dve.wait_ge(s["q2_hi"], 2 * c + j + 1)
                    tt((QL, KL)[j][:], (TA, TB)[j][:], (QH, KH)[j][:].bitcast(f32), ALU.subtract)\
                        .then_inc(s["q2_lo"], 1)
                evac2(2, TC)
                dve.wait_ge(s["q2_lo"], 2 * c + 2)
                for n in range(len(tiles)):
                    h, half, b, l0, w = tiles[n]
                    N = c * len(tiles) + n
                    sp_ = SP_[n % 2]
                    dve.wait_ge(s["sb_lse"], N + 1)
                    if n >= 2:
                        dve.wait_ge(s["sb_cum"], N - 1)
                    if b < 4 * half + 3:
                        top, pl = tiles[n - 1][2] == 4 * half + 3, tiles[n - 1][3]
                        before = SP_[(n - 1) % 2][:, pl:]
                        run, run0 = RUN[n % 2], RUN[(n - 1) % 2]
                        if pl > l0:
                            chain(dve_.memset(run[:, l0:pl], 0.0))
                        if top:
                            chain(dve_.tensor_copy(run[:, pl:], before))
                        else:
                            chain(tt(run[:, pl:], run0[:, pl:], before, ALU.add))
                        chain.wait()
                    softplus = stt(sp_[:, l0:], PS[:, n % 4, l0:], 0.0, EX[n % 2][:, l0:], ALU.max, ALU.add)
                    if b * P >= half * H2:
                        chain(softplus)
                        chain.wait()
                        softplus = tt(sp_[:, l0:l0 + P], sp_[:, l0:l0 + P], KEEP[:], ALU.mult)
                    softplus.then_inc(s["sb_sp"], 1)
                    dve.wait_ge(s["sb_sp"], N + 1)
                dve.wait_ge(s["sb_o0"], c + 1)
                chain(refine(bank(4), TB[:]))
                chain.wait()
                stt(OB[c][:], OB[c][:], g("g_sb", c), TB[:], ALU.mult, ALU.mult).then_inc(s["sb_on"], 1)
                dve.wait_ge(s["sb_on"], c + 1)

            for k in range(KD):
                mix_lo(k, UB[:, k, :] if k < 4 else OB[k - 4][:], 8)
            dve.wait_ge(s["mix_lo"], 16)
            for k in range(KD):
                dve.wait_ge(s["unit_done"], U_OUT2 + k + 1)
                dve_.tensor_copy(MM[:, k, :], bank(2 * (k % 4))).then_inc(s["bank_free"], 1)
                if k:
                    add_square()
            add_square()

            scale_from(4)
            for k in range(KD):
                if k == 0:
                    chain(tt(MM[:, 0, :], MM[:, 0, :], RS[:], ALU.mult))
                    chain.wait()
                else:
                    dve.wait_ge(s["post_scaled"], k)
                stt(X[:, k, :], MM[:, k, :], g("g_mix_post", k), X[:, k, :], ALU.mult, ALU.add)\
                    .then_inc(s["post_x"], 1)
                if k:
                    dve.wait_ge(s["split_hi"], 3 * KD + k)
                    lo(k - 1, X[:, k - 1, :], g("g_mlp_pre", k - 1))
                if k > 1:
                    add_square()
            dve.wait_ge(s["split_hi"], 4 * KD)
            lo(KD - 1, X[:, KD - 1, :], g("g_mlp_pre", KD - 1))
            add_square()
            add_square()
            scale_from(5)
            h0 = NG1 * G + TAIL
            ff_lo(0, U_MLP, G, 1, h0, MM, after="fill")
            with dve.Fori(1, NG2 - 1) as i:
                dve.wait_ge(s["bank_free"], i * (2 * G) + U_MLP)
                dve.wait_ge(s["ff_acc"], i * 4 + 4 * (NG1 + 1))
                ff_lo(i, U_MLP, G, 1, h0, MM)

            def p_and_squares(m):
                if m == 0:
                    for k in range(2):
                        dve.wait_ge(s["ple_hi"], k + 1)
                        tt(PPL[:, k, :], PPF[:, k, :], PPH[:, k, :].bitcast(f32), ALU.subtract)\
                            .then_inc(s["ple_lo"], 1)
                add_square()
                if m:
                    add_square()
            dve.wait_ge(s["bank_free"], (NG2 - 1) * (2 * G) + U_MLP)
            dve.wait_ge(s["ff_acc"], (NG2 - 1) * 4 + 4 * (NG1 + 1))
            ff_lo(NG2 - 1, U_MLP, G, 1, h0, MM, beside=p_and_squares)
            add_square()
            scale_from(6)
            for k in range(KD):
                chain(stt(MM[:, k, :], MM[:, k, :], g("g_mlp_post", k), RS[:], ALU.mult, ALU.mult))
                chain.wait()
                tt(X[:, k, :], X[:, k, :], MM[:, k, :], ALU.add).then_inc(s["post_x"], 1)
                dve.wait_ge(s["post_x"], KD + k + 1)
                if k:
                    dve.wait_ge(s["split_hi"], 4 * KD + k)
                    tt(GL[:, k - 1, :], X[:, k - 1, :], INL[:, k - 1, :].bitcast(f32), ALU.subtract)\
                        .then_inc(s["split_lo"], 1)
            dve.wait_ge(s["split_hi"], 5 * KD)
            tt(GL[:, KD - 1, :], X[:, KD - 1, :], INL[:, KD - 1, :].bitcast(f32), ALU.subtract)\
                .then_inc(s["split_lo"], 1)
            for k in range(KD):
                add_square()
            scale_from(7)
            for k in range(KD):
                chain(stt(EMB[:, k, :], EMB[:, k, :], g("g_ple", k), RS[:], ALU.mult, ALU.mult))
            chain.wait()
            for k in range(KD):
                dve.wait_ge(s["bank_free"], U_PLEG + k + 1)
                t = (TA, TB)[k % 2]
                chain(tt(t[:], t[:], EMB[:, k, :], ALU.mult))
                chain.wait()
                tt(X[:, k, :], X[:, k, :], t[:], ALU.add).then_inc(s["ple_out"], 1)


def units(w, k_chunks, cols):
    k, n = w.shape
    w = w.reshape(k // (P * k_chunks), k_chunks, P, n // cols, cols)
    return w.transpose(0, 3, 2, 1, 4).reshape(-1, P, k_chunks * cols)


def columns(*vectors):
    import numpy as np
    return np.concatenate([v.reshape(-1, P).T for v in vectors], axis=1)


def kernel(x, norm1_g, w_in, q_norm_g, k_norm_g, rpb, dw_kernel, dw_bias, conv_ln_g, conv_ln_b, w_out,
           norm2_g, w_gate, w_up, w_down, p_2, g_mix_pre_2, w_in_2, w_pool_2, pool_scale_2, g_sb_2,
           w_out_2, g_mix_post_2, g_mlp_pre_2, w_up_2, w_down_2, g_mlp_post_2, w_ple_gate_2,
           w_ple_proj_2, g_ple_2):
    import numpy as np
    import concourse.bacc as bacc
    from concourse.bass_utils import run_bass_kernel_spmd

    def interleave(*ws):
        return np.stack(ws, axis=1).reshape(-1, *ws[0].shape[1:])

    def chunks(a):
        return a.T.reshape(-1, P, T).transpose(1, 0, 2)

    w = units(w_in[0], KD, P)
    main = NG1 * G
    ffu = interleave(units(w_gate[0], KD, P), units(w_up[0], KD, P))
    w2 = units(w_in_2[0], KD, P)
    arrays = {
        "x": chunks(x[0]),
        "w_glu": interleave(w[4:8], w[0:4]),
        "w_qkv": interleave(w[8:12], w[12:16], w[16:20]),
        "w_out": units(w_out[0], KD, P),
        "w_ff": ffu[:2 * main],
        "w_ffd": units(w_down[0][:main * P], G, 2 * P),
        "w_tail": ffu[2 * main:],
        "w_taild": units(w_down[0][main * P:], TAIL, 2 * P),
        "gains": columns(norm1_g[0], norm2_g[0], g_mix_pre_2[0], g_mix_post_2[0], g_mlp_pre_2[0],
                         g_mlp_post_2[0], g_ple_2[0], np.concatenate([q_norm_g[0], q_norm_g[0]]),
                         np.concatenate([k_norm_g[0], k_norm_g[0]]), dw_bias[0], conv_ln_g[0],
                         conv_ln_b[0], pool_scale_2[0], g_sb_2[0]),
        "taps": dw_kernel[0].T.reshape(4, P, TAPS).transpose(1, 0, 2),
        "rpb": rpb[0],
        "p_t": p_2[0, 0].T.reshape(2, P, T).transpose(1, 0, 2),
        "w_in2": np.concatenate([w2[0:4], interleave(w2[4:8], w2[8:12], w2[12:16])]),
        "w_pool": w_pool_2[0].transpose(1, 0, 2),
        "w_out2": units(w_out_2[0], KD, P),
        "w_mlp": units(w_up_2[0], KD, P),
        "w_mlpd": units(w_down_2[0], G, 2 * P),
        "w_plep": units(w_ple_proj_2[0], 2, 2 * P),
        "w_pleg": units(w_ple_gate_2[0], KD, P),
    }
    nc = bacc.Bacc("TRN2", target_bir_lowering=False, num_devices=1)
    aps = {}
    for name, a in arrays.items():
        arrays[name] = a = np.ascontiguousarray(a)
        aps[name] = nc.dram_tensor(name, a.shape, mybir.dt.from_np(a.dtype), kind="ExternalInput").ap()
    aps["out"] = nc.dram_tensor("out", (P, KD, T), mybir.dt.float32, kind="ExternalOutput").ap()
    program(nc, **aps)
    r = run_bass_kernel_spmd(nc, [arrays], core_ids=[0])
    got = r.results[0]["out"]
    return np.ascontiguousarray(got.transpose(2, 1, 0).reshape(1, T, D))
```

```python
import concourse.bass as bass
from concourse import mybir
from contextlib import ExitStack

T = 1024
D = 1024
P = 128
KD = D // P
H2 = T // 2
EPS = 1e-6
GRID_W, ROWS, NA_ROWS, NA_COLS = 64, 16, 8, 16
HEADS, DH = 8, 64
TAPS = 31
PADT = TAPS // 2
FF1, FF2 = 2816, 4096
G = 4
NG1, TAIL = FF1 // P // G, FF1 // P % G
NG2 = FF2 // P // G
MASKED = -1.0e30
WINDOWS = (2, 4, 8, 16)

U_GLU = 0
U_QKV = U_GLU + 8
U_OUT = U_QKV + 12
U_FF = U_OUT + 8
U_TAIL = U_FF + NG1 * 3 * G
U_POOL = U_TAIL + 2 * TAIL + 4
U_QKV2 = U_POOL + 4
U_OUT2 = U_QKV2 + 12
U_MLP = U_OUT2 + 8
U_PLEP = U_MLP + NG2 * 2 * G
U_PLEG = U_PLEP + 4
U_END = U_PLEG + 8


class Chain:

    def __init__(self, eng, sem):
        self.eng, self.sem, self.base, self.local, self.i, self.per = eng, sem, 0, 0, None, 0

    def __call__(self, ins):
        ins.then_inc(self.sem, 1)
        self.local += 1
        return self.local

    def wait(self, mark=None):
        mark = self.local if mark is None else mark
        value = self.base + mark
        self.eng.wait_ge(self.sem, value if self.i is None else self.i * self.per + value)

    def enter(self, i, per):
        self.base, self.local, self.i, self.per = self.base + self.local, 0, i, per

    def leave(self, turns):
        assert self.local == self.per, (self.local, self.per)
        self.base, self.local, self.i = self.base + turns * self.per, 0, None


def key_rows(rp):
    first = [min(max(r - NA_ROWS // 2, 0), ROWS - NA_ROWS) for r in (2 * rp, 2 * rp + 1)]
    return first[0], first[1] + NA_ROWS - first[0]


def sb_tiles():
    out = []
    for h in range(2):
        for half in range(2):
            for b in range(4 * half + 3, -1, -1):
                lo = max(0, b * P - half * H2)
                out.append((h, half, b, lo, H2 - lo))
    return out


def runs_to(tiles, n):
    return sum(b != 4 * half + 3 for _, half, b, _, _ in tiles[:n + 1])


GAINS = (("norm1", 8), ("norm2", 8), ("g_mix_pre", 8), ("g_mix_post", 8), ("g_mlp_pre", 8),
         ("g_mlp_post", 8), ("g_ple", 8), ("q_g", 1), ("k_g", 1), ("dw_bias", 4), ("ln_g", 4),
         ("ln_b", 4), ("pool_scale", 4), ("g_sb", 4))


def up32(n):
    return -(-n // 32) * 32


def gains_at():
    at, out = 0, {}
    for name, n in GAINS:
        out[name] = at
        at += n
    return out


def program(nc, x, w_glu, w_qkv, w_out, w_ff, w_ffd, w_tail, w_taild, gains, taps, rpb,
            p_t, w_in2, w_pool, w_out2, w_mlp, w_mlpd, w_plep, w_pleg, out):
    f32, f32r = mybir.dt.float32, mybir.dt.float32r
    ALU, ACT = mybir.AluOpType, mybir.ActivationFunctionType

    ctx = ExitStack()
    with ctx:
        base = 16512

        def at(name, shape, offset, dt=f32):
            return nc.alloc_sbuf_tensor_at(name, shape, dt, offset=base + offset)

        def sem(name):
            return ctx.enter_context(nc.semaphore(name))

        KB32 = 4 * KD * T
        X = at("residual", [P, KD, T], 0)
        INH = at("input_hi", [P, KD, T], KB32, f32r)
        INL = at("input_lo", [P, KD, T], 2 * KB32, f32r)
        QK0 = 3 * KB32
        R2 = 4 * KB32
        W0 = 5 * KB32
        RAW = at("weight_raw", [P, 2, 1024], W0)
        WH = at("weight_hi", [P, 2, 1024], W0 + 8192, f32r)
        WL = at("weight_lo", [P, 2, 1024], W0 + 16384, f32r)
        S0 = W0 + 24576
        RS = at("token_scale", [P, T], S0)
        SQ = at("squares", [P, T], S0 + 4096)
        TA = at("work_a", [P, T], S0 + 8192)
        TB = at("work_b", [P, T], S0 + 12288)
        TC = at("work_c", [P, T], S0 + 16384)
        C0 = S0 + 20480
        IDENT = at("identity", [P, P], C0)
        MEAN = at("mean_all", [P, P], C0 + 512)
        MEANH = at("mean_head", [P, P], C0 + 1024)
        NGAIN = gains.shape[1]
        GN = at("gains_sb", [P, NGAIN], C0 + 1536)
        TP = at("taps_sb", [P, 4, TAPS], C0 + 1536 + up32(4 * NGAIN))
        C1 = C0 + 1536 + up32(4 * NGAIN) + up32(16 * TAPS)
        EPSC = at("eps_col", [P, 1], C1)
        ZERO = at("zero_col", [P, 1], C1 + 64)
        GS = at("qk_gain", [P, 2], C1 + 32)
        UP = at("glu_padded", [P, 4, T + 2 * PADT], 0)
        UW = 4 * (T + 2 * PADT)
        U4 = up32(4 * UW)
        BT = [at(f"bias_table{i}", [P, 16, GRID_W], U4 + 4096 * i) for i in range(2)]
        BI = at("bias_inner", [P, 9, GRID_W], U4 + 8192)
        SB = [at(f"scores{i}", [P, 9 * GRID_W], U4 + 8192 + 2304 * (i + 1)) for i in range(2)]
        ST = at("softmax_stats", [P, 3, 16], U4 + 8192 + 3 * 2304)
        OC = [at(f"attn_out{c}", [P, T], up32(c * UW)) for c in range(4)]
        QH, QL, KH, KL = (at(n, [P, T], QK0 + 4096 * i, f32r)
                          for i, n in enumerate(("q_hi", "q_lo", "k_hi", "k_lo")))
        V = at("v_tokens", [P, 8, P], QK0 + 16384)
        PT = [at(f"probs_t{i}", [P, 5, P], QK0 + 20480 + 2560 * i) for i in range(2)]
        Y = at("conv_out", [P, 4, T], R2)
        NEG = at("masked_tile", [P, T], R2 + 16384)
        LT = [at(f"ln_work{c}", [P, T], R2 + 16384 + 4096 * c) for c in range(4)]
        HH = at("hidden_hi", [P, G, T], R2, f32r)
        HL = at("hidden_lo", [P, G, T], R2 + 16384, f32r)
        UB = at("pool_u", [P, 4, T], R2)
        OB = [at(f"sb_out{c}", [P, T], QK0 + 16384 + 4096 * c) for c in range(4)]
        V2 = at("v2_tokens", [P, 8, P], R2 + 16384)
        NTRI = at("minus_tri", [P, P], R2 + 20480)
        NONE = at("minus_ones", [P, P], R2 + 20992)
        NMASK = at("diag_masked", [P, P], R2 + 21504)
        KEEP = at("diag_keep", [P, P], R2 + 22016)
        WP = at("w_pool_sb", [P, 4, P], R2 + 22528)
        EX = [at(f"sb_e{i}", [P, H2], R2 + 24576 + 2048 * i) for i in range(2)]
        SPH = [at(f"sb_softplus_hi{i}", [P, H2], R2 + 28672 + 2048 * i, f32r) for i in range(2)]
        SPL = [at(f"sb_softplus_lo{i}", [P, H2], S0 + 12288 + 2048 * i, f32r) for i in range(2)]
        NTRIR = at("minus_tri_r", [P, P], C1 + 96, f32r)
        RUN = [at(f"sb_running{i}", [P, H2], o) for i, o in enumerate((S0 + 4096, R2 + 22528))]
        AW = [at("sb_weights0", [P, H2], S0 + 6144), TA[:, 0:H2]]
        MM = at("branch_out", [P, KD, T], QK0)
        PPH = at("ple_in_hi", [P, 2, T], 2 * KB32, f32r)
        PPL = at("ple_in_lo", [P, 2, T], 2 * KB32 + 8192, f32r)
        GL = at("gate_lo", [P, KD, T], QK0, f32r)
        EMB = at("embedding", [P, KD, T], KB32)
        GT = at("gate_out", [P, KD, T], R2)
        PPF = at("ple_in", [P, 2, T], 2 * KB32 + 16384)

        PS = ctx.enter_context(nc.psum_tensor("ps", [P, 8, H2], f32))

        def bank(b, n=2):
            return PS[:, b:b + n, :].rearrange("p b t -> p (b t)")

        names = """w_loaded0 w_loaded1 w_hi w_split unit_done bank_free consts_ready gains_in x_in0 x_in1
            x_in2 x_in3 split_hi split_lo sq_ready sq_added mean_done ln_exp scale_ready glu_sig
            qk_sq norm_sum qk_y0 qk_scaled qk_hi qk_lo v_tr v_ready neg_ready neg_out table_out
            bt_in0 bt_in1 scores_done scores_max probs_done probs_scaled pt_done pt_sb pv_done
            conv_out_done attn_out_done ln_in ln_mean ln_cent ln_sq ln_ssq ln_var ln_y0 ln_norm
            ln_silu mix_hi mix_lo aux_free ff_silu ff_h ff_hi ff_lo ff_acc act_chain dve_chain
            pool_chain sb_const sb_z sb_lse sb_sp sb_cum sb_exp sb_pv sb_osq sb_osum sb_o0 sb_on
            pool_d pool_y pool_done q2_hi q2_lo v2_tr v2_ready pool_w_in post_x ple_p_in ple_hi
            ple_lo ple_out stored post_scaled x_first sb_soft sb_run""".split()
        s = {n: sem(n) for n in names}
        block = ctx.enter_context(nc.Block())
        pool_, act_, dve_ = nc.gpsimd, nc.scalar, nc.vector
        g_of = gains_at()
        RUNS = runs_to(sb_tiles(), len(sb_tiles()))

        def g(name, k=0):
            return GN[:, g_of[name] + k:g_of[name] + k + 1]

        BD = nc.dram_tensor("bias_tables", [HEADS, P, 16 * GRID_W], f32).ap()
        N_TABLE_DMAS = 2 * (HEADS + NA_COLS - 1)

        @block.sync
        def _(sp):
            def load_unit(u, slot, src, width=1024):
                if not isinstance(u, int) or u >= 2:
                    sp.wait_ge(s["w_split"], u - 1)
                sp.dma_start(RAW[:, slot, 0:width], src).then_inc(s[f"w_loaded{slot}"], 16)

            def load_units(u0, w, n, width=1024):
                with sp.Fori(0, n // 2) as i:
                    for slot in range(2):
                        load_unit(i * 2 + u0 + slot, slot, w[bass.ds(i * 2 + slot, 1), :, :]
                                  .rearrange("u p n -> (u p) n"), width)

            load_unit(0, 0, w_glu[0])
            sp.dma_start(GN[:], gains).then_inc(s["gains_in"], 16)
            sp.dma_start(TP[:], taps).then_inc(s["gains_in"], 16)
            sp.dma_start(X[:, 0, :], x[:, 0, :]).then_inc(s["x_first"], 16)
            load_unit(1, 1, w_glu[1])
            sp.dma_start(X[:, 1, :], x[:, 1, :]).then_inc(s["x_in0"], 16)
            for k in range(1, 4):
                sp.dma_start(X[:, 2 * k:2 * k + 2, :], x[:, 2 * k:2 * k + 2, :]).then_inc(s[f"x_in{k}"], 16)
            for u in range(2, 8):
                load_unit(u, u % 2, w_glu[u])
            for c in range(4):
                for j in range(3):
                    u = U_QKV + 3 * c + j
                    load_unit(u, u % 2, w_qkv[3 * c + j])
                for h in (2 * c, 2 * c + 1):
                    if h >= 2:
                        sp.wait_ge(s["scores_max"], 8 * (h - 1))
                    sp.wait_ge(s["scale_ready"], 1)
                    sp.wait_ge(s["table_out"], 16 * N_TABLE_DMAS)
                    sp.dma_start(BT[h % 2][:], BD[h]).then_inc(s[f"bt_in{h % 2}"], 16)
            for j in range(2):
                load_unit(U_OUT + j, j % 2, w_out[j])
            sp.wait_ge(s["mix_lo"], 8)
            for k in range(4):
                sp.dma_start(X[:, 2 * k:2 * k + 2, :], x[:, 2 * k:2 * k + 2, :]).then_inc(s[f"x_in{k}"], 16)
            for j in range(2, 8):
                load_unit(U_OUT + j, j % 2, w_out[j])
            with sp.Fori(0, NG1) as i:
                for j in range(2 * G):
                    load_unit(i * (3 * G) + (U_FF + j), j % 2,
                              w_ff[bass.ds(i * (2 * G) + j, 1), :, :].rearrange("u p n -> (u p) n"))
                for j in range(G):
                    load_unit(i * (3 * G) + (U_FF + 2 * G + j), j % 2,
                              w_ffd[bass.ds(i * G + j, 1), :, :].rearrange("u p n -> (u p) n"))
            for j in range(2 * TAIL):
                load_unit(U_TAIL + j, j % 2, w_tail[j])
            for j in range(4):
                load_unit(U_TAIL + 2 * TAIL + j, j % 2, w_taild[j], TAIL * 256)
            for j in range(16):
                load_unit(U_POOL + j, j % 2, w_in2[j])
                if j == 1:
                    sp.wait_ge(s["unit_done"], U_POOL)
                    sp.dma_start(WP[:], w_pool).then_inc(s["pool_w_in"], 16)
            load_units(U_OUT2, w_out2, 8)
            with sp.Fori(0, NG2) as i:
                for j in range(G):
                    load_unit(i * (2 * G) + (U_MLP + j), j % 2,
                              w_mlp[bass.ds(i * G + j, 1), :, :].rearrange("u p n -> (u p) n"))
                for j in range(G):
                    load_unit(i * (2 * G) + (U_MLP + G + j), j % 2,
                              w_mlpd[bass.ds(i * G + j, 1), :, :].rearrange("u p n -> (u p) n"))
            sp.wait_ge(s["unit_done"], U_PLEP - 4)
            sp.dma_start(PPF[:], p_t).then_inc(s["ple_p_in"], 16)
            for j in range(4):
                load_unit(U_PLEP + j, j % 2, w_plep[j], 512)
            for j in range(8):
                load_unit(U_PLEG + j, j % 2, w_pleg[j])
            for k in range(KD):
                sp.wait_ge(s["ple_out"], k + 1)
                sp.dma_start(out[:, k, :], X[:, k, :]).then_inc(s["stored"], 16)
            sp.wait_ge(s["stored"], 16 * KD)

        @block.gpsimd
        def _(pool):
            pool_.memset(NEG[:], MASKED).then_inc(s["neg_ready"], 1)
            chain = Chain(pool, s["pool_chain"])
            chain(pool_.memset(EPSC[:, 0:1], EPS))
            chain(pool_.memset(ZERO[:], 0.0))
            chain(pool_.memset(IDENT[:], 0.0))
            chain(pool_.memset(MEAN[:], 1.0 / D))
            chain(pool_.memset(MEANH[:], 1.0 / DH))
            chain.wait()
            chain(pool_.affine_select(out=IDENT[:], in_=IDENT[:], compare_op=ALU.not_equal, fill=1.0,
                                      base=0, pattern=[[-1, P]], channel_multiplier=1))
            chain.wait()
            chain(pool_.memset(MEANH[0:DH, DH:P], 0.0))
            chain.wait()
            pool_.memset(MEANH[DH:P, 0:DH], 0.0).then_inc(s["consts_ready"], 1)
            pool.wait_ge(s["consts_ready"], 1)

            def split(u, slot, turn, width=1024):
                pool.wait_ge(s[f"w_loaded{slot}"], turn)
                if not isinstance(u, int) or u >= 2:
                    pool.wait_ge(s["unit_done"], u - 1)
                raw = RAW[:, slot, 0:width]
                pool_.tensor_tensor(WH[:, slot, 0:width], raw, ZERO[:].to_broadcast([P, width]), ALU.add).then_inc(s["w_hi"], 1)
                pool.wait_ge(s["w_hi"], u + 1)
                pool_.tensor_tensor(WL[:, slot, 0:width], raw, WH[:, slot, 0:width].bitcast(f32),
                                    ALU.subtract).then_inc(s["w_split"], 1)

            def splits(u0, n, width=1024):
                with pool.Fori(0, n // 2) as i:
                    for slot in range(2):
                        split(i * 2 + (u0 + slot), slot, i * 16 + 8 * u0 + 16, width)

            pool.wait_ge(s["w_split"], 1)
            split(1, 1, 16)
            splits(2, U_TAIL + 2 * TAIL - 2)
            splits(U_TAIL + 2 * TAIL, 4, TAIL * 256)
            splits(U_POOL, 2)
            pool.wait_ge(s["unit_done"], U_POOL)
            chain(pool_.memset(NTRI[:], -1.0))
            chain(pool_.memset(NMASK[:], 0.0))
            chain(pool_.memset(KEEP[:], 1.0))
            chain(pool_.memset(NONE[:], -1.0))
            chain.wait()
            chain(pool_.affine_select(out=NTRI[:], in_=NTRI[:], compare_op=ALU.is_ge, fill=0.0,
                                      base=0, pattern=[[-1, P]], channel_multiplier=1))
            chain(pool_.affine_select(out=NMASK[:], in_=NMASK[:], compare_op=ALU.is_ge, fill=MASKED,
                                      base=-1, pattern=[[1, P]], channel_multiplier=-1))
            chain(pool_.affine_select(out=KEEP[:], in_=KEEP[:], compare_op=ALU.is_ge, fill=0.0,
                                      base=-1, pattern=[[1, P]], channel_multiplier=-1))
            chain.wait()
            pool_.tensor_tensor(NTRIR[:], NTRI[:], ZERO[:].to_broadcast([P, P]), ALU.add).then_inc(s["sb_const"], 1)
            splits(U_POOL + 2, U_QKV2 - U_POOL - 2)
            tiles = sb_tiles()
            for c in range(4):
                u = U_QKV2 + 3 * c
                for v in range(u if c == 0 else u + 2, min(u + 5, U_OUT2 + 2)):
                    split(v, v % 2, 8 * (v - v % 2) + 16)
                for n, (h, half, b, l0, w) in enumerate(tiles):
                    if b == 4 * half + 3:
                        continue
                    N = c * len(tiles) + n
                    pool.wait_ge(s["sb_soft"], N)
                    if n >= 2:
                        pool.wait_ge(s["sb_cum"], N - 1)
                    top, pl = tiles[n - 1][2] == 4 * half + 3, tiles[n - 1][3]
                    before = EX[(n - 1) % 2][:, pl:]
                    run, run0 = RUN[n % 2], RUN[(n - 1) % 2]
                    if pl > l0:
                        chain(pool_.memset(run[:, l0:pl], 0.0))
                    if not top:
                        pool.wait_ge(s["sb_run"], c * RUNS + runs_to(tiles, n - 1))
                    chain.wait()
                    pool_.tensor_tensor(run[:, pl:], ZERO[:].to_broadcast([P, H2 - pl]) if top else run0[:, pl:],
                                        before, ALU.add).then_inc(s["sb_run"], 1)
            splits(U_OUT2 + 2, U_MLP - U_OUT2)
            pool.wait_ge(s["scale_ready"], 4)
            for k in range(1, KD):
                pool_.tensor_tensor(MM[:, k, :], MM[:, k, :], RS[:], ALU.mult).then_inc(s["post_scaled"], 1)
            splits(U_MLP + 2, U_PLEP - U_MLP - 2)
            splits(U_PLEP, 4, 512)
            splits(U_PLEG, 2)

            def add_square(k):
                pool.wait_ge(s["sq_ready"], 6 * KD + k + 1)
                pool.wait_ge(s["sq_added"], 6 * KD + k)
                pool_.tensor_tensor(SQ[:], (TA, TB)[k % 2][:], SQ[:] if k else ZERO[:].to_broadcast([P, T]),
                                    ALU.add).then_inc(s["sq_added"], 1)
            pool.wait_ge(s["mean_done"], 2 * 6)
            for k in range(KD - 2):
                add_square(k)
            split(U_PLEG + 2, 0, 8 * (U_PLEG + 2) + 16)
            for k in range(KD - 2, KD):
                add_square(k)
            split(U_PLEG + 3, 1, 8 * (U_PLEG + 2) + 16)
            splits(U_PLEG + 4, 4)

        Q_BESIDE = (0, 1, 4, 12, 13, 16, 23)

        @block.tensor
        def _(pe):
            mm = nc.tensor.matmul

            def unit(u, slot, b, kc=8, nc_=1, inh=INH, inl=INL, k_ready=None):
                pe.wait_ge(s["w_split"], u + 1)
                for k in range(kc):
                    if k_ready:
                        k_ready(k)
                    last = chunk(slot, b, k, kc, nc_, inh, inl)
                last.then_inc(s["unit_done"], 1)

            def chunk(slot, b, k, kc=8, nc_=1, inh=INH, inl=INL):
                n = P * nc_
                for step, (w, a) in enumerate(((WH, inh), (WH, inl), (WL, inh))):
                    for c in range(nc_):
                        for h in range(2):
                            last = mm(PS[:, b + 2 * c + h, :],
                                      w[:, slot, k * n + P * c:k * n + P * (c + 1)],
                                      a[:, k, h * H2:(h + 1) * H2],
                                      start=(k == 0 and step == 0),
                                      stop=(k == kc - 1 and step == 2))
                return last

            def first_two(u, k_ready, inh=INH, inl=INL):
                order = [(j, k) for k in range(6) for j in range(2)] + [(0, 6), (0, 7), (1, 6), (1, 7)]
                for j, k in order:
                    if k == 0:
                        pe.wait_ge(s["w_split"], u + j + 1)
                    if j == 0:
                        k_ready(k)
                    last = chunk(j, 2 * j, k, inh=inh, inl=inl)
                    if k == KD - 1:
                        last.then_inc(s["unit_done"], 1)

            def mean(mat, src, b, signal):
                for h in range(2):
                    mm(PS[:, b + h, :], mat[:], src[:, h * H2:(h + 1) * H2], start=True, stop=True)\
                        .then_inc(s[signal], 1)

            def inputs(hi0, lo0):
                def ready(k):
                    pe.wait_ge(s["split_hi"], hi0 + k + 1)
                    pe.wait_ge(s["split_lo"], lo0 + k + 1)
                return ready

            pe.wait_ge(s["consts_ready"], 1)
            first_two(0, inputs(0, 0))
            for u in range(2, 8):
                if u == 2:
                    pe.wait_ge(s["sq_added"], KD)
                    mean(MEAN, SQ, 6, "mean_done")
                if u == 3:
                    pe.wait_ge(s["scale_ready"], 1)
                if u >= 4:
                    pe.wait_ge(s["bank_free"], u - 3)
                unit(u, u % 2, 2 * (u % 4))

            for c in range(4):
                u = U_QKV + 3 * c
                pe.wait_ge(s["bank_free"], u if c else 5)
                if c:
                    pe.wait_ge(s["scores_max"], 16 * c)
                unit(u, u % 2, 2 * (u % 2))
                if c == 3:
                    pe.wait_ge(s["attn_out_done"], 3)
                    pe.wait_ge(s["ln_in"], 1)
                    mean(MEAN, LT[0], 6, "ln_mean")

                def head_sum(j):
                    def at_chunk(k):
                        if k == 3 - 2 * j:
                            pe.wait_ge(s["qk_sq"], 2 * c + j + 1)
                            if c == 3 and j:
                                pe.wait_ge(s["ln_cent"], 4)
                            if c and j:
                                pe.wait_ge(s["attn_out_done"], c)
                            elif c:
                                pe.wait_ge(s["pt_sb"], 16 * c)
                            mean(MEANH, (SQ, TC)[j], 4 + 2 * j, "norm_sum")
                    return at_chunk
                if c == 0:
                    pe.wait_ge(s["bank_free"], 6)
                unit(u + 1, (u + 1) % 2, 2 * ((u + 1) % 2), k_ready=head_sum(0))
                pe.wait_ge(s["bank_free"], u + 1)
                unit(u + 2, u % 2, 2 * (u % 2), k_ready=head_sum(1))

                def scores(n):
                    h, rp = n // 8, n % 8
                    ks, nk = key_rows(rp)
                    lo = DH * h
                    if n == 0:
                        pe.wait_ge(s["qk_hi"], 2 * c + 2)
                        pe.wait_ge(s["qk_lo"], 2 * c + 2)
                    else:
                        pe.wait_ge(s["scores_max"], 16 * c + n)
                    for q, k_, step in ((QH, KH, 0), (QH, KL, 1), (QL, KH, 2)):
                        for b, w in ((0, 512), (1, nk * GRID_W - 512)):
                            if w:
                                last = mm(PS[:, 2 + b, 0:w], q[lo:lo + DH, rp * P:(rp + 1) * P],
                                          k_[lo:lo + DH, ks * GRID_W + b * 512:ks * GRID_W + b * 512 + w],
                                          start=(step == 0), stop=(step == 2))
                    last.then_inc(s["scores_done"], 1)

                def turn(n):
                    _, nk = key_rows(n % 8)
                    pe.wait_ge(s["probs_scaled"], 16 * c + n + 1)
                    if n:
                        pe.wait_ge(s["pt_sb"], 16 * c + n)
                    else:
                        pe.wait_ge(s["v_ready"], c + 1)
                    for b in range(5 if nk == 9 else 4):
                        w = P if b < 4 else GRID_W
                        last = nc.tensor.transpose(PS[0:w, 4 + b // 4, (b % 4) * P:(b % 4 + 1) * P],
                                                   SB[n % 2][:, b * P:b * P + w], IDENT[:])
                    last.then_inc(s["pt_done"], 1)

                def values(n):
                    h, rp = n // 8, n % 8
                    ks, nk = key_rows(rp)
                    pe.wait_ge(s["pt_sb"], 16 * c + n + 1)
                    nb = 5 if nk == 9 else 4
                    for b in range(nb):
                        w = P if b < 4 else GRID_W
                        last = mm(PS[DH * h:DH * (h + 1), 6 + rp // 4, (rp % 4) * P:(rp % 4 + 1) * P],
                                  V[0:w, ks // 2 + b, DH * h:DH * (h + 1)], PT[n % 2][0:w, b, :],
                                  start=(b == 0), stop=(b == nb - 1), skip_group_check=True)
                    last.then_inc(s["pv_done"], 1)

                pe.wait_ge(s["bank_free"], u + 3)
                scores(0)
                if c:
                    pe.wait_ge(s["attn_out_done"], c)
                for b in range(8):
                    last = nc.tensor.transpose(PS[:, 6 + b // 4, (b % 4) * P:(b % 4 + 1) * P],
                                               TC[:, b * P:(b + 1) * P], IDENT[:])
                last.then_inc(s["v_tr"], 1)
                if c == 3:
                    pe.wait_ge(s["ln_ssq"], 3)
                    mean(MEAN, LT[0], 0, "ln_var")
                for n in range(16):
                    if n < 15:
                        scores(n + 1)
                    if n:
                        values(n - 1)
                    turn(n)
                values(15)

            for j in range(8):
                u = U_OUT + j
                if j >= 4:
                    pe.wait_ge(s["bank_free"], u - 3)
                elif j == 3:
                    pe.wait_ge(s["attn_out_done"], 4)
                elif j == 2:
                    pe.wait_ge(s["pt_sb"], 64)
                elif j == 1:
                    pe.wait_ge(s["scores_max"], 64)
                else:
                    pe.wait_ge(s["aux_free"], 1)

                def mix_ready(k):
                    pe.wait_ge(s["mix_hi"], k + 1)
                    pe.wait_ge(s["mix_lo"], k + 1)
                unit(u, j % 2, 2 * (j % 4), k_ready=mix_ready if j == 0 else None)

            def scale_sum(squares):
                pe.wait_ge(s["sq_added"], squares)
                mean(MEAN, SQ, 6, "mean_done")

            def scale_left(n):
                pe.wait_ge(s["scale_ready"], n)

            def ff_group(i, u0, n_h, up, split0, first=False, ready=None, scale=0):
                for j in range(2 if first else 0, up * n_h):
                    u = i * (up * G + G) + (u0 + j)
                    if first and j == 2:
                        pe.wait_ge(s["bank_free"], u0 - 2)
                        first_two(u0, ready)
                        pe.wait_ge(s["bank_free"], u0)
                        scale_sum(scale * KD)
                    if j < 4:
                        if not first:
                            pe.wait_ge(s["bank_free"], u - j + (-1 if j < 2 else 0))
                    else:
                        pe.wait_ge(s["bank_free"], u - 3)
                    if first and j == 3:
                        scale_left(scale)
                    unit(u, j % 2, 2 * (j % 4))
                for m in range(4):
                    u = i * (up * G + G) + (u0 + up * n_h + m)
                    if up * n_h >= 4 and m < 2:
                        pe.wait_ge(s["bank_free"], u - m - (2 if m == 0 else 0))
                    else:
                        pe.wait_ge(s["bank_free"], u - 1)

                    def hidden(k):
                        pe.wait_ge(s["ff_hi"], i * n_h + (split0 + k + 1))
                        pe.wait_ge(s["ff_lo"], i * n_h + (split0 + k + 1))
                    unit(u, m % 2, 4 * (m % 2), kc=n_h, nc_=2, inh=HH, inl=HL,
                         k_ready=hidden if m == 0 else None)

            ff_group(0, U_FF, G, 2, 0, first=True, ready=inputs(KD, KD), scale=2)
            with pe.Fori(1, NG1) as i:
                ff_group(i, U_FF, G, 2, 0)
            ff_group(0, U_TAIL, TAIL, 2, NG1 * G)

            pe.wait_ge(s["bank_free"], U_POOL - 1)
            first_two(U_POOL, inputs(2 * KD, 2 * KD))
            pe.wait_ge(s["bank_free"], U_POOL)
            scale_sum(3 * KD)
            for j in range(2, 4):
                if j == 3:
                    scale_left(3)
                unit(U_POOL + j, j % 2, 2 * (j % 4))
            pe.wait_ge(s["pool_w_in"], 16)

            def pool_product(j):
                pe.wait_ge(s["pool_d"], j + 1)
                b = 4 + 2 * (j % 2)
                for h in range(2):
                    last = mm(PS[:, b + h, :], WP[:, j, :], UB[:, j, h * H2:(h + 1) * H2], start=True, stop=True)
                last.then_inc(s["pool_y"], 1)

            pe.wait_ge(s["sb_const"], 1)
            tile = 0
            for c in range(4):
                u = U_QKV2 + 3 * c
                if c == 0:
                    pe.wait_ge(s["bank_free"], U_POOL + 1)
                    unit(u, 0, 0)
                    pe.wait_ge(s["bank_free"], U_QKV2)
                    pool_product(0)
                    pool_product(1)
                else:
                    pe.wait_ge(s["sb_exp"], tile)

                def beside_k(k):
                    if k == 2 and c:
                        pe.wait_ge(s["sb_osq"], c)
                        mean(MEANH, TA, 0, "sb_osum")
                    elif k == 3 and c == 0:
                        for m in (2, 3):
                            pe.wait_ge(s["pool_done"], m - 1)
                            pool_product(m)
                unit(u + 1, (u + 1) % 2, 2, k_ready=beside_k)
                if c == 0:
                    pe.wait_ge(s["pool_done"], 4)
                pe.wait_ge(s["bank_free"], u + 1)
                unit(u + 2, u % 2, 4)
                pe.wait_ge(s["q2_hi"], 2 * c + 2)
                pe.wait_ge(s["q2_lo"], 2 * c + 2)
                pe.wait_ge(s["bank_free"], u + 2)
                if c:
                    pe.wait_ge(s["sb_on"], c)

                def v_by_tokens():
                    pe.wait_ge(s["bank_free"], u + 3)
                    if c:
                        pe.wait_ge(s["sb_osq"], c)
                    for b in range(8):
                        last = nc.tensor.transpose(PS[:, 6 + b // 4, (b % 4) * P:(b % 4 + 1) * P],
                                                   TC[:, b * P:(b + 1) * P], IDENT[:])
                    last.then_inc(s["v2_tr"], 1)

                def next_q(k):
                    if k == 0:
                        pe.wait_ge(s["w_split"], u + 4)
                    last = chunk((u + 3) % 2, 4, k)
                    if k == KD - 1:
                        last.then_inc(s["unit_done"], 1)
                tiles = sb_tiles()

                def z_tile(n):
                    h, half, b, lo, w = tiles[n]
                    r = DH * h
                    if n >= 4:
                        pe.wait_ge(s["sb_exp"], c * len(tiles) + n - 3)
                    for q, k_, step in ((QH, KH, 0), (QL, KH, 1), (QH, KL, 2)):
                        last = mm(PS[:, n % 4, lo:], k_[r:r + DH, b * P:(b + 1) * P],
                                  q[r:r + DH, half * H2 + lo:(half + 1) * H2],
                                  start=(step == 0), stop=(step == 2), skip_group_check=True)
                    last.then_inc(s["sb_z"], 1)

                def cum_tile(n):
                    h, half, b, lo, w = tiles[n]
                    diag = b * P >= half * H2
                    pe.wait_ge(s["sb_soft"], c * len(tiles) + n + 1)
                    if diag:
                        mm(PS[:, n % 4, lo:lo + P], IDENT[:], NMASK[:], start=False, stop=False,
                           skip_group_check=True)
                    if b < 4 * half + 3:
                        pe.wait_ge(s["sb_run"], c * RUNS + runs_to(tiles, n))
                        mm(PS[:, n % 4, lo:], NONE[:], RUN[n % 2][:, lo:], start=False, stop=False,
                           skip_group_check=True)
                    pe.wait_ge(s["sb_sp"], c * len(tiles) + n + 1)
                    mm(PS[:, n % 4, lo:], NTRIR[:], SPH[n % 2][:, lo:], start=False, stop=False,
                       skip_group_check=True)
                    mm(PS[:, n % 4, lo:], NTRIR[:], SPL[n % 2][:, lo:], start=False, stop=True,
                       skip_group_check=True).then_inc(s["sb_cum"], 1)

                def pv_tile(n):
                    h, half, b, lo, w = tiles[n]
                    pe.wait_ge(s["sb_exp"], c * len(tiles) + n + 1)
                    if n == 0:
                        pe.wait_ge(s["v2_ready"], c + 1)
                    mm(PS[DH * h:DH * (h + 1), 6 + half, lo:], V2[:, b, DH * h:DH * (h + 1)],
                       AW[n % 2][:, lo:], start=(b == 4 * half + 3), stop=(b == 0),
                       skip_group_check=True).then_inc(s["sb_pv"], 1)

                z_tile(0)
                z_tile(1)
                v_by_tokens()
                for n in range(len(tiles)):
                    if n + 2 < len(tiles):
                        z_tile(n + 2)
                    if c < 3 and n in Q_BESIDE:
                        next_q(Q_BESIDE.index(n))
                    cum_tile(n)
                    if n:
                        pv_tile(n - 1)
                if c < 3:
                    next_q(KD - 1)
                pv_tile(len(tiles) - 1)
                tile += len(tiles)
            def mix_ready(k):
                if k == 2:
                    pe.wait_ge(s["sb_osq"], 4)
                    mean(MEANH, TA, 4, "sb_osum")
                pe.wait_ge(s["mix_hi"], 8 + k + 1)
                pe.wait_ge(s["mix_lo"], 8 + k + 1)
            pe.wait_ge(s["sb_exp"], tile)
            first_two(U_OUT2, mix_ready)
            for j in range(2, 8):
                u = U_OUT2 + j
                if j >= 4:
                    pe.wait_ge(s["bank_free"], u - 3)
                elif j == 2:
                    pe.wait_ge(s["sb_on"], 4)
                unit(u, j % 2, 2 * (j % 4))
            pe.wait_ge(s["bank_free"], U_MLP)
            scale_sum(4 * KD)
            ff_group(0, U_MLP, G, 1, NG1 * G + TAIL, first=True, ready=inputs(3 * KD, 3 * KD), scale=5)
            with pe.Fori(1, NG2) as i:
                ff_group(i, U_MLP, G, 1, NG1 * G + TAIL)
            for m in range(4):
                u = U_PLEP + m
                b = (0, 0, 4, 0)[m]
                if m == 1:
                    pe.wait_ge(s["bank_free"], U_PLEP)
                    scale_sum(6 * KD)
                if m == 2:
                    scale_left(6)
                pe.wait_ge(s["bank_free"], u - 1 if m != 1 else u)

                def p_ready(k):
                    pe.wait_ge(s["ple_hi"], k + 1)
                    pe.wait_ge(s["ple_lo"], k + 1)
                unit(u, m % 2, b, kc=2, nc_=2, inh=PPH, inl=PPL,
                     k_ready=p_ready if m == 0 else None)
            pe.wait_ge(s["bank_free"], U_PLEG)
            first_two(U_PLEG, inputs(4 * KD, 4 * KD), INL, GL)
            for j in range(2, 8):
                u = U_PLEG + j
                if j >= 3:
                    pe.wait_ge(s["bank_free"], u - 2)
                if j == 4:
                    scale_sum(7 * KD)
                unit(u, j % 2, 2 * (j % 3), inh=INL, inl=GL)

        @block.scalar
        def _(act):
            chain = Chain(act, s["act_chain"])
            copy = lambda out, in_, scale=1.0: act_.activation(out, in_, ACT.Copy, scale=scale)
            lnexp = "natural_log_exp_and_others"

            sq_count = [0]

            def square(src, dst):
                n = sq_count[0]
                if n >= 2:
                    act.wait_ge(s["sq_added"], n - 1)
                act_.activation(dst, src, ACT.Square).then_inc(s["sq_ready"], 1)
                sq_count[0] += 1

            def first_guess(ps, dst, wait, value, signal, scale=1.0, halves=(0, 1)):
                act_.preload_act_table_set(lnexp)
                for h in halves:
                    y0 = dst[:, h * H2:(h + 1) * H2]
                    act.wait_ge(s[wait], 2 * value - 1 + h)
                    chain(act_.activation(y0, ps[:, h * H2:(h + 1) * H2], ACT.Ln, bias=EPSC[:, 0:1], scale=scale))
                    chain.wait()
                    act_.activation(y0, y0, ACT.Exp, scale=-0.5).then_inc(s[signal], 1)

            def hi(k, src, gain):
                act_.activation(INH[:, k, :], src, ACT.Identity, scale=gain).then_inc(s["split_hi"], 1)

            act.wait_ge(s["w_loaded0"], 16)
            copy(WH[:, 0, :], RAW[:, 0, :]).then_inc(s["w_hi"], 1)
            act.wait_ge(s["gains_in"], 32)
            act.wait_ge(s["consts_ready"], 1)
            for k in range(KD):
                act.wait_ge(s[f"x_in{k // 2}" if k else "x_first"], 16)
                hi(k, X[:, k, :], g("norm1", k))
                square(X[:, k, :], (TA, TB)[k % 2][:])
            first_guess(bank(6), RS[:], "mean_done", 1, "ln_exp")
            act.wait_ge(s["neg_ready"], 1)
            for h in range(HEADS):
                act.dma_start(BD[h], NEG[:]).then_inc(s["neg_out"], 16)

            def bias_windows():
                act.wait_ge(s["neg_out"], 16 * HEADS)
                rows, cols = 2 * NA_ROWS - 1, 2 * NA_COLS - 1
                half = NA_COLS // 2
                inner = GRID_W - NA_COLS + 1
                with nc.allow_non_contiguous_dma(reason="64-byte windows of the bias"):
                    for r in range(2):
                        for h in range(HEADS):
                            dst = bass.AP(tensor=BD.tensor, offset=((h * P + r * GRID_W + half) * 16 + r) * GRID_W,
                                          ap=[[16 * GRID_W + 1, inner], [GRID_W, rows], [1, NA_COLS]])
                            src = bass.AP(tensor=rpb.tensor, offset=h * rows * cols + half - 1,
                                          ap=[[0, inner], [cols, rows], [1, NA_COLS]])
                            act.dma_start(dst, src).then_inc(s["table_out"], 16)
                        for q in [*range(half), *range(half + inner, GRID_W)]:
                            start = 0 if q < half else GRID_W - NA_COLS
                            dst = bass.AP(tensor=BD.tensor, offset=((r * GRID_W + q) * 16 + r) * GRID_W + start,
                                          ap=[[P * 16 * GRID_W, HEADS], [GRID_W, rows], [1, NA_COLS]])
                            src = bass.AP(tensor=rpb.tensor, offset=start - q + NA_COLS - 1,
                                          ap=[[rows * cols, HEADS], [cols, rows], [1, NA_COLS]])
                            act.dma_start(dst, src).then_inc(s["table_out"], 16)

            for c in range(4):
                act.wait_ge(s["bank_free"], 2 * c + 1)
                act_.activation(TB[:], TA[:], ACT.Sigmoid).then_inc(s["glu_sig"], 1)
                if c == 1:
                    bias_windows()

            MIX = [Y[:, c, :] for c in range(4)] + [OC[c][:] for c in range(4)]

            def mix_hi(k, src):
                copy(INH[:, k, :], src).then_inc(s["mix_hi"], 1)

            for c in range(4):
                def head_square(j):
                    act.wait_ge(s["bank_free"], U_QKV + 3 * c + j + 1)
                    if j and c:
                        act.wait_ge(s["v_tr"], c)
                    act_.activation((SQ, TC)[j][:], (TA, TB)[j][:], ACT.Square).then_inc(s["qk_sq"], 1)

                def head_hi(j):
                    act.wait_ge(s["qk_scaled"], 2 * c + j + 1)
                    if j == 0 and c:
                        act.wait_ge(s["scores_done"], 16 * c)
                    copy((QH, KH)[j][:], (TA, TB)[j][:]).then_inc(s["qk_hi"], 1)

                head_square(0)
                if c == 3:
                    for m in range(4):
                        act.wait_ge(s["ln_cent"], m + 1)
                        act_.activation(LT[m][:], Y[:, m, :], ACT.Square).then_inc(s["ln_sq"], 1)
                first_guess(bank(4), SQ[:], "norm_sum", 2 * c + 1, "qk_y0")
                head_square(1)
                head_hi(0)
                first_guess(bank(6), TC[:], "norm_sum", 2 * c + 2, "qk_y0")
                head_hi(1)
                act.wait_ge(s["v_tr"], c + 1)
                if c:
                    act.wait_ge(s["pv_done"], 16 * c)
                copy(V[:, :, :].rearrange("p b d -> p (b d)"), bank(6)).then_inc(s["v_ready"], 1)
                for n in range(16):
                    _, nk = key_rows(n % 8)
                    w = nk * GRID_W

                    def exps(m):
                        wm = key_rows(m % 8)[1] * GRID_W
                        act.wait_ge(s["scores_max"], 16 * c + m + 1)
                        act_.activation(SB[m % 2][:, 0:wm], SB[m % 2][:, 0:wm], ACT.Exp, scale=-1.0,
                                        bias=ST[:, 0, m:m + 1], accum_out=ST[:, 1, m:m + 1])\
                            .then_inc(s["probs_done"], 1)
                    if n == 0:
                        exps(0)
                    if n < 15:
                        exps(n + 1)
                    if c == 3 and n in (1, 2):
                        first_guess(bank(0), LT[1][:], "ln_var", 1, "ln_y0", scale=2.0, halves=(n - 1,))
                    if c == 3 and n == 10:
                        for m in range(4):
                            act.wait_ge(s["ln_norm"], m + 1)
                            act_.activation(Y[:, m, :], Y[:, m, :], ACT.Silu, bias=g("ln_b", m),
                                            scale=g("ln_g", m)).then_inc(s["ln_silu"], 1)
                    if c == 3 and n >= 10:
                        if n == 10:
                            act.wait_ge(s["unit_done"], U_OUT)
                            act.wait_ge(s["ln_silu"], 4)
                        mix_hi(n - 10, MIX[n - 10])
                    act.wait_ge(s["pt_done"], 16 * c + n + 1)
                    if n >= 2:
                        act.wait_ge(s["pv_done"], 16 * c + n - 1)
                    if nk == 9:
                        copy(PT[n % 2][0:GRID_W, 4, :], PS[0:GRID_W, 5, 0:P])
                    copy(PT[n % 2][:, 0:4, :].rearrange("p b q -> p (b q)"), PS[:, 4, :])\
                        .then_inc(s["pt_sb"], 1)
                if c == 3:
                    mix_hi(6, MIX[6])
                act.wait_ge(s["pv_done"], 16 * (c + 1))
                act.wait_ge(s["conv_out_done"], c + 1)
                copy(OC[c][:], bank(6)).then_inc(s["attn_out_done"], 1)
            act.wait_ge(s["attn_out_done"], 4)
            mix_hi(7, OC[3][:])

            for k in range(KD):
                if k < KD - 1:
                    act.wait_ge(s["bank_free"], U_OUT + k + 1)
                    square(X[:, k, :], (TA, TB)[k % 2][:])
            act.wait_ge(s["unit_done"], U_FF)
            for k in range(KD):
                if k == 2:
                    act.wait_ge(s["bank_free"], U_FF)
                    square(X[:, KD - 1, :], (TA, TB)[(KD - 1) % 2][:])
                hi(k, X[:, k, :], g("norm2", k))
            first_guess(bank(6), RS[:], "mean_done", 2, "ln_exp")

            def ff_hi(i, u0, n_h, up, h0):
                for n in range(n_h):
                    act.wait_ge(s["bank_free"], i * (up * G + G) + (u0 + up * n + 1))
                    if up == 2:
                        act_.activation(TB[:], TA[:], ACT.Silu).then_inc(s["ff_silu"], 1)
                    else:
                        act_.activation(TB[:], TA[:], ACT.Square).then_inc(s["ff_silu"], 1)
                    if up == 2:
                        act.wait_ge(s["ff_h"], i * n_h + (h0 + n + 1))
                        src = TC
                    else:
                        act.wait_ge(s["ff_silu"], i * n_h + (h0 + n + 1))
                        src = TB
                    act.wait_ge(s["unit_done"], i * (up * G + G) + u0)
                    copy(HH[:, n, :], src[:]).then_inc(s["ff_hi"], 1)

            with act.Fori(0, NG1) as i:
                ff_hi(i, U_FF, G, 2, 0)
            ff_hi(0, U_TAIL, TAIL, 2, NG1 * G)

            def two_chunks(u0, name):
                for m in range(4):
                    act.wait_ge(s["bank_free"], u0 + m + 1)
                    for k in (2 * m, 2 * m + 1):
                        hi(k, X[:, k, :], g(name, k))
                    for k in (2 * m, 2 * m + 1):
                        square(X[:, k, :], (TA, TB)[k % 2][:])
            two_chunks(U_TAIL + 2 * TAIL, "g_mix_pre")
            first_guess(bank(6), RS[:], "mean_done", 3, "ln_exp")

            act_.preload_act_table_set(lnexp)
            MIX2 = [UB[:, c, :] for c in range(4)] + [OB[c][:] for c in range(4)]
            tiles = sb_tiles()
            for c in range(4):
                for j in range(2):
                    act.wait_ge(s["bank_free"], U_QKV2 + 3 * c + j + 1)
                    if c:
                        act.wait_ge(s["sb_z"], c * len(tiles))
                    copy((QH, KH)[j][:], (SQ, TB)[j][:]).then_inc(s["q2_hi"], 1)

                def lse(n):
                    h, half, b, lo, w = tiles[n]
                    act.wait_ge(s["sb_z"], c * len(tiles) + n + 1)
                    if n >= 2:
                        act.wait_ge(s["sb_sp"], c * len(tiles) + n - 1)
                        act.wait_ge(s["sb_run"], c * RUNS + runs_to(tiles, n - 1))
                    e = EX[n % 2][:, lo:]
                    chain(act_.activation(e, PS[:, n % 4, lo:], ACT.Abs))
                    chain.wait()
                    chain(act_.activation(e, e, ACT.Exp, scale=-1.0))
                    chain.wait()
                    act_.activation(e, e, ACT.Ln, bias=1.0).then_inc(s["sb_lse"], 1)

                lse(0)
                act.wait_ge(s["v2_tr"], c + 1)
                if c:
                    act.wait_ge(s["sb_pv"], c * len(tiles))
                copy(V2[:, :, :].rearrange("p b d -> p (b d)"), bank(6)).then_inc(s["v2_ready"], 1)
                for n in range(len(tiles)):
                    h, half, b, lo, w = tiles[n]
                    if n + 1 < len(tiles):
                        lse(n + 1)
                    act.wait_ge(s["sb_cum"], c * len(tiles) + n + 1)
                    if n >= 2:
                        act.wait_ge(s["sb_pv"], c * len(tiles) + n - 1)
                    act_.activation(AW[n % 2][:, lo:], PS[:, n % 4, lo:], ACT.Exp).then_inc(s["sb_exp"], 1)
                    if c == 3 and n % 3 == 0 and n < 21:
                        if n == 0:
                            act.wait_ge(s["unit_done"], U_OUT2)
                            act.wait_ge(s["pool_done"], 4)
                            act.wait_ge(s["sb_on"], 3)
                        mix_hi(n // 3, MIX2[n // 3])
                act.wait_ge(s["sb_pv"], (c + 1) * len(tiles))
                chain(copy(OB[c][:], bank(6)))
                chain.wait()
                act_.activation(TA[:], OB[c][:], ACT.Square).then_inc(s["sb_osq"], 1)
                first_guess(bank(0 if c < 3 else 4), TB[:], "sb_osum", c + 1, "sb_o0")

            act.wait_ge(s["sb_on"], 4)
            mix_hi(7, OB[3][:])

            for k in range(KD):
                act.wait_ge(s["bank_free"], U_OUT2 + k + 1)
                square(MM[:, k, :], (TA, TB)[k % 2][:])
            first_guess(bank(6), RS[:], "mean_done", 4, "ln_exp")

            for k in range(KD):
                act.wait_ge(s["post_x"], k + 1)
                hi(k, X[:, k, :], g("g_mlp_pre", k))
                square(X[:, k, :], (TA, TB)[k % 2][:])
            first_guess(bank(6), RS[:], "mean_done", 5, "ln_exp")
            with act.Fori(0, NG2) as i:
                ff_hi(i, U_MLP, G, 1, NG1 * G + TAIL)
            act.wait_ge(s["ple_p_in"], 16)
            for k in range(2):
                copy(PPH[:, k, :], PPF[:, k, :]).then_inc(s["ple_hi"], 1)
            for m in range(4):
                act.wait_ge(s["bank_free"], U_PLEP - 4 + m + 1)
                for k in (2 * m, 2 * m + 1):
                    square(MM[:, k, :], (TA, TB)[k % 2][:])

            def embedding(m):
                act.wait_ge(s["unit_done"], U_PLEP + m + 1)
                chain(copy(EMB[:, 2 * m, :], bank((0, 0, 4, 0)[m])))
                copy(EMB[:, 2 * m + 1, :], bank((2, 2, 6, 2)[m])).then_inc(s["bank_free"], 1)
            embedding(0)
            first_guess(bank(6), RS[:], "mean_done", 6, "ln_exp")
            embedding(1)
            embedding(2)
            embedding(3)
            for k in range(KD):
                act.wait_ge(s["post_x"], KD + k + 1)
                copy(INL[:, k, :], X[:, k, :]).then_inc(s["split_hi"], 1)
                if k == 0:
                    act.wait_ge(s["bank_free"], U_PLEG)
                    chain.wait()
                square(EMB[:, k, :], (TA, TB)[k % 2][:])

            def gate(k):
                act.wait_ge(s["unit_done"], U_PLEG + k + 1)
                act_.activation(GT[:, k, :], bank(2 * (k % 3)), ACT.Sigmoid).then_inc(s["bank_free"], 1)
            gate(0)
            gate(1)
            first_guess(bank(6), RS[:], "mean_done", 7, "ln_exp")
            for k in range(2, KD):
                gate(k)

        @block.vector
        def _(dve):
            chain = Chain(dve, s["dve_chain"])
            stt, tt, ts = dve_.scalar_tensor_tensor, dve_.tensor_tensor, dve_.tensor_scalar

            added = [0]

            def add_square():
                n = added[0]
                dve.wait_ge(s["sq_ready"], n + 1)
                if n % KD:
                    dve.wait_ge(s["sq_added"], n)
                t = (TA, TB)[n % 2]
                if n % KD == 0:
                    dve_.tensor_copy(SQ[:], t[:]).then_inc(s["sq_added"], 1)
                else:
                    tt(SQ[:], SQ[:], t[:], ALU.add).then_inc(s["sq_added"], 1)
                added[0] += 1

            def refine(ps, y0, guess, n, scale=1.0):
                half = [slice(0, H2), slice(H2, T)]

                def shifted(h):
                    dve.wait_ge(s[guess], 2 * n - 1 + h)
                    return chain(stt(ps[:, half[h]], ps[:, half[h]], EPS / scale, y0[:, half[h]], ALU.add, ALU.mult))

                def scaled(h):
                    return chain(stt(ps[:, half[h]], ps[:, half[h]], -0.5 * scale, y0[:, half[h]],
                                     ALU.mult, ALU.mult))

                def last(h):
                    return stt(y0[:, half[h]], ps[:, half[h]], 1.5, y0[:, half[h]], ALU.add, ALU.mult)
                mark0 = shifted(0)
                chain.wait(mark0)
                mark0 = scaled(0)
                mark1 = shifted(1)
                chain.wait(mark0)
                chain(last(0))
                chain.wait(mark1)
                scaled(1)
                chain.wait()
                return last(1)

            def lo(k, src, gain=1.0):
                stt(INL[:, k, :], src, gain, INH[:, k, :].bitcast(f32), ALU.mult, ALU.subtract)\
                    .then_inc(s["split_lo"], 1)

            def scale_from(n):
                refine(bank(6), RS[:], "ln_exp", n).then_inc(s["scale_ready"], 1)
                dve.wait_ge(s["scale_ready"], n)

            dve.wait_ge(s["w_hi"], 1)
            tt(WL[:, 0, :], RAW[:, 0, :], WH[:, 0, :].bitcast(f32), ALU.subtract).then_inc(s["w_split"], 1)
            for k in range(KD):
                dve.wait_ge(s["split_hi"], k + 1)
                lo(k, X[:, k, :], g("norm1", k))
                add_square()
            scale_from(1)
            for m in (slice(0, PADT), slice(T + PADT, T + 2 * PADT)):
                chain(dve_.memset(UP[:, :, m], 0.0))
            chain(ts(GS[:, 0:1], g("q_g"), DH ** -0.5, None, ALU.mult))
            chain(dve_.tensor_copy(GS[:, 1:2], g("k_g")))
            chain.wait()

            tap = [0]

            def conv(n):
                for _ in range(n):
                    c, t = divmod(tap[0], TAPS)
                    src = UP[:, c, t:t + T]
                    if t == 0:
                        ins = ts(Y[:, c, :], src, TP[:, c, 0:1], g("dw_bias", c), ALU.mult, ALU.add)
                    else:
                        ins = stt(Y[:, c, :], src, TP[:, c, t:t + 1], Y[:, c, :], ALU.mult, ALU.add)
                    if t == TAPS - 1:
                        ins.then_inc(s["conv_out_done"], 1)
                        dve.wait_ge(s["conv_out_done"], c + 1)
                    else:
                        chain(ins)
                        chain.wait()
                    tap[0] += 1

            for c in range(4):
                dve.wait_ge(s["unit_done"], 2 * c + 1)
                if c:
                    dve.wait_ge(s["glu_sig"], c)
                tt(TA[:], bank(4 * (c % 2)), RS[:], ALU.mult).then_inc(s["bank_free"], 1)
                dve.wait_ge(s["bank_free"], 2 * c + 1)
                if c:
                    conv(4 if c == 3 else 6)
                dve.wait_ge(s["unit_done"], 2 * c + 2)
                tt(TC[:], bank(4 * (c % 2) + 2), RS[:], ALU.mult).then_inc(s["bank_free"], 1)
                dve.wait_ge(s["bank_free"], 2 * c + 2)
                dve.wait_ge(s["glu_sig"], c + 1)
                chain(tt(UP[:, c, PADT:PADT + T], TC[:], TB[:], ALU.mult))
                if c:
                    conv(2 if c == 3 else 6)
            MIX = [Y[:, c, :] for c in range(4)] + [OC[c][:] for c in range(4)]

            def mix_lo(k, src, n0):
                dve.wait_ge(s["mix_hi"], n0 + k + 1)
                tt(INL[:, k, :], src, INH[:, k, :].bitcast(f32), ALU.subtract).then_inc(s["mix_lo"], 1)

            for c in range(4):
                u = U_QKV + 3 * c
                if c == 3:
                    assert tap[0] == 4 * TAPS

                def evac(j, t):
                    dve.wait_ge(s["unit_done"], u + j + 1)
                    tt(t[:], bank(2 * ((u + j) % 2)), RS[:], ALU.mult).then_inc(s["bank_free"], 1)
                    dve.wait_ge(s["bank_free"], u + j + 1)

                def head_refine(j):
                    chain(refine(bank(4 + 2 * j), (SQ, TC)[j][:], "qk_y0", 2 * c + j + 1))

                def head_scale(j):
                    t = (TA, TB)[j]
                    chain.wait()
                    stt(t[:], t[:], GS[:, j:j + 1], (SQ, TC)[j][:], ALU.mult, ALU.mult).then_inc(s["qk_scaled"], 1)

                def head_lo(j):
                    dve.wait_ge(s["qk_hi"], 2 * c + j + 1)
                    tt((QL, KL)[j][:], (TA, TB)[j][:], (QH, KH)[j][:].bitcast(f32), ALU.subtract)\
                        .then_inc(s["qk_lo"], 1)

                def probs(m):
                    w = key_rows(m % 8)[1] * GRID_W
                    dve.wait_ge(s["probs_done"], 16 * c + m + 1)
                    chain(dve_.reciprocal(ST[:, 2, m:m + 1], ST[:, 1, m:m + 1]))
                    chain.wait()
                    ts(SB[m % 2][:, 0:w], SB[m % 2][:, 0:w], ST[:, 2, m:m + 1], None, ALU.mult)\
                        .then_inc(s["probs_scaled"], 1)

                if c == 3:
                    chain(tt(LT[0][:], Y[:, 0, :], Y[:, 1, :], ALU.add))
                    chain.wait()
                    chain(tt(LT[0][:], LT[0][:], Y[:, 2, :], ALU.add))
                    chain.wait()
                    tt(LT[0][:], LT[0][:], Y[:, 3, :], ALU.add).then_inc(s["ln_in"], 1)
                else:
                    conv((4, 10, 10)[c])
                evac(0, TA)
                if c < 3:
                    conv(6)
                else:
                    dve.wait_ge(s["ln_mean"], 2)
                    for m in range(4):
                        stt(Y[:, m, :], bank(6), -2.0, Y[:, m, :], ALU.mult, ALU.add).then_inc(s["ln_cent"], 1)
                head_refine(0)
                evac(1, TB)
                head_scale(0)
                if c == 3:
                    for m in range(1, 4):
                        dve.wait_ge(s["ln_sq"], m + 1)
                        if m > 1:
                            dve.wait_ge(s["ln_ssq"], m - 1)
                        tt(LT[0][:], LT[0][:], LT[m][:], ALU.add).then_inc(s["ln_ssq"], 1)
                head_lo(0)
                if c < 3:
                    conv(2 if c == 2 else 1)
                head_refine(1)
                head_scale(1)
                dve.wait_ge(s["qk_scaled"], 2 * c + 2)
                head_lo(1)
                evac(2, TC)
                for n in range(16):
                    h, rp = 2 * c + n // 8, n % 8
                    ks, nk = key_rows(rp)
                    w = nk * GRID_W
                    if rp == 0:
                        dve.wait_ge(s[f"bt_in{h % 2}"], 16 * (h // 2 + 1))
                        chain(dve_.tensor_copy(BI[:], BT[h % 2][:, 3:12, :]))
                        chain.wait()
                        chain(dve_.memset(BI[0:GRID_W, 8, :], MASKED))
                        chain(dve_.memset(BI[GRID_W:P, 0, :], MASKED))
                        chain.wait()
                    first = ks - 2 * rp + NA_ROWS - 1
                    bias = BI[:] if nk == 9 else BT[h % 2][:, first:first + nk, :]
                    dve.wait_ge(s["scores_done"], 16 * c + n + 1)
                    if n >= 2:
                        dve.wait_ge(s["pt_done"], 16 * c + n - 1)
                    dve_.tensor_tensor_reduce(
                        out=SB[n % 2][:, 0:w], in0=bank(2)[:, 0:w], in1=bias.rearrange("p r c -> p (r c)"),
                        scale=-1.0, scalar=3.0e38, op0=ALU.add, op1=ALU.min,
                        accum_out=ST[:, 0, n:n + 1]).then_inc(s["scores_max"], 1)
                    if c < 3:
                        conv(1)
                    elif 3 <= n < 6:
                        if n == 3:
                            dve.wait_ge(s["ln_y0"], 2)
                            chain(stt(bank(0), bank(0), EPS / 2.0, LT[1][:], ALU.add, ALU.mult))
                        elif n == 4:
                            chain(stt(bank(0), bank(0), -1.0, LT[1][:], ALU.mult, ALU.mult))
                        else:
                            stt(LT[1][:], bank(0), 1.5, LT[1][:], ALU.add, ALU.mult).then_inc(s["aux_free"], 1)
                            dve.wait_ge(s["aux_free"], 1)
                        if n < 5:
                            chain.wait()
                    elif 6 <= n < 10:
                        tt(Y[:, n - 6, :], Y[:, n - 6, :], LT[1][:], ALU.mult).then_inc(s["ln_norm"], 1)
                    elif n >= 11:
                        mix_lo(n - 11, MIX[n - 11], 0)
                    probs(n)
            for k in range(5, KD):
                mix_lo(k, MIX[k], 0)

            for k in range(KD):
                dve.wait_ge(s["unit_done"], U_OUT + k + 1)
                dve.wait_ge(s[f"x_in{k // 2}"], 32)
                tt(X[:, k, :], bank(2 * (k % 4)), X[:, k, :], ALU.add).then_inc(s["bank_free"], 1)
                if 0 < k < KD - 1:
                    add_square()
            for k in range(KD):
                dve.wait_ge(s["split_hi"], KD + k + 1)
                lo(k, X[:, k, :], g("norm2", k))
                if k < 2:
                    add_square()
            scale_from(2)

            def ff_lo(i, u0, n_h, up, h0, target, ff_first=False, after=None, beside=None):
                per = up * G + G
                for n in range(n_h):
                    b = 4 * (n % 2) if up == 2 else 2 * (n % 4)
                    dve.wait_ge(s["unit_done"], i * per + (u0 + up * n + 1))
                    if not (ff_first and n == 0):
                        dve.wait_ge(s["ff_silu"], i * n_h + (h0 + n))
                        dve.wait_ge(s["ff_lo"], i * n_h + (h0 + n))
                    if up == 2:
                        tt(TA[:], bank(b), RS[:], ALU.mult).then_inc(s["bank_free"], 1)
                        dve.wait_ge(s["bank_free"], i * per + (u0 + up * n + 1))
                        dve.wait_ge(s["unit_done"], i * per + (u0 + up * n + 2))
                        tt(TC[:], bank(b + 2), RS[:], ALU.mult).then_inc(s["bank_free"], 1)
                        dve.wait_ge(s["bank_free"], i * per + (u0 + up * n + 2))
                        dve.wait_ge(s["ff_silu"], i * n_h + (h0 + n + 1))
                        tt(TC[:], TC[:], TB[:], ALU.mult).then_inc(s["ff_h"], 1)
                        dve.wait_ge(s["ff_h"], i * n_h + (h0 + n + 1))
                        src = TC
                    else:
                        stt(TA[:], bank(b), 0.0, RS[:], ALU.max, ALU.mult).then_inc(s["bank_free"], 1)
                        dve.wait_ge(s["bank_free"], i * per + (u0 + up * n + 1))
                        dve.wait_ge(s["ff_silu"], i * n_h + (h0 + n + 1))
                        src = TB
                    dve.wait_ge(s["ff_hi"], i * n_h + (h0 + n + 1))
                    tt(HL[:, n, :], src[:], HH[:, n, :].bitcast(f32), ALU.subtract).then_inc(s["ff_lo"], 1)
                for m in range(4):
                    dve.wait_ge(s["unit_done"], i * per + (u0 + up * n_h + m + 1))
                    for c in range(2):
                        dst = target[:, 2 * m + c, :]
                        src = bank(4 * (m % 2) + 2 * c)
                        if after == "fill":
                            ins = dve_.tensor_copy(dst, src)
                        else:
                            ins = tt(dst, src, dst, ALU.add)
                        if c == 0:
                            ins.then_inc(s["ff_acc"], 1)
                        else:
                            ins.then_inc(s["bank_free"], 1)
                    if beside:
                        beside(m)

            def tail_lo(m):
                if m:
                    add_square()
                for k in (2 * m, 2 * m + 1):
                    dve.wait_ge(s["split_hi"], 2 * KD + k + 1)
                    lo(k, X[:, k, :], g("g_mix_pre", k))
                add_square()

            ff_lo(0, U_FF, G, 2, 0, X, ff_first=True)
            with dve.Fori(1, NG1) as i:
                dve.wait_ge(s["bank_free"], i * (3 * G) + U_FF)
                dve.wait_ge(s["ff_acc"], i * 4)
                ff_lo(i, U_FF, G, 2, 0, X)
            dve.wait_ge(s["bank_free"], U_TAIL)
            dve.wait_ge(s["ff_acc"], NG1 * 4)
            ff_lo(0, U_TAIL, TAIL, 2, NG1 * G, X, beside=tail_lo)
            add_square()
            scale_from(3)

            def pool_in(j):
                dve.wait_ge(s["unit_done"], U_POOL + j + 1)
                tt(UB[:, j, :], bank(2 * (j % 4)), RS[:], ALU.mult).then_inc(s["bank_free"], 1)
                dve.wait_ge(s["bank_free"], U_POOL + j + 1)

            def pooled(j):
                w = WINDOWS[j]
                src, bufs, step = UB[:, j, :], [TA[:], TB[:]], 1
                while step < w:
                    dst = bufs[0]
                    chain(dve_.tensor_copy(dst[:, 0:step], src[:, 0:step]))
                    chain(tt(dst[:, step:], src[:, step:], src[:, 0:T - step], ALU.add))
                    chain.wait()
                    src, bufs, step = dst, bufs[::-1], 2 * step
                for t in range(w - 1):
                    chain(ts(src[:, t:t + 1], src[:, t:t + 1], float(w) / (t + 1), None, ALU.mult))
                chain.wait()
                stt(UB[:, j, :], src, 1.0 / w, UB[:, j, :], ALU.mult, ALU.subtract).then_inc(s["pool_d"], 1)
                dve.wait_ge(s["pool_d"], j + 1)

            def pool_out(j):
                dve.wait_ge(s["pool_y"], j + 1)
                ts(UB[:, j, :], bank(4 + 2 * (j % 2)), g("pool_scale", j), None, ALU.mult).then_inc(s["pool_done"], 1)
            pool_in(0)
            pool_in(1)
            pooled(0)
            pooled(1)
            pool_in(2)
            pooled(2)
            pool_in(3)
            pooled(3)

            MIX2 = [UB[:, c, :] for c in range(4)] + [OB[c][:] for c in range(4)]
            tiles = sb_tiles()
            for c in range(4):
                u = U_QKV2 + 3 * c

                def evac2(j, t, b, u=u):
                    dve.wait_ge(s["unit_done"], u + j + 1)
                    stt(t[:], bank(b), DH ** -0.5 if j == 0 else 1.0, RS[:],
                        ALU.mult, ALU.mult).then_inc(s["bank_free"], 1)
                    dve.wait_ge(s["bank_free"], u + j + 1)
                for j in range(2):
                    if j:
                        evac2(1, TB, 2)
                    elif c == 0:
                        evac2(0, SQ, 0)
                    dve.wait_ge(s["q2_hi"], 2 * c + j + 1)
                    tt((QL, KL)[j][:], (SQ, TB)[j][:], (QH, KH)[j][:].bitcast(f32), ALU.subtract)\
                        .then_inc(s["q2_lo"], 1)
                    if c == 0:
                        pool_out(2 * j)
                        pool_out(2 * j + 1)
                evac2(2, TC, 4)
                dve.wait_ge(s["q2_lo"], 2 * c + 2)
                for n in range(len(tiles)):
                    h, half, b, l0, w = tiles[n]
                    N = c * len(tiles) + n
                    e = EX[n % 2]
                    dve.wait_ge(s["sb_lse"], N + 1)
                    softplus = stt(e[:, l0:], PS[:, n % 4, l0:], 0.0, e[:, l0:], ALU.max, ALU.add)
                    if b * P >= half * H2:
                        chain(softplus)
                        chain.wait()
                        softplus = tt(e[:, l0:l0 + P], e[:, l0:l0 + P], KEEP[:], ALU.mult)
                    softplus.then_inc(s["sb_soft"], 1)
                    dve.wait_ge(s["sb_soft"], N + 1)
                    if n >= 2:
                        dve.wait_ge(s["sb_cum"], N - 1)
                    chain(dve_.tensor_copy(SPH[n % 2][:, l0:], e[:, l0:]))
                    chain.wait()
                    tt(SPL[n % 2][:, l0:], e[:, l0:], SPH[n % 2][:, l0:].bitcast(f32), ALU.subtract)\
                        .then_inc(s["sb_sp"], 1)
                    if c == 3 and n % 3 == 2 and n < 21:
                        mix_lo(n // 3, MIX2[n // 3], 8)
                if c < 3:
                    dve.wait_ge(s["sb_pv"], (c + 1) * len(tiles))
                    evac2(0, SQ, 4, u + 3)
                chain(refine(bank(0 if c < 3 else 4), TB[:], "sb_o0", c + 1))
                chain.wait()
                stt(OB[c][:], OB[c][:], g("g_sb", c), TB[:], ALU.mult, ALU.mult).then_inc(s["sb_on"], 1)
                dve.wait_ge(s["sb_on"], c + 1)

            mix_lo(7, OB[3][:], 8)
            dve.wait_ge(s["mix_lo"], 16)
            for k in range(KD):
                dve.wait_ge(s["unit_done"], U_OUT2 + k + 1)
                dve_.tensor_copy(MM[:, k, :], bank(2 * (k % 4))).then_inc(s["bank_free"], 1)
                add_square()

            scale_from(4)
            for k in range(KD):
                if k == 0:
                    chain(tt(MM[:, 0, :], MM[:, 0, :], RS[:], ALU.mult))
                    chain.wait()
                else:
                    dve.wait_ge(s["post_scaled"], k)
                stt(X[:, k, :], MM[:, k, :], g("g_mix_post", k), X[:, k, :], ALU.mult, ALU.add)\
                    .then_inc(s["post_x"], 1)
                if k:
                    dve.wait_ge(s["split_hi"], 3 * KD + k)
                    lo(k - 1, X[:, k - 1, :], g("g_mlp_pre", k - 1))
                if k > 1:
                    add_square()
            dve.wait_ge(s["split_hi"], 4 * KD)
            lo(KD - 1, X[:, KD - 1, :], g("g_mlp_pre", KD - 1))
            add_square()
            add_square()
            scale_from(5)
            h0 = NG1 * G + TAIL
            ff_lo(0, U_MLP, G, 1, h0, MM, after="fill")
            with dve.Fori(1, NG2 - 1) as i:
                dve.wait_ge(s["bank_free"], i * (2 * G) + U_MLP)
                dve.wait_ge(s["ff_acc"], i * 4 + 4 * (NG1 + 1))
                ff_lo(i, U_MLP, G, 1, h0, MM)

            def p_and_squares(m):
                if m == 0:
                    for k in range(2):
                        dve.wait_ge(s["ple_hi"], k + 1)
                        tt(PPL[:, k, :], PPF[:, k, :], PPH[:, k, :].bitcast(f32), ALU.subtract)\
                            .then_inc(s["ple_lo"], 1)
                add_square()
                if m:
                    add_square()
            dve.wait_ge(s["bank_free"], (NG2 - 1) * (2 * G) + U_MLP)
            dve.wait_ge(s["ff_acc"], (NG2 - 1) * 4 + 4 * (NG1 + 1))
            ff_lo(NG2 - 1, U_MLP, G, 1, h0, MM, beside=p_and_squares)
            add_square()
            scale_from(6)
            for k in range(KD):
                chain(stt(MM[:, k, :], MM[:, k, :], g("g_mlp_post", k), RS[:], ALU.mult, ALU.mult))
                chain.wait()
                tt(X[:, k, :], X[:, k, :], MM[:, k, :], ALU.add).then_inc(s["post_x"], 1)
                dve.wait_ge(s["post_x"], KD + k + 1)
                if k:
                    dve.wait_ge(s["split_hi"], 4 * KD + k)
                    tt(GL[:, k - 1, :], X[:, k - 1, :], INL[:, k - 1, :].bitcast(f32), ALU.subtract)\
                        .then_inc(s["split_lo"], 1)
            dve.wait_ge(s["split_hi"], 5 * KD)
            tt(GL[:, KD - 1, :], X[:, KD - 1, :], INL[:, KD - 1, :].bitcast(f32), ALU.subtract)\
                .then_inc(s["split_lo"], 1)
            scale_from(7)
            for k in range(KD):
                chain(stt(EMB[:, k, :], EMB[:, k, :], g("g_ple", k), RS[:], ALU.mult, ALU.mult))
            chain.wait()
            for k in range(KD):
                dve.wait_ge(s["bank_free"], U_PLEG + k + 1)
                chain(tt(GT[:, k, :], GT[:, k, :], EMB[:, k, :], ALU.mult))
                chain.wait()
                tt(X[:, k, :], X[:, k, :], GT[:, k, :], ALU.add).then_inc(s["ple_out"], 1)


def units(w, k_chunks, cols):
    k, n = w.shape
    w = w.reshape(k // (P * k_chunks), k_chunks, P, n // cols, cols)
    return w.transpose(0, 3, 2, 1, 4).reshape(-1, P, k_chunks * cols)


def columns(*vectors):
    import numpy as np
    return np.concatenate([v.reshape(-1, P).T for v in vectors], axis=1)


def kernel(x, norm1_g, w_in, q_norm_g, k_norm_g, rpb, dw_kernel, dw_bias, conv_ln_g, conv_ln_b, w_out,
           norm2_g, w_gate, w_up, w_down, p_2, g_mix_pre_2, w_in_2, w_pool_2, pool_scale_2, g_sb_2,
           w_out_2, g_mix_post_2, g_mlp_pre_2, w_up_2, w_down_2, g_mlp_post_2, w_ple_gate_2,
           w_ple_proj_2, g_ple_2):
    import numpy as np
    import concourse.bacc as bacc
    from concourse.bass_utils import run_bass_kernel_spmd

    def interleave(*ws):
        return np.stack(ws, axis=1).reshape(-1, *ws[0].shape[1:])

    def chunks(a):
        return a.T.reshape(-1, P, T).transpose(1, 0, 2)

    w = units(w_in[0], KD, P)
    main = NG1 * G
    ffu = interleave(units(w_gate[0], KD, P), units(w_up[0], KD, P))
    w2 = units(w_in_2[0], KD, P)
    arrays = {
        "x": chunks(x[0]),
        "w_glu": interleave(w[4:8], w[0:4]),
        "w_qkv": interleave(w[8:12], w[12:16], w[16:20]),
        "w_out": units(w_out[0], KD, P),
        "w_ff": ffu[:2 * main],
        "w_ffd": units(w_down[0][:main * P], G, 2 * P),
        "w_tail": ffu[2 * main:],
        "w_taild": units(w_down[0][main * P:], TAIL, 2 * P),
        "gains": columns(norm1_g[0], norm2_g[0], g_mix_pre_2[0], g_mix_post_2[0], g_mlp_pre_2[0],
                         g_mlp_post_2[0], g_ple_2[0], np.concatenate([q_norm_g[0], q_norm_g[0]]),
                         np.concatenate([k_norm_g[0], k_norm_g[0]]), dw_bias[0], conv_ln_g[0],
                         conv_ln_b[0], pool_scale_2[0], g_sb_2[0]),
        "taps": dw_kernel[0].T.reshape(4, P, TAPS).transpose(1, 0, 2),
        "rpb": rpb[0],
        "p_t": p_2[0, 0].T.reshape(2, P, T).transpose(1, 0, 2),
        "w_in2": np.concatenate([w2[0:4], interleave(w2[4:8], w2[8:12], w2[12:16])]),
        "w_pool": w_pool_2[0].transpose(1, 0, 2),
        "w_out2": units(w_out_2[0], KD, P),
        "w_mlp": units(w_up_2[0], KD, P),
        "w_mlpd": units(w_down_2[0], G, 2 * P),
        "w_plep": units(w_ple_proj_2[0], 2, 2 * P),
        "w_pleg": units(w_ple_gate_2[0], KD, P),
    }
    nc = bacc.Bacc("TRN2", target_bir_lowering=False, num_devices=1)
    aps = {}
    for name, a in arrays.items():
        arrays[name] = a = np.ascontiguousarray(a)
        aps[name] = nc.dram_tensor(name, a.shape, mybir.dt.from_np(a.dtype), kind="ExternalInput").ap()
    aps["out"] = nc.dram_tensor("out", (P, KD, T), mybir.dt.float32, kind="ExternalOutput").ap()
    program(nc, **aps)
    r = run_bass_kernel_spmd(nc, [arrays], core_ids=[0])
    got = r.results[0]["out"]
    return np.ascontiguousarray(got.transpose(2, 1, 0).reshape(1, T, D))
```
